# Optimizing a Trainium2 kernel written in Bass

```python
import jax, jax.numpy as jnp
from jax import lax
import numpy as np

D_MODEL = 1024
BATCH = 1
SEQ = 128
DEPTH = 2
DEC_BATCH = 1
DEC_SEQ = 128
PAST_LEN = 128

GRID_W = 64
HEAD_DIM = 128
N_Q_HEADS = 8
N_KV_HEADS = 2
WINDOW = 128
BLOCK = 128
ROPE_BASE = 10000.0
DN_HEADS = 8
DN_DK = 128
DN_DV = 128
DN_CONV = 5
DN_CHUNK = 64
D_FF = 2816
N_EXPERTS = 8
TOP_K = 2
D_EXPERT = 3584
N_DENSE = (DEPTH + 1) // 2
N_MOE = DEPTH // 2
EPS = 1e-6
NEG_INF = -1e30

Q_W = N_Q_HEADS * HEAD_DIM
KV_W = N_KV_HEADS * HEAD_DIM
DN_KW = DN_HEADS * DN_DK
DN_VW = DN_HEADS * DN_DV
DN_QKV = 2 * DN_KW + DN_VW
SPLITS = (Q_W, KV_W, KV_W, DN_QKV, DN_VW, 2 * DN_HEADS, 2 * DN_HEADS, D_MODEL, D_MODEL)
IN_W = sum(SPLITS)

kernel_name = "hybrid_diffusion_swa_deltanet_prefix_ctx"

F32 = jnp.float32

def rmsnorm(x, g):
    xf = x.astype(F32)
    y = xf * lax.rsqrt(jnp.mean(xf * xf, axis=-1, keepdims=True) + EPS) * g.astype(F32)
    return y.astype(x.dtype)

def l2norm(x):
    return x * lax.rsqrt(jnp.sum(x * x, axis=-1, keepdims=True) + EPS)

def axial_rope_tables(n_rows):
    rows = jnp.repeat(jnp.arange(n_rows), GRID_W).astype(F32)
    cols = jnp.tile(jnp.arange(GRID_W), n_rows).astype(F32)
    n_freq = HEAD_DIM // 4
    inv = ROPE_BASE ** (-jnp.arange(n_freq, dtype=F32) / n_freq)
    ar = rows[:, None] * inv
    ac = cols[:, None] * inv
    return (jnp.cos(ar), jnp.sin(ar), jnp.cos(ac), jnp.sin(ac))

def _rotate(x, cos, sin):
    x1, x2 = jnp.split(x, 2, axis=-1)
    cos = cos[None, :, None, :]
    sin = sin[None, :, None, :]
    return jnp.concatenate([x1 * cos - x2 * sin, x2 * cos + x1 * sin], axis=-1)

def axial_rope(x, tables):
    cos_r, sin_r, cos_c, sin_c = tables
    xf = x.astype(F32)
    half = HEAD_DIM // 2
    y = jnp.concatenate([_rotate(xf[..., :half], cos_r, sin_r), _rotate(xf[..., half:], cos_c, sin_c)], axis=-1)
    return y.astype(x.dtype)

def softmax_with_sink(q, k, v, mask, sink):
    B, Q, Hq, d = q.shape
    Hkv = k.shape[2]
    G = Hq // Hkv
    qg = q.reshape(B, Q, Hkv, G, d)
    s = jnp.einsum('bqhgd,bkhd->bhgqk', qg, k).astype(F32) * (d ** -0.5)
    s = jnp.where(mask, s, NEG_INF)
    sk = jnp.broadcast_to(sink.astype(F32).reshape(1, Hkv, G, 1, 1), (B, Hkv, G, Q, 1))
    p = jax.nn.softmax(jnp.concatenate([s, sk], axis=-1), axis=-1)[..., :-1]
    o = jnp.einsum('bhgqk,bkhd->bqhgd', p.astype(v.dtype), v)
    return o.reshape(B, Q, Hq, d)

def context_attention(q, k, v, sink):
    B, L, Hq, d = q.shape
    nb = L // BLOCK
    qb = jnp.moveaxis(q.reshape(B, nb, BLOCK, Hq, d), 1, 0)
    mask = jnp.ones((BLOCK, L), bool)
    o = lax.map(lambda qi: softmax_with_sink(qi, k, v, mask, sink), qb)
    return jnp.moveaxis(o, 0, 1).reshape(B, L, Hq, d)

def latent_attention(q, k, v, k_ctx, v_ctx, sink):
    B, T, Hq, d = q.shape
    nb = T // BLOCK
    pad = ((0, 0), (BLOCK, BLOCK), (0, 0), (0, 0))
    kp = jnp.pad(k, pad)
    vp = jnp.pad(v, pad)
    k_ctx = k_ctx.astype(k.dtype)
    v_ctx = v_ctx.astype(v.dtype)
    ctx_mask = jnp.ones((BLOCK, k_ctx.shape[1]), bool)
    qb = jnp.moveaxis(q.reshape(B, nb, BLOCK, Hq, d), 1, 0)
    offs = jnp.arange(BLOCK)
    koffs = jnp.arange(3 * BLOCK)

    def one(args):
        i, qi = args
        start = i * BLOCK
        kl = lax.dynamic_slice_in_dim(kp, start, 3 * BLOCK, axis=1)
        vl = lax.dynamic_slice_in_dim(vp, start, 3 * BLOCK, axis=1)
        qpos = start + offs
        kpos = start - BLOCK + koffs
        band = (jnp.abs(qpos[:, None] - kpos[None, :]) <= WINDOW) & (kpos >= 0)[None, :] & (kpos < T)[None, :]
        keys = jnp.concatenate([k_ctx, kl], axis=1)
        vals = jnp.concatenate([v_ctx, vl], axis=1)
        mask = jnp.concatenate([ctx_mask, band], axis=1)
        return softmax_with_sink(qi, keys, vals, mask, sink)

    o = lax.map(one, (jnp.arange(nb), qb))
    return jnp.moveaxis(o, 0, 1).reshape(B, T, Hq, d)

def short_conv(x, w):
    C = x.shape[-1]
    return lax.conv_general_dilated(
        x, w[:, None, :].astype(x.dtype), window_strides=(1,),
        padding=((DN_CONV // 2, DN_CONV // 2),),
        dimension_numbers=('NWC', 'WIO', 'NWC'), feature_group_count=C)

def delta_inputs(qkv, beta_logit, a_in, conv_w, a_log, dt_bias):
    B, T, _ = qkv.shape
    qkv = jax.nn.silu(short_conv(qkv, conv_w)).astype(F32)
    q, k, v = jnp.split(qkv, [DN_KW, 2 * DN_KW], axis=-1)
    q = l2norm(q.reshape(B, T, DN_HEADS, DN_DK)) * (DN_DK ** -0.5)
    k = l2norm(k.reshape(B, T, DN_HEADS, DN_DK))
    v = v.reshape(B, T, DN_HEADS, DN_DV)
    beta = jax.nn.sigmoid(beta_logit.astype(F32)).reshape(B, T, 2, DN_HEADS)
    g = -jnp.exp(a_log.astype(F32)) * jax.nn.softplus(
        a_in.astype(F32).reshape(B, T, 2, DN_HEADS) + dt_bias.astype(F32))
    return q, k, v, g, beta

def gated_delta_chunked(q, k, v, g, beta, s0):
    B, T, H, _ = q.shape
    n = T // DN_CHUNK

    def chunks(x):
        x = x.reshape((B, n, DN_CHUNK, H) + x.shape[3:])
        return jnp.swapaxes(jnp.moveaxis(x, 1, 0), 2, 3)

    qc, kc, vc, bc = chunks(q), chunks(k), chunks(v), chunks(beta)
    gc = jnp.cumsum(chunks(g), axis=-1)
    idx = jnp.arange(DN_CHUNK)
    incl = idx[:, None] >= idx[None, :]
    strict = idx[:, None] > idx[None, :]
    diff = gc[..., :, None] - gc[..., None, :]
    decay = jnp.where(incl, jnp.exp(jnp.where(incl, diff, 0.0)), 0.0)
    kb = kc * bc[..., None]
    eye = jnp.eye(DN_CHUNK, dtype=F32)
    a_mat = jnp.where(strict, jnp.einsum('nbhik,nbhjk->nbhij', kb, kc) * decay, 0.0) + eye
    t_inv = lax.linalg.triangular_solve(a_mat, jnp.broadcast_to(eye, a_mat.shape),
                                        left_side=True, lower=True, unit_diagonal=True)
    u = jnp.einsum('nbhij,nbhjv->nbhiv', t_inv, vc * bc[..., None])
    w = jnp.einsum('nbhij,nbhjk->nbhik', t_inv, kb * jnp.exp(gc)[..., None])
    qk = jnp.einsum('nbhik,nbhjk->nbhij', qc, kc) * decay
    q_dec = qc * jnp.exp(gc)[..., None]
    g_last = gc[..., -1]
    k_dec = kc * jnp.exp(g_last[..., None] - gc)[..., None]

    def step(S, xs):
        u_c, w_c, qk_c, qd_c, kd_c, gl_c = xs
        v_new = u_c - jnp.einsum('bhck,bhkv->bhcv', w_c, S)
        o_c = jnp.einsum('bhck,bhkv->bhcv', qd_c, S) + jnp.einsum('bhij,bhjv->bhiv', qk_c, v_new)
        S = S * jnp.exp(gl_c)[..., None, None] + jnp.einsum('bhck,bhcv->bhkv', kd_c, v_new)
        return S, o_c

    s_fin, o = lax.scan(step, s0, (u, w, qk, q_dec, k_dec, g_last))
    o = jnp.moveaxis(jnp.swapaxes(o, 2, 3), 0, 1).reshape(B, T, H, DN_DV)
    return o, s_fin

def bidir_delta(q, k, v, g, beta, s0):
    flip = lambda t: jnp.flip(t, axis=1)
    o_f, s_f = gated_delta_chunked(q, k, v, g[:, :, 0], beta[:, :, 0], s0[:, 0])
    o_b, s_b = gated_delta_chunked(flip(q), flip(k), flip(v), flip(g[:, :, 1]), flip(beta[:, :, 1]), s0[:, 1])
    return o_f + flip(o_b), jnp.stack([s_f, s_b], axis=1)

def token_mixers(h, P, l, latent):
    B, T, _ = h.shape
    offsets = np.cumsum(SPLITS)[:-1].tolist()
    q_a, k_a, v_a, qkv_b, z_b, b_b, a_b, gt_a, gt_b = jnp.split(h @ P['w_in'][l], offsets, axis=-1)
    q_a = q_a.reshape(B, T, N_Q_HEADS, HEAD_DIM)
    k_a = k_a.reshape(B, T, N_KV_HEADS, HEAD_DIM)
    v_a = v_a.reshape(B, T, N_KV_HEADS, HEAD_DIM)
    sink = P['attn_sink'][l]
    q_b, k_b, v_b, g_b, beta_b = delta_inputs(qkv_b, b_b, a_b, P['conv_w'][l], P['dn_a_log'][l], P['dn_dt_bias'][l])
    if latent is None:
        o_a = context_attention(q_a, k_a, v_a, sink)
        s0 = jnp.zeros((B, 2, DN_HEADS, DN_DK, DN_DV), F32)
    else:
        rope, ctx_k, ctx_v, ctx_s = latent
        o_a = latent_attention(axial_rope(q_a, rope), axial_rope(k_a, rope), v_a, ctx_k, ctx_v, sink)
        s0 = ctx_s.astype(F32)
    o_b, s_fin = bidir_delta(q_b, k_b, v_b, g_b, beta_b, s0)
    o_b = rmsnorm(o_b, P['dn_norm_g'][l]) * jax.nn.silu(z_b.astype(F32).reshape(B, T, DN_HEADS, DN_DV))
    o_b = o_b.astype(h.dtype)
    br_a = o_a.reshape(B, T, Q_W) @ P['w_pa'][l]
    br_b = o_b.reshape(B, T, DN_VW) @ P['w_pb'][l]
    y = (jax.nn.sigmoid(gt_a) * br_a + jax.nn.sigmoid(gt_b) * br_b) @ P['w_o'][l]
    ctx_out = (k_a, v_a, s_fin.astype(h.dtype)) if latent is None else None
    return y, ctx_out

def swiglu(h, wg, wu, wd):
    return (jax.nn.silu(h @ wg) * (h @ wu)) @ wd

def moe_swiglu(h, w_router, wg, wu, wd):
    logits = (h @ w_router).astype(F32)
    top_v, top_i = lax.top_k(logits, TOP_K)
    wts = jax.nn.softmax(top_v, axis=-1)
    combine = jnp.sum(jax.nn.one_hot(top_i, N_EXPERTS, dtype=F32) * wts[..., None], axis=-2).astype(h.dtype)
    out = jnp.zeros_like(h)
    for e in range(N_EXPERTS):
        out = out + combine[..., e:e + 1] * swiglu(h, wg[e], wu[e], wd[e])
    return out

def sandwich_layer(x, cond, P, l, latent):
    mod = (jax.nn.silu(cond) @ P['w_ada'][l] + P['b_ada'][l])[:, None, :]
    sh1, sc1, gt1, sh2, sc2, gt2 = jnp.split(mod, 6, axis=-1)
    gn = P['norm_g'][l]
    h = rmsnorm(x, gn[0]) * (1 + sc1) + sh1
    y, ctx_out = token_mixers(h, P, l, latent)
    x = x + gt1 * rmsnorm(y, gn[1])
    h = rmsnorm(x, gn[2]) * (1 + sc2) + sh2
    if l % 2 == 0:
        i = l // 2
        f = swiglu(h, P['w_ff_gate'][i], P['w_ff_up'][i], P['w_ff_down'][i])
    else:
        i = l // 2
        f = moe_swiglu(h, P['w_router'][i], P['w_e_gate'][i], P['w_e_up'][i], P['w_e_down'][i])
    x = x + gt2 * rmsnorm(f, gn[3])
    return x, ctx_out

def setup_inputs(seed: int = 0) -> dict:
    key = jax.random.key(seed)
    keys = jax.random.split(key, 64)
    counter = [0]

    def nxt():
        counter[0] += 1
        return keys[counter[0] - 1]

    def rnd(shape, scale):
        return jax.random.normal(nxt(), shape, F32) * scale

    d = {}
    d['x_prompt'] = rnd((BATCH, SEQ, D_MODEL), 1.0)
    d['x_sample'] = rnd((DEC_BATCH, DEC_SEQ, D_MODEL), 1.0)
    d['c'] = rnd((DEC_BATCH, D_MODEL), 1.0)
    for l in range(DEPTH):
        d['cache_k_l%d' % l] = rnd((DEC_BATCH, PAST_LEN, N_KV_HEADS, HEAD_DIM), 1.0)
        d['cache_v_l%d' % l] = rnd((DEC_BATCH, PAST_LEN, N_KV_HEADS, HEAD_DIM), 1.0)
        d['state_delta_l%d' % l] = rnd((DEC_BATCH, 2, DN_HEADS, DN_DK, DN_DV), 0.5)
    d['c_ctx'] = rnd((D_MODEL,), 1.0)
    d['w_ada'] = rnd((DEPTH, D_MODEL, 6 * D_MODEL), 0.5 * D_MODEL ** -0.5)
    d['b_ada'] = rnd((DEPTH, 6 * D_MODEL), 0.02)
    d['norm_g'] = 1.0 + rnd((DEPTH, 4, D_MODEL), 0.02)
    d['w_in'] = rnd((DEPTH, D_MODEL, IN_W), D_MODEL ** -0.5)
    d['attn_sink'] = rnd((DEPTH, N_Q_HEADS), 0.5)
    d['conv_w'] = rnd((DEPTH, DN_CONV, DN_QKV), DN_CONV ** -0.5)
    d['dn_a_log'] = jnp.log(jax.random.uniform(nxt(), (DEPTH, 2, DN_HEADS), F32, 1.0, 16.0))
    dt = jnp.exp(jax.random.uniform(nxt(), (DEPTH, 2, DN_HEADS), F32, float(np.log(1e-3)), float(np.log(1e-1))))
    d['dn_dt_bias'] = dt + jnp.log(-jnp.expm1(-dt))
    d['dn_norm_g'] = 1.0 + rnd((DEPTH, DN_DV), 0.02)
    d['w_pa'] = rnd((DEPTH, Q_W, D_MODEL), Q_W ** -0.5)
    d['w_pb'] = rnd((DEPTH, DN_VW, D_MODEL), DN_VW ** -0.5)
    d['w_o'] = rnd((DEPTH, D_MODEL, D_MODEL), D_MODEL ** -0.5)
    d['w_ff_gate'] = rnd((N_DENSE, D_MODEL, D_FF), D_MODEL ** -0.5)
    d['w_ff_up'] = rnd((N_DENSE, D_MODEL, D_FF), D_MODEL ** -0.5)
    d['w_ff_down'] = rnd((N_DENSE, D_FF, D_MODEL), D_FF ** -0.5)
    d['w_router'] = rnd((N_MOE, D_MODEL, N_EXPERTS), D_MODEL ** -0.5)
    d['w_e_gate'] = rnd((N_MOE, N_EXPERTS, D_MODEL, D_EXPERT), D_MODEL ** -0.5)
    d['w_e_up'] = rnd((N_MOE, N_EXPERTS, D_MODEL, D_EXPERT), D_MODEL ** -0.5)
    d['w_e_down'] = rnd((N_MOE, N_EXPERTS, D_EXPERT, D_MODEL), D_EXPERT ** -0.5)
    return d

def reference(x_prompt, x_sample, c, cache_k_l0, cache_v_l0, state_delta_l0, cache_k_l1, cache_v_l1,
              state_delta_l1, c_ctx, w_ada, b_ada, norm_g, w_in, attn_sink, conv_w, dn_a_log, dn_dt_bias,
              dn_norm_g, w_pa, w_pb, w_o, w_ff_gate, w_ff_up, w_ff_down, w_router, w_e_gate, w_e_up, w_e_down):
    P = {'w_ada': w_ada, 'b_ada': b_ada, 'norm_g': norm_g, 'w_in': w_in, 'attn_sink': attn_sink,
         'conv_w': conv_w, 'dn_a_log': dn_a_log, 'dn_dt_bias': dn_dt_bias, 'dn_norm_g': dn_norm_g,
         'w_pa': w_pa, 'w_pb': w_pb, 'w_o': w_o, 'w_ff_gate': w_ff_gate, 'w_ff_up': w_ff_up,
         'w_ff_down': w_ff_down, 'w_router': w_router, 'w_e_gate': w_e_gate, 'w_e_up': w_e_up,
         'w_e_down': w_e_down}
    caches = ((cache_k_l0, cache_v_l0, state_delta_l0), (cache_k_l1, cache_v_l1, state_delta_l1))

    xp = x_prompt
    cond_ctx = c_ctx[None, :]
    ctx_state = []
    for l in range(DEPTH):
        xp, ctx_out = sandwich_layer(xp, cond_ctx, P, l, None)
        ctx_state.append(ctx_out)

    n_tok = x_sample.shape[1]
    ROWS = n_tok // GRID_W
    rope = axial_rope_tables(ROWS)
    xs = x_sample
    for l in range(DEPTH):
        k_c, v_c, s_c = caches[l]
        xs, _ = sandwich_layer(xs, c, P, l, (rope, k_c, v_c, s_c))

    return (xp, xs, ctx_state[0][0], ctx_state[0][1], ctx_state[0][2], ctx_state[1][0], ctx_state[1][1], ctx_state[1][2])


_drawn_inputs = setup_inputs


def setup_inputs(seed=0):
    import zlib

    import numpy as np

    out = dict(_drawn_inputs(seed))
    spreads = {}
    factors = {}
    for name, (base, spread) in spreads.items():
        noise = np.random.default_rng([zlib.crc32(name.encode()), seed]).standard_normal(out[name].shape)
        drawn = base * np.exp(spread * noise) if base else spread * noise
        out[name] = __import__('jax').numpy.asarray(drawn.astype(out[name].dtype))
    for name, factor in factors.items():
        out[name] = (out[name] * factor).astype(out[name].dtype)
    return out
```

```python
from contextlib import ExitStack

import numpy as np

import concourse.bass as bass
from concourse import mybir

F32 = mybir.dt.float32
I32 = mybir.dt.int32
ACT = mybir.ActivationFunctionType
ALU = mybir.AluOpType
AX_X = mybir.AxisListType.X

P = 128
G = 2
D = 1024
KC = D // P
DEPTH = 2
HQ, HKV = 8, 2
DH = 8
TAPS = 5
PAD = TAPS // 2
TP = P + 2 * PAD
QKV_CH = 3 * DH
DFF = 2816
NEXP = 8
DEXP = 3584
EPS = 1e-6
IN_W = 7712
C_QKVB, C_Z, C_BA, C_GATES = 1536, 4608, 5632, 5664
COLS = 4608
T_K, T_V, T_Z, T_GA, T_GB = 1024, 1280, 1536, 2560, 3584
UNIT = 2048
RING = 6
LEVELS = 7
FF_STEPS = DFF // 256
FB = DEXP // 512
EXTRA = 3
NEG = -3.0e38
SCALE = float(P) ** -0.5

K_ID = 0
K_TRI = K_ID + P
K_STR = K_TRI + 2 * P
K_ONE = K_STR + 2 * P
K_LEV = K_ONE + P
K_ROPE = K_LEV + LEVELS * 2 * P
K_IOTA = K_ROPE + 128
K_SEL = K_IOTA + 256
K_ALL = K_SEL + 2 * P


def constants():
    c = np.zeros((P, K_ALL), np.float32)
    r, k = np.arange(P)[:, None], np.arange(P)[None, :]
    c[:, K_ID:K_ID + P] = r == k
    c[:, K_TRI:K_TRI + P] = r <= k
    c[:, K_TRI + P:K_TRI + 2 * P] = r >= k
    c[:, K_STR:K_STR + P] = r < k
    c[:, K_STR + P:K_STR + 2 * P] = r > k
    c[:, K_ONE:K_ONE + P] = 1.0
    for n in range(LEVELS):
        s = 1 << n
        same = (r // (2 * s)) == (k // (2 * s))
        low = same & (r % (2 * s) >= s) & (k % (2 * s) < s)
        m = (r == k).astype(np.float32)
        c[:, K_LEV + 2 * n * P:K_LEV + (2 * n + 1) * P] = m - low
        c[:, K_LEV + (2 * n + 1) * P:K_LEV + (2 * n + 2) * P] = m - low.T
    inv = 10000.0 ** (-np.arange(32, dtype=np.float32) / 32)
    ang = np.stack([(np.arange(P) // 64)[:, None] * inv, (np.arange(P) % 64)[:, None] * inv], 1)
    ang = ang.astype(np.float32).reshape(P, 64)
    c[:, K_ROPE:K_ROPE + 64] = np.cos(ang)
    c[:, K_ROPE + 64:K_ROPE + 128] = np.sin(ang)
    c[:, K_IOTA:K_IOTA + 256] = np.arange(256)[None, :]
    for g in range(G):
        c[:, K_SEL + g * P:K_SEL + (g + 1) * P] = (np.arange(P) % 32 == g)[:, None]
    return c


class Steps:

    def __init__(self, sem, iters, names):
        self.sem, self.iters, self.off = sem, iters, {}
        n = 0
        for x in names:
            name, k = x if isinstance(x, tuple) else (x, 1)
            assert name not in self.off
            n += k
            self.off[name] = n
        self.per = n

    def at(self, name, l=0, i=0):
        return i * self.per + ((l * self.iters + 1) * self.per + self.off[name])


class Order:

    def __init__(self, steps):
        self.s, self.n = steps, 0

    def inc(self, ins, name):
        self.n += 1
        lo = 0
        for k, v in self.s.off.items():
            if lo < self.n <= v:
                assert k == name, (k, name)
            lo = v
        ins.then_inc(self.s.sem, 1)
        if self.n == self.s.per:
            self.n = 0


def program(nc, A):
    ctx = ExitStack()
    with ctx:
        def sb(name, shape, dt=F32):
            return ctx.enter_context(nc.sbuf_tensor(name, shape, dt))

        def sem(name):
            return ctx.enter_context(nc.semaphore(name))

        def steps(name, iters, names):
            return Steps(sem(name), iters, names)

        ring = sb("ring", [P, RING, UNIT])
        con = sb("con", [P, K_ALL])
        xt = sb("xt", [P, G, D])
        hreg = sb("hreg", [P, 4096])
        tok = sb("tok", [P, G, COLS])
        qreg = sb("qreg", [P, QKV_CH * G * TP])
        mod = sb("mod", [P, 2, D])
        s0 = sb("s0", [P, DH, 2, P])
        dnx = sb("dnx", [P, 8448])
        cache_k = sb("cache_k", [P, HKV, P])
        cache_v = sb("cache_v", [P, HKV, P])
        small = sb("small", [P, 1024])
        wba = sb("wba", [P, KC, 32])
        ps = ctx.enter_context(nc.psum_tensor("ps", [P, 8, 512], F32))

        def cut(t, at, shape):
            n = 1
            for k in shape:
                n *= k
            flat = t[:, at:at + n]
            names = "abcd"[:len(shape)]
            if len(shape) == 1:
                return flat
            return flat.rearrange("p (%s) -> p %s" % (" ".join(names), " ".join(names)),
                                  **{names[j]: shape[j] for j in range(len(shape))})

        ident = con[:, K_ID:K_ID + P]
        ones = con[:, K_ONE:K_ONE + P]

        def tri(d):
            return con[:, K_TRI + d * P:K_TRI + (d + 1) * P]

        def two(at):
            t = con[:, at:at + 2 * P].rearrange("p (d o k) -> p d o k", d=2, o=1)
            return t.to_broadcast([P, 2, G, P])

        h_tok = cut(hreg, 0, (G, D))
        h_t = cut(hreg, 2048, (KC, G * P))
        qkv = cut(qreg, 0, (QKV_CH, G, TP))

        kqv = [cut(hreg, 768 * s, (3, G, P)) for s in range(2)]
        XX = [cut(hreg, 1536 + 1024 * s, (2, 2, G, P)) for s in range(2)]
        at = [0]

        def slot(shape):
            n = int(np.prod(shape))
            r = [cut(dnx, at[0] + n * s, shape) for s in range(2)]
            at[0] += 2 * n
            return r

        ktv = slot((3, P))
        ET = slot((2, G, P))
        attn = slot((2, G, P))
        AT = slot((2, G, P))
        MM = slot((2, G, P))
        RP = slot((2, P))
        VN = slot((2, G, P))
        VD = slot((2, P))
        osb = slot((G, P))
        sfo = slot((2, P))
        junk = slot((G, P))
        assert at[0] <= 8448
        acc = [cut(dnx, 256 * s, (G, P)) for s in range(2)]
        l2s = [cut(dnx, 512 + 512 * s, (2, G, P)) for s in range(2)]
        l2c = cut(dnx, 1536, (8,))
        at[0] = 0
        qst = slot((G, P))
        qT = slot((G, P))
        pr = slot((3, P))
        prT = slot((3, P))
        kTb = cut(dnx, at[0], (HKV, 3, P))
        at[0] += 768
        rope_t = [cut(dnx, at[0] + 640 * j, (10, 2, 32)) for j in range(4)]
        assert at[0] + 2560 <= 8448
        oaT = cut(qreg, 0, (KC, G * P))
        obT = cut(qreg, 2048, (KC, G * P))
        y_sb = cut(qreg, 4096, (G, D))
        ngr = cut(qreg, 0, (2, D))
        sqj = cut(dnx, 0, (D,))
        tokf = tok[:, :, :].rearrange("p g c -> p (g c)")
        f_hs = [cut(tokf, 512 * s, (512,)) for s in range(2)]
        f_hid = [cut(tokf, 1024 + 512 * s, (512,)) for s in range(2)]
        f_hT = [cut(tokf, 2048 + 512 * s, (4, P)) for s in range(2)]
        hTe = cut(tokf, 3072, (KC, P))
        sel = cut(tokf, 4096, (G, P))
        selc = cut(tokf, 4352, (G, P))
        selT = cut(tokf, 4608, (G, P))
        ye = cut(tokf, 4864, (D,))
        f_acc = cut(tokf, 5888, (G, D))
        sm = [0]

        def col(n):
            sm[0] += n
            assert sm[0] <= 1024
            return small[:, sm[0] - n:sm[0]]

        condT = col(2 * KC).rearrange("p (k c) -> p k c", c=2)
        ss, ms, rstd = col(2), col(2), col(2)
        mhalf = col(16)
        ba = col(64).rearrange("p (g c) -> p g c", g=G)
        eb = col(32).rearrange("p (g c) -> p g c", g=G)
        ga = [col(32).rearrange("p (g c) -> p g c", g=G) for _ in range(5)]
        dtb, alog, ealog = col(16), col(16), col(16)
        gcs, gex = col(64), col(64)
        GT = col(192).rearrange("p (h q d g) -> p h q d g", h=DH, q=6, d=2)
        cw = col(128)
        hc = [col(24).rearrange("p (q d g) -> p q d g", q=6, d=2) for _ in range(2)]
        oss = [col(2) for _ in range(2)]
        ors = [col(2) for _ in range(2)]
        sinkb = col(8)
        am = [[col(2) for _ in range(7)] for _ in range(2)]
        cwr = sb("cwr", [P, P])
        dng = sb("dng", [P, P])
        cond = hreg[0:2, 0:D]
        condS = hreg[0:2, D:2 * D]
        wr = sb("wr", [P, KC, NEXP])
        over_tab = sb("over_tab", [P, EXTRA + 1], I32)
        rt = [cut(tokf, 8000 + 16 * j, (G, NEXP)) for j in range(12)]
        rcol = [cut(tokf, 8192 + 2 * j, (G, 1)) for j in range(8)]

        ready = [sem("unit_ready%d" % j) for j in range(RING)]
        unit_used = sem("unit_used")
        s_in = sem("inputs_in")
        s_out = sem("outputs_out")
        s_state = [sem("state_out%d" % s) for s in range(2)]
        s_lay = sem("layer_small_in")
        LAY_DMAS = 20
        init_a = steps("init_act", 1, ["cond"])
        init_p = steps("init_pe", 1, ["condT"])
        init_v = steps("init_dve", 1, ["half", "condT"])
        lay_g = steps("layer_pool", 1, [("pads", 2)])
        ada_v = steps("ada_dve", 1, [("row", 12), ("mod", 4)])
        rms_a = steps("rms_act", 4, [("ss", 2)])
        rms_v = steps("rms_dve", 4, ["ms"])
        rms_g = steps("rms_pool", 4, ["rstd"])
        nrm_p = steps("norm_pe", 2, ["bc0", "bc1", "t00", "t01", "t10", "t11"])
        nrm_v = steps("norm_dve", 2, ["a0", "h0", "a1", "h1"])
        nrm_a = steps("norm_act", 2, ["e00", "e01", "e10", "e11"])
        evac = steps("proj_evac", 5, ["b0", "b1", "b2"])
        gat_p = steps("gates_pe", 1, ["ba", "cw", "gc"])
        gat_v = steps("gates_dve", 1, ["cw", "ba", "a", "na", "e1", "sp", "g0", "gcol", "gcs", "kd",
                                       "gc", "egc", "negc", "ekd", "b1", "rb", "beta"])
        gat_a = steps("gates_act", 1, ["eb", "ea", "el", "ln", ("ex", 2)])
        cnv_v = steps("conv_dve", QKV_CH // 2, ["t%d%d" % (j, s) for j in range(TAPS) for s in range(2)])
        cnv_a = steps("conv_act", QKV_CH // 2, ["s0", "s1"])
        nl_a = steps("gate_act", 1, ["z", "sig"])
        nl_v = steps("gate_dve", 1, ["z"])
        l2_g = steps("l2_pool", 4, ["sq0", "sq1", "pw"])
        l2_p = steps("l2_pe", 4, ["ss", "bc0", "bc1"])
        l2_v = steps("l2_dve", 4, ["ep", "nm0", "nm1"])

        def both(names):
            return [(x[0] % s, x[1]) if isinstance(x, tuple) else x % s for x in names for s in range(2)]

        lv = range(1, LEVELS)
        dn_g = steps("dn_pool", 4, both(["kqv%d", "hc%d", "EM%d", ("XT%d", 2), "rs%d"]))
        dn_p = steps("dn_pe", 4, both(["tr%d", "G%d", "gr%d", "m%d"])
                     + [x for v in lv for x in both(["a%d_%%d" % v, "b%d_%%d" % v])]
                     + both(["kS%d", "V%d", "O%d", "SF%d"]))
        dn_v = steps("dn_dve", 4, both([("t%d", 4), "at%d", "W%d", ("A%d", 4), "AI%d", "X%d"])
                     + [x for v in lv for x in both(["M%d_%%d" % v])]
                     + both([("R%d", 2), ("VD%d", 2), "oc%d", "oa%d", "ob%d", "ms%d", ("y%d", 2)]))
        dn_a = steps("dn_act", 4, both(["tok%d", "ET%d"]) + [x for v in lv for x in both(["E%d_%%d" % v])]
                     + both([("VN%d", 4), "Sf%d", ("sq%d", 2)]))
        rp_v = steps("rope_dve", 1, ["m0", "m1", "m2", "m3", "x1", "x2"])
        kt_p = steps("keys_pe", 1, ["k"])
        kt_a = steps("keys_act", 1, ["k", "o"])
        at_g = steps("attn_pool", 4, both(["q%d"]))
        at_p = steps("attn_pe", 4, both(["qt%d", "sc%d", "pt%d", "pv%d"]))
        at_v = steps("attn_dve", 4, both([("mx%d", 2), "mm%d", "nm%d", "sd%d", "dn%d", "rc%d", ("o%d", 2)]))
        at_a = steps("attn_act", 4, both(["qe%d", ("P%d", 2), "se%d", "pe%d"]))
        out_p = steps("out_pe", 1, ["tr%d" % j for j in range(8)] + ["mt%d" % j for j in range(4)])
        out_a = steps("out_act", 1, ["ev%d" % j for j in range(8)] + ["me%d" % j for j in range(4)])
        out_v = steps("out_dve", 1, [("ga", 4), ("gb", 4), ("m", 2), ("y", 2)])
        res_p = steps("resid_pe", 2, ["gb"])
        res_v = steps("resid_dve", 2, [("t", 2), ("x", 2)])
        ff_a = steps("ff_act", FF_STEPS, [("si", 2), "he"])
        ff_v = steps("ff_dve", FF_STEPS, [("mu", 2)])
        ff_p = steps("ff_pe", FF_STEPS, ["ht"])
        ffe_v = steps("ff_end", 1, [("y", 2)])
        rt_p = steps("router_pe", 1, ["lg", "pos"])
        rt_v = steps("router_dve", 1, ["lg", "m1", "e1", ("c1", 2), "f1", "l2", "m2", "e2", ("c2", 2), "f2",
                                       "mk", "d", "x1", "rc", "w2", "a1", "a2", "cmb", "pos", "acc",
                                       "ov", "cum", "ovi"] + [x % j for j in range(EXTRA) for x in ("eq%d", "id%d")]
                     + ["n", "tab"])
        rt_a = steps("router_act", 1, ["ex"])
        moe_v = steps("moe_dve", NEXP + EXTRA, [("sel", 2), ("selc", 2), "selT"] + ["mu%d" % f for f in range(FB)]
                      + ["ye", ("add", 2), "done"])
        moe_a = steps("moe_act", NEXP + EXTRA, ["ge0", "ge1"] + [x % f for f in range(FB) for x in ("si%d", "he%d")])
        moe_p = steps("moe_pe", NEXP + EXTRA, ["sct", "ga0", "ga1"] + ["ht%d" % f for f in range(FB)] + ["sc0", "sc1"])

        V_STEPS = [init_v, ada_v, rms_v, nrm_v, gat_v, cnv_v, nl_v, l2_v, dn_v, rp_v, at_v, out_v, res_v,
                   ff_v, ffe_v, rt_v, moe_v]
        A_STEPS = [init_a, rms_a, nrm_a, evac, gat_a, cnv_a, nl_a, dn_a, kt_a, at_a, out_a, ff_a, rt_a, moe_a]
        P_STEPS = [init_p, nrm_p, gat_p, l2_p, dn_p, kt_p, at_p, out_p, res_p, ff_p, rt_p, moe_p]
        G_STEPS = [lay_g, rms_g, l2_g, dn_g, at_g]

        U_ADA, U_PROJ, U_OUT, U_FF, U_EXP = 24, 30, 12, 3 * FF_STEPS, 6 * FB
        u_ada = [0, U_ADA + U_PROJ + U_OUT + U_FF]
        u_proj = [u + U_ADA for u in u_ada]
        u_out = [u + U_PROJ for u in u_proj]
        u_ff = u_out[0] + U_OUT
        u_moe = u_out[1] + U_OUT

        def unit(u):
            return ring[:, u % RING, :]

        def wait_unit(pe, u, i=0):
            pe.wait_ge(ready[u % RING], i * 16 + (16 * (u // RING) + 16))

        def wait_used(eng, u, i=0):
            eng.wait_ge(unit_used, i * RING + (u + 1 + RING))

        def mod_row(q, c, n):
            return mod[32 * q:32 * q + 2, c, 512 * n:512 * n + 512]

        def gu_last(f):
            return 6 * f + 1 if f else 3

        def second_blocks(eng, body):
            eng.wait_ge(rt_v.sem, rt_v.at("tab"))
            n = eng.value_load(over_tab[0:1, EXTRA:EXTRA + 1], min_val=0, max_val=EXTRA)
            with eng.Fori(0, EXTRA) as x:
                with eng.If(n > x):
                    e = eng.value_load(over_tab[0:1, bass.ds(x, 1)], min_val=0, max_val=NEXP - 1)
                    body(e, x)

        MODS = [(0, 0), (1, 0), (2, 0), (3, 0), (0, 1), (1, 1)]
        GAIN = {1: 0, 2: 1, 4: 2, 5: 3}

        x_in = [A["x_prompt"], A["x_sample"]]
        block = ctx.enter_context(nc.Block())

        @block.sync
        def _(sp):
            def load(u, src, dst=None, i=0):
                wait_used(sp, u - RING, i)
                d = unit(u) if dst is None else dst
                sp.dma_start(d, src).then_inc(ready[u % RING], 16)

            def rows(u, w, k0, c0, i=0, kn=4, cn=512):
                src = w[k0:k0 + kn, :, bass.ds(c0, cn)].rearrange("k p n -> p k n")
                load(u, src, unit(u)[:, 0:kn * cn].rearrange("p (k n) -> p k n", k=kn), i)

            sp.sem_inc(unit_used, RING)
            for l in range(DEPTH):
                w = A["w_ada"][l].rearrange("(k p) n -> k p n", p=P)
                with sp.Fori(0, 4) as i:
                    for j in range(3):
                        for h in range(2):
                            rows(u_ada[l] + 2 * j + h, w, 4 * h, i * 1536 + 512 * j, i)
                w = A["w_in"][l].rearrange("(k p) n -> k p n", p=P)
                with sp.Fori(0, 2) as i:
                    for j in range(3):
                        for h in range(2):
                            rows(u_proj[l] + 2 * j + h, w, 4 * h, i * 1536 + (C_QKVB + 512 * j), i)
                cols = [512 * j for j in range(3)] + [C_Z, C_Z + 512] + [C_GATES + 512 * j for j in range(4)]
                for j, c in enumerate(cols):
                    for h in range(2):
                        rows(u_proj[l] + 12 + 2 * j + h, w, 4 * h, c)
                u = u_out[l]
                for name in ("w_pa", "w_pb", "w_o"):
                    w = A[name][l].rearrange("(k p) n -> k p n", p=P)
                    for n in range(2):
                        for h in range(2):
                            rows(u, w, 4 * h, 512 * n)
                            u += 1
                if l == 0:
                    wg, wu = (A[n][0].rearrange("(k p) n -> k p n", p=P) for n in ("w_ff_gate", "w_ff_up"))
                    wd = A["w_ff_down"][0].rearrange("(f k p) n -> f p k n", p=P, k=2)

                    def ff_gu(u, f, i=0):
                        rows(u, wg, 0, f * 256, i, 8, 256)
                        rows(u + 1, wu, 0, f * 256, i, 8, 256)

                    def ff_d(u, f, i=0):
                        load(u, wd[bass.ds(f, 1)].rearrange("f p k n -> p (f k) n"),
                             unit(u).rearrange("p (k n) -> p k n", k=2), i)

                    ff_gu(u_ff, 0)
                    ff_gu(u_ff + 2, 1)
                    ff_d(u_ff + 4, 0)
                    with sp.Fori(0, (FF_STEPS - 3) // 2) as i:
                        for j in range(2):
                            ff_gu(u_ff + 5 + 3 * j, i * 2 + (2 + j), i)
                            ff_d(u_ff + 7 + 3 * j, i * 2 + (1 + j), i)
                    u = u_ff + 3 * FF_STEPS - 4
                    ff_gu(u, FF_STEPS - 1)
                    ff_d(u + 2, FF_STEPS - 2)
                    ff_d(u + 3, FF_STEPS - 1)
                else:
                    def expert(e, i):
                        we = [A[n][0, bass.ds(e, 1)].rearrange("e (k p) n -> (e k) p n", p=P)
                              for n in ("w_e_gate", "w_e_up")]
                        wd = A["w_e_down"][0, bass.ds(e, 1)].rearrange("e (f k p) n -> (e f) p k n", p=P, k=2)
                        u = u_moe
                        for f in range(FB + 1):
                            if f < FB:
                                for w in we:
                                    for h in range(2):
                                        rows(u, w, 4 * h, 512 * f, i)
                                        u += 1
                            if f > 0:
                                for h in range(2):
                                    load(u, wd[2 * (f - 1) + h], unit(u).rearrange("p (k n) -> p k n", k=2), i)
                                    u += 1

                    with sp.Fori(0, NEXP) as e:
                        expert(e, e * (U_EXP // RING))
                    second_blocks(sp, lambda e, x: expert(e, (x + NEXP) * (U_EXP // RING)))

        @block.gpsimd
        def _(pool):
            for s in G_STEPS:
                pool.sem_inc(s.sem, s.per)
            D0 = pool.dma_start
            D0(con[:, :], A["consts"]).then_inc(s_in, 16)
            D0(cond[0:1, :], A["c_ctx"].rearrange("(a n) -> a n", a=1)).then_inc(s_in, 16)
            D0(cond[1:2, :], A["c"]).then_inc(s_in, 16)
            for g in range(G):
                D0(xt[:, g, :], x_in[g][0]).then_inc(s_in, 16)

            D0(wr[:, :, :], A["w_router"][0].rearrange("(k p) e -> p k e", p=P)).then_inc(s_in, 16)

            def bc(row, n):
                return row.rearrange("(a n) -> a n", a=1).to_broadcast([n, row.shape[0]])

            def rstd_(l, k):
                pool.wait_ge(rms_v.sem, rms_v.at("ms", l, k))
                pool.wait_ge(init_v.sem, init_v.at("half"))
                rg.inc(pool.tensor_tensor(rstd[:, :], ms[:, :], mhalf[:, 0:2], ALU.pow), "rstd")

            lg, rg, l2g, dg, ag = (Order(s) for s in G_STEPS)
            for l in range(DEPTH):
                if l:
                    pool.wait_ge(res_v.sem, res_v.at("x", 0, 1))
                for m, (q, c) in enumerate(MODS):
                    pool.dma_start(mod[32 * q:32 * q + 2, c, :], bc(A["b_ada"][l, m * D:(m + 1) * D], 2)).then_inc(s_lay, 16)
                for m, r in GAIN.items():
                    q, c = MODS[m]
                    pool.dma_start(ngr[32 * q:32 * q + 2, c, :], bc(A["norm_g"][l, r], 2)).then_inc(s_lay, 16)
                pool.dma_start(wba[:, :, :], A["w_in"][l, :, C_BA:C_BA + 32].rearrange("(k p) n -> p k n", p=P)).then_inc(s_lay, 16)
                pool.dma_start(cwr[0:TAPS * QKV_CH, :], A["conv_w"][l].rearrange("j (c p) -> (j c) p", p=P)).then_inc(s_lay, 16)
                pool.dma_start(dtb, bc(A["dn_dt_bias"][l].rearrange("d h -> (d h)"), P)).then_inc(s_lay, 16)
                pool.dma_start(alog, bc(A["dn_a_log"][l].rearrange("d h -> (d h)"), P)).then_inc(s_lay, 16)
                pool.dma_start(dng[:, :], bc(A["dn_norm_g"][l], P)).then_inc(s_lay, 16)
                pool.dma_start(sinkb, bc(A["attn_sink"][l], P)).then_inc(s_lay, 16)
                for d in range(2):
                    pool.dma_start(s0[:, :, d, :], A["state%d" % l][0, d].rearrange("h k v -> k h v")).then_inc(s_lay, 16)
                pool.dma_start(cache_k[:, :, :], A["cache_k%d" % l][0]).then_inc(s_lay, 16)
                pool.dma_start(cache_v[:, :, :], A["cache_v%d" % l][0]).then_inc(s_lay, 16)
                rstd_(l, 0)
                pool.wait_ge(ada_v.sem, ada_v.at("mod", l))
                lg.inc(pool.memset(qkv[:, :, :, 0:PAD], 0.0), "pads")
                lg.inc(pool.memset(qkv[:, :, :, PAD + P:TP], 0.0), "pads")
                with pool.Fori(0, 4) as i:
                    for s in range(2):
                        x = qkv[:, bass.ds(i * 2 + 8 * s, 2), :, PAD:PAD + P]
                        if s == 0:
                            pool.wait_ge(cnv_a.sem, cnv_a.at("s1", l, QKV_CH // 2 - 1))
                        pool.wait_ge(l2_p.sem, l2_p.at("ss", l, i - 1))
                        l2g.inc(pool.tensor_tensor(l2s[s], x, x, ALU.mult), "sq%d" % s)
                    pool.wait_ge(l2_v.sem, l2_v.at("ep", l, i))
                    l2g.inc(pool.tensor_tensor(l2c, l2c, mhalf[:, 0:8], ALU.pow), "pw")
                with pool.Fori(0, 4) as i:
                    for s in range(2):
                        if s == 0:
                            pool.wait_ge(l2_v.sem, l2_v.at("nm1", l, 3))
                            wait_used(pool, u_proj[l] + U_PROJ - 1)
                        pool.wait_ge(dn_p.sem, dn_p.at("kS%d" % s, l, i - 1))
                        src = qkv[:, bass.ds(i * 2 + s, 17), :, PAD:PAD + P][:, 0:17:8]
                        dg.inc(pool.tensor_copy(kqv[s], src), "kqv%d" % s)
                    for s in range(2):
                        if s == 0:
                            pool.wait_ge(gat_v.sem, gat_v.at("beta", l))
                        pool.wait_ge(dn_v.sem, dn_v.at("ob%d" % s, l, i - 1))
                        pool.wait_ge(dn_a.sem, dn_a.at("VN%d" % s, l, i - 1))
                        dg.inc(pool.tensor_copy(hc[s].rearrange("p q d g -> p (q d g)"),
                                                GT[:, bass.ds(i * 2 + s, 1)].rearrange("p h q d g -> p (h q d g)")),
                               "hc%d" % s)
                    for s in range(2):
                        pool.wait_ge(dn_a.sem, dn_a.at("ET%d" % s, l, i))
                        dg.inc(pool.tensor_tensor(ET[s], ET[s], two(K_TRI), ALU.mult), "EM%d" % s)
                    for s in range(2):
                        pool.wait_ge(dn_v.sem, dn_v.at("AI%d" % s, l, i))
                        pool.wait_ge(dn_p.sem, dn_p.at("V%d" % s, l, i - 1))
                        for d in range(2):
                            dg.inc(pool.tensor_tensor(XX[s][:, 1, d], AT[s][:, d],
                                                     con[:, K_LEV + (1 - d) * P:K_LEV + (2 - d) * P]
                                                     .rearrange("p (o k) -> p o k", o=1).to_broadcast([P, G, P]), ALU.mult), "XT%d" % s)
                    for s in range(2):
                        pool.wait_ge(dn_v.sem, dn_v.at("ms%d" % s, l, i))
                        dg.inc(pool.tensor_tensor(ors[s], oss[s], mhalf[:, 0:2], ALU.pow), "rs%d" % s)
                        pool.wait_ge(dn_a.sem, dn_a.at("Sf%d" % s, l, i))
                        pool.dma_start(A["s_out%d" % l][0, :, bass.ds(i * 2 + s, 1)].rearrange("d h k v -> k (d h) v"),
                                       sfo[s]).then_inc(s_state[s], 16)
                with pool.Fori(0, 4) as i:
                    for s in range(2):
                        if s == 0:
                            pool.wait_ge(rp_v.sem, rp_v.at("x2", l))
                            pool.wait_ge(dn_v.sem, dn_v.at("y1", l, 3))
                        pool.wait_ge(at_p.sem, at_p.at("qt%d" % s, l, i - 1))
                        ag.inc(pool.tensor_copy(qst[s], tok[:, :, bass.ds(i * P + 4 * P * s, P)]), "q%d" % s)
                pool.wait_ge(evac.sem, evac.at("b2", l, 2))
                for n, c in (("k", T_K), ("v", T_V)):
                    pool.dma_start(A["%s_out%d" % (n, l)][0], tok[:, 0, c:c + 256].rearrange("p (h d) -> p h d", h=HKV))\
                        .then_inc(s_out, 16)
                rstd_(l, 1)
                rstd_(l, 2)
                rstd_(l, 3)
            for s in range(2):
                pool.wait_ge(s_state[s], 16 * 4 * DEPTH)
            pool.wait_ge(res_v.sem, res_v.at("x", 1, 1))
            for g in range(G):
                pool.dma_start(A["y_out%d" % g][0], xt[:, g, :]).then_inc(s_out, 16)
            pool.wait_ge(s_out, 32 * DEPTH + 32)

        @block.scalar
        def _(act):
            for s in A_STEPS:
                act.sem_inc(s.sem, s.per)
            (oi, orr, onr, oev, oga, ocv, onl, odn, okt, oat, oout, off, ort, omo) = (Order(s) for s in A_STEPS)
            AC = act.activation
            act.wait_ge(s_in, 16 * 6)
            oi.inc(AC(condS, cond, ACT.Silu), "cond")

            def ss_(l, k, src, ready_):
                for g in range(G):
                    ready_(g)
                    if g or l or k:
                        act.wait_ge(rms_a.sem, rms_a.at("ss", l, k) - 2 + g)
                    orr.inc(AC(sqj, src(g), ACT.Square, accum_out=ss[:, g:g + 1]), "ss")

            def norm_(l, n):
                for g in range(G):
                    for h in range(2):
                        act.wait_ge(nrm_p.sem, nrm_p.at("t%d%d" % (g, h), l, n))
                        onr.inc(AC(h_t[:, 4 * h:4 * h + 4, g * P:(g + 1) * P],
                                   ps[:, 4 * g + h, :].rearrange("p (k t) -> p k t", k=4), ACT.Copy), "e%d%d" % (g, h))

            for l in range(DEPTH):
                def x_there(g):
                    if l:
                        act.wait_ge(res_v.sem, res_v.at("x", 0, 1) - 1 + g)
                ss_(l, 0, lambda g: xt[:, g, :], x_there)
                norm_(l, 0)
                act.wait_ge(gat_v.sem, gat_v.at("ba", l))
                oga.inc(AC(eb, ba[:, :, 0:16], ACT.Exp, scale=-1.0), "eb")
                act.wait_ge(s_lay, 16 * LAY_DMAS * (l + 1))
                oga.inc(AC(ealog, alog, ACT.Exp), "ea")
                act.wait_ge(gat_v.sem, gat_v.at("na", l))
                oga.inc(AC(ga[2], ga[1], ACT.Exp), "el")
                act.wait_ge(gat_v.sem, gat_v.at("e1", l))
                oga.inc(AC(ga[3], ga[2], ACT.Ln), "ln")
                with act.Fori(0, 2) as i:
                    for j in range(3):
                        wait_used(act, u_proj[l] + 2 * j + 1, i)
                        if j == 0:
                            act.wait_ge(lay_g.sem, lay_g.at("pads", l))
                        oev.inc(AC(qkv[:, bass.ds(i * 12 + 4 * j, 4), :, PAD:PAD + P],
                                   ps[:, 2 + 2 * j:4 + 2 * j, :].rearrange("p b (c g t) -> p (b c) g t", c=2, g=G),
                                   ACT.Copy), "b%d" % j)
                act.wait_ge(gat_v.sem, gat_v.at("kd", l))
                oga.inc(AC(gex[:, 0:32], gcs[:, 0:32], ACT.Exp), "ex")
                oga.inc(AC(gex[:, 32:64], gcs[:, 32:64], ACT.Exp), "ex")
                with act.Fori(0, 3) as i:
                    for j in range(3):
                        wait_used(act, u_proj[l] + 12 + 2 * j + 1, i)
                        oev.inc(AC(tok[:, :, bass.ds(i * 1536 + 512 * j, 512)], ps[:, 2 + 2 * j:4 + 2 * j, :], ACT.Copy),
                                "b%d" % j)
                        for c in ((0, 1, 2), (3, 4, 5), (6, 7))[j]:
                            act.wait_ge(cnv_v.sem, i * (4 * cnv_v.per) + cnv_v.at("t%d%d" % (TAPS - 1, c % 2), l, c // 2))
                            ocv.inc(AC(qkv[:, bass.ds(i * 8 + c, 1), :, PAD:PAD + P],
                                       acc[c % 2].rearrange("p (o g) t -> p o g t", o=1), ACT.Silu), "s%d" % (c % 2))
                act.wait_ge(evac.sem, evac.at("b2", l, 4))
                z = tok[:, :, T_Z:T_Z + D]
                onl.inc(AC(z, z, ACT.Silu), "z")
                gt = tok[:, :, T_GA:COLS]
                onl.inc(AC(gt, gt, ACT.Sigmoid), "sig")
                with act.Fori(0, 4) as i:
                    for s in range(2):
                        act.wait_ge(dn_p.sem, dn_p.at("tr%d" % s, l, i))
                        act.wait_ge(dn_p.sem, dn_p.at("SF%d" % s, l, i - 1))
                        if s == 0:
                            act.wait_ge(l2_v.sem, l2_v.at("nm1", l, 3))
                        odn.inc(AC(ktv[s], ps[:, 3 * s, 0:384].rearrange("p (a b) -> p a b", a=3), ACT.Copy), "tok%d" % s)
                    for s in range(2):
                        act.wait_ge(dn_v.sem, dn_v.at("t%d" % s, l, i))
                        odn.inc(AC(ET[s], ET[s], ACT.Exp), "ET%d" % s)
                    for v in lv:
                        for s in range(2):
                            act.wait_ge(dn_p.sem, dn_p.at("b%d_%d" % (v, s), l, i))
                            if v < LEVELS - 1:
                                odn.inc(AC(XX[s].rearrange("p x d g t -> p x (d g t)"), ps[:, 3 * s + 1:3 * s + 3, :], ACT.Copy),
                                        "E%d_%d" % (v, s))
                            else:
                                odn.inc(AC(XX[s][:, 1].rearrange("p d g t -> p (d g t)"), ps[:, 3 * s + 2, :], ACT.Copy),
                                        "E%d_%d" % (v, s))
                    for s in range(2):
                        act.wait_ge(dn_p.sem, dn_p.at("V%d" % s, l, i))
                        for d in range(2):
                            for g in range(G):
                                odn.inc(AC(VN[s][:, d, g], ps[:, 3 * s + 1, (2 * d + g) * P:(2 * d + g + 1) * P], ACT.Copy,
                                           scale=hc[s][:, 4, d, g:g + 1]), "VN%d" % s)
                    for s in range(2):
                        act.wait_ge(dn_p.sem, dn_p.at("SF%d" % s, l, i))
                        act.wait_ge(s_state[s], i * 16 + 64 * l)
                        odn.inc(AC(sfo[s], ps[:, 3 * s + 1, 0:256].rearrange("p (a b) -> p a b", a=2), ACT.Copy), "Sf%d" % s)
                    for s in range(2):
                        act.wait_ge(dn_v.sem, dn_v.at("ob%d" % s, l, i))
                        for g in range(G):
                            odn.inc(AC(junk[s][:, g], osb[s][:, g], ACT.Square, accum_out=oss[s][:, g:g + 1]), "sq%d" % s)
                act.wait_ge(kt_p.sem, kt_p.at("k", l))
                okt.inc(AC(kTb[:, 0], ps[:, 0, 0:384].rearrange("p (a b) -> p a b", a=3), ACT.Copy), "k")
                okt.inc(AC(kTb[:, 1], ps[:, 1, 0:384].rearrange("p (a b) -> p a b", a=3), ACT.Copy), "o")
                with act.Fori(0, 4) as i:
                    for s in range(2):
                        act.wait_ge(at_p.sem, at_p.at("qt%d" % s, l, i))
                        act.wait_ge(at_p.sem, at_p.at("sc%d" % s, l, i - 1))
                        oat.inc(AC(qT[s], ps[:, 4 * s, 0:256].rearrange("p (a b) -> p a b", a=2), ACT.Copy, scale=SCALE), "qe%d" % s)
                    for s in range(2):
                        act.wait_ge(at_v.sem, at_v.at("nm%d" % s, l, i))
                        act.wait_ge(at_p.sem, at_p.at("pt%d" % s, l, i - 1))
                        for g in range(G):
                            oat.inc(AC(pr[s][:, g:1 + 2 * g], ps[:, 4 * s + 1, g * P:(1 + 2 * g) * P]
                                       .rearrange("p (a b) -> p a b", b=P), ACT.Exp, bias=am[s][2][:, g:g + 1],
                                       accum_out=am[s][3][:, g:g + 1]), "P%d" % s)
                    for s in range(2):
                        act.wait_ge(at_v.sem, at_v.at("sd%d" % s, l, i))
                        oat.inc(AC(am[s][5][:, 0:2], am[s][4][:, 0:2], ACT.Exp), "se%d" % s)
                    for s in range(2):
                        act.wait_ge(at_p.sem, at_p.at("pt%d" % s, l, i))
                        act.wait_ge(at_p.sem, at_p.at("pv%d" % s, l, i - 1))
                        oat.inc(AC(prT[s], ps[:, 4 * s + 2, 0:384].rearrange("p (a b) -> p a b", a=3), ACT.Copy), "pe%d" % s)
                for j in range(8):
                    b, g, h = j // 4, j // 2 % 2, j % 2
                    act.wait_ge(out_p.sem, out_p.at("tr%d" % j, l))
                    oout.inc(AC((oaT, obT)[b][:, 4 * h:4 * h + 4, g * P:(g + 1) * P],
                                ps[:, j, :].rearrange("p (k t) -> p k t", k=4), ACT.Copy), "ev%d" % j)
                for j in range(4):
                    g, h = j // 2, j % 2
                    act.wait_ge(out_p.sem, out_p.at("mt%d" % j, l))
                    oout.inc(AC(oaT[:, 4 * h:4 * h + 4, g * P:(g + 1) * P],
                                ps[:, j, :].rearrange("p (k t) -> p k t", k=4), ACT.Copy), "me%d" % j)
                ss_(l, 1, lambda g: y_sb[:, g, :], lambda g: act.wait_ge(out_v.sem, out_v.at("y", l) - 1 + g))
                ss_(l, 2, lambda g: xt[:, g, :], lambda g: act.wait_ge(res_v.sem, res_v.at("x", l, 0) - 1 + g))
                norm_(l, 1)
                act.wait_ge(s_out, 32 * (l + 1))
                if l == 0:
                    def gate(i):
                        act.wait_ge(ff_v.sem, ff_v.at("mu", 0, i - 1))
                        for g in range(G):
                            off.inc(AC(f_hs[0][:, 256 * g:256 * g + 256], ps[:, g, 0:256], ACT.Silu), "si")

                    def one(s, i, first=False):
                        if first:
                            wait_used(act, u_ff + 1)
                        else:
                            act.wait_ge(unit_used, i * 3 + (u_ff + 1 + RING))
                        gate(i)
                        act.wait_ge(ff_p.sem, ff_p.at("ht", 0, i))
                        off.inc(AC(f_hT[s].rearrange("p a b -> p (a b)"), ps[:, 2 + s, :], ACT.Copy), "he")

                    one(0, 0, True)
                    with act.Fori(0, (FF_STEPS - 1) // 2) as i:
                        for j in range(2):
                            one((1 + j) % 2, i * 2 + (1 + j))
                else:
                    act.wait_ge(rt_v.sem, rt_v.at("d"))
                    ort.inc(AC(rcol[3], rcol[2], ACT.Exp), "ex")

                    def expert(i):
                        for h in range(2):
                            act.wait_ge(moe_p.sem, moe_p.at("ga%d" % h, 0, i))
                            omo.inc(AC(hTe[:, 4 * h:4 * h + 4], ps[:, 6 + h, :].rearrange("p (k t) -> p k t", k=4), ACT.Copy),
                                    "ge%d" % h)
                        for f in range(FB):
                            wait_used(act, u_moe + gu_last(f), i * (U_EXP // RING))
                            if f == 0:
                                act.wait_ge(moe_v.sem, moe_v.at("mu%d" % (FB - 1), 0, i - 1))
                            else:
                                act.wait_ge(moe_v.sem, moe_v.at("mu%d" % (f - 1), 0, i))
                            omo.inc(AC(f_hs[0], ps[:, 0, :], ACT.Silu), "si%d" % f)
                            act.wait_ge(moe_p.sem, moe_p.at("ht%d" % f, 0, i))
                            omo.inc(AC(f_hT[f % 2].rearrange("p a b -> p (a b)"), ps[:, 2 + f % 2, :], ACT.Copy), "he%d" % f)

                    with act.Fori(0, NEXP) as e:
                        expert(e)
                    second_blocks(act, lambda e, x: expert(x + NEXP))
                ss_(l, 3, lambda g: y_sb[:, g, :], lambda g: act.wait_ge(ffe_v.sem, ffe_v.at("y", l) - 1 + g))

        @block.tensor
        def _(pe):
            for s in P_STEPS:
                pe.sem_inc(s.sem, s.per)
            (oi, onr, oga, ol2, odn, okt, oat, oout, ore, off, ort, omo) = (Order(s) for s in P_STEPS)
            mm = pe.matmul

            def tr(out, src, n=P):
                return pe.transpose(out, src, con[0:n, K_ID:K_ID + n])

            pe.wait_ge(init_a.sem, init_a.at("cond"))
            for k in range(KC):
                ins = tr(ps[:, 0, 2 * k:2 * k + 2], condS[:, k * P:(k + 1) * P], 2)
            oi.inc(ins, "condT")
            pe.wait_ge(init_v.sem, init_v.at("condT"))

            def used(ins, n=1):
                ins.then_inc(unit_used, n)

            def bcast(bank, m, g):
                q, c = MODS[m]
                for n in range(2):
                    ins = mm(ps[:, bank + n, :], con[32 * q:32 * q + 2, K_SEL + g * P:K_SEL + (g + 1) * P],
                             mod_row(q, c, n), start=True, stop=True)
                return ins

            def norm_(l, n):
                for g in range(G):
                    bcast(4 * g, (1, 4)[n], g)
                    onr.inc(bcast(4 * g + 2, (0, 3)[n], g), "bc%d" % g)
                for g in range(G):
                    pe.wait_ge(nrm_v.sem, nrm_v.at("h%d" % g, l, n))
                    for h in range(2):
                        for k in range(4):
                            ins = tr(ps[:, 4 * g + h, k * P:(k + 1) * P], h_tok[:, g, (4 * h + k) * P:(4 * h + k + 1) * P])
                        onr.inc(ins, "t%d%d" % (g, h))
                pe.wait_ge(nrm_a.sem, nrm_a.at("e11", l, n))

            for l in range(DEPTH):
                if l:
                    pe.wait_ge(res_v.sem, res_v.at("x", l - 1, 1))
                with pe.Fori(0, 4) as i:
                    for j in range(3):
                        pe.wait_ge(ada_v.sem, i * 3 + (ada_v.at("row", l) - 12 + j - 2))
                        for h in range(2):
                            u = u_ada[l] + 2 * j + h
                            wait_unit(pe, u, i)
                            for k in range(4):
                                ins = mm(ps[0:2, j, :], condT[:, 4 * h + k, :], unit(u)[:, k * 512:(k + 1) * 512],
                                         start=(h + k == 0), stop=(h == 1 and k == 3))
                            used(ins)
                pe.wait_ge(ada_v.sem, ada_v.at("mod", l))
                if l:
                    pe.wait_ge(res_v.sem, res_v.at("x", l - 1, 1))
                norm_(l, 0)
                pe.wait_ge(s_lay, 16 * LAY_DMAS * (l + 1))
                for g in range(G):
                    for k in range(KC):
                        ins = mm(ps[:, 0, 32 * g:32 * g + 32], h_t[:, k, g * P:(g + 1) * P], wba[:, k, :],
                                 start=(k == 0), stop=(k == KC - 1))
                oga.inc(ins, "ba")
                oga.inc(tr(ps[:, 0, P:P + TAPS * QKV_CH], cwr[0:TAPS * QKV_CH, :], TAPS * QKV_CH), "cw")
                with pe.Fori(0, 2) as i:
                    for j in range(3):
                        u = u_proj[l] + 2 * j
                        pe.wait_ge(evac.sem, evac.at("b%d" % j, l, i - 1))
                        wait_unit(pe, u, i)
                        wait_unit(pe, u + 1, i)
                        for c in range(4):
                            for k in range(KC):
                                ins = mm(ps[:, 2 + 2 * j + c // 2, c % 2 * 256:c % 2 * 256 + 256],
                                         unit(u + k // 4)[:, k % 4 * 512 + c * P:k % 4 * 512 + (c + 1) * P],
                                         h_t[:, k, :], start=(k == 0), stop=(k == KC - 1))
                        used(ins, 2)
                pe.wait_ge(gat_v.sem, gat_v.at("g0", l))
                for d in range(2):
                    gd = ga[4][:, :, 8 * d:8 * d + 8]
                    mm(ps[:, 1, 16 * d:16 * d + 16], tri(d), gd, start=True, stop=True)
                    ins = mm(ps[:, 1, 32 + 16 * d:48 + 16 * d], ones, gd, start=True, stop=True)
                oga.inc(ins, "gc")
                with pe.Fori(0, 3) as i:
                    for j in range(3):
                        pe.wait_ge(evac.sem, i * evac.per + evac.at("b%d" % j, l, 1))
                        for h in range(2):
                            u = u_proj[l] + 12 + 2 * j + h
                            wait_unit(pe, u, i)
                            for k in range(4):
                                for g in range(G):
                                    ins = mm(ps[:, 2 + 2 * j + g, :], h_t[:, 4 * h + k, g * P:(g + 1) * P],
                                             unit(u)[:, k * 512:(k + 1) * 512], start=(h + k == 0), stop=(h == 1 and k == 3))
                            used(ins)
                pe.wait_ge(gat_v.sem, gat_v.at("gcs", l))
                pe.wait_ge(evac.sem, evac.at("b2", l, 4))
                with pe.Fori(0, 4) as i:
                    pe.wait_ge(l2_g.sem, l2_g.at("sq1", l, i))
                    pe.wait_ge(l2_v.sem, l2_v.at("nm1", l, i - 1))
                    for s in range(2):
                        for c in range(2):
                            for g in range(G):
                                ins = mm(ps[:, 0, 4 * s + 2 * c + g:4 * s + 2 * c + g + 1], l2s[s][:, c, g], ones[:, 0:1],
                                         start=True, stop=True)
                    ol2.inc(ins, "ss")
                    pe.wait_ge(l2_g.sem, l2_g.at("pw", l, i))
                    for s in range(2):
                        for x in range(4):
                            ins = mm(ps[:, 6 + s, x * P:(x + 1) * P], l2c[:, 4 * s + x:4 * s + x + 1].to_broadcast([P, P]), ident,
                                     start=True, stop=True)
                        ol2.inc(ins, "bc%d" % s)
                pe.wait_ge(l2_v.sem, l2_v.at("ep", l, 3))
                with pe.Fori(0, 4) as i:
                    def each(f):
                        for s in range(2):
                            f(s, 3 * s)

                    def inst():
                        return [(d, g, (2 * d + g) * P) for d in range(2) for g in range(G)]

                    def turn(s, b):
                        pe.wait_ge(dn_g.sem, dn_g.at("kqv%d" % s, l, i))
                        pe.wait_ge(dn_v.sem, dn_v.at("ob%d" % s, l, i - 1))
                        tr(ps[:, b, 0:P], kqv[s][:, 1, 0])
                        tr(ps[:, b, P:2 * P], kqv[s][:, 2, 0])
                        odn.inc(tr(ps[:, b, 2 * P:3 * P], kqv[s][:, 2, 1]), "tr%d" % s)
                    each(turn)

                    def gram(s, b):
                        pe.wait_ge(dn_a.sem, dn_a.at("Sf%d" % s, l, i - 1))
                        for g in range(G):
                            ins = mm(ps[:, b + 1, 256 * g:256 * g + 256], kqv[s][:, 1, g], kqv[s][:, 0:2, g, :], start=True, stop=True)
                        odn.inc(ins, "G%d" % s)
                    each(gram)

                    def decay(s, b):
                        pe.wait_ge(dn_g.sem, dn_g.at("hc%d" % s, l, i))
                        pe.wait_ge(dn_v.sem, dn_v.at("oc%d" % s, l, i - 1))
                        for d, g, c in inst():
                            ins = mm(ps[:, b + 2, c:c + P], hc[s][:, 0, d, g:g + 1].to_broadcast([P, P]), tri(d), start=True, stop=True)
                        odn.inc(ins, "gr%d" % s)
                    each(decay)

                    def first(s, b):
                        pe.wait_ge(dn_v.sem, dn_v.at("AI%d" % s, l, i))
                        pe.wait_ge(dn_a.sem, dn_a.at("tok%d" % s, l, i))
                        for d, g, c in inst():
                            ins = tr(ps[:, b, c:c + P], AT[s][:, d, g])
                        odn.inc(ins, "m%d" % s)
                    each(first)
                    for v in lv:
                        def left(s, b):
                            if v == 1:
                                pe.wait_ge(dn_v.sem, dn_v.at("X%d" % s, l, i))
                            else:
                                pe.wait_ge(dn_a.sem, dn_a.at("E%d_%d" % (v - 1, s), l, i))
                            for d, g, c in inst():
                                ins = mm(ps[:, b, c:c + P], AT[s][:, d, g], XX[s][:, 0, d, g], start=True, stop=True)
                            odn.inc(ins, "a%d_%d" % (v, s))
                        each(left)

                        def right(s, b):
                            if v == 1:
                                pe.wait_ge(dn_g.sem, dn_g.at("XT%d" % s, l, i))
                                pe.wait_ge(dn_v.sem, dn_v.at("AI%d" % s, l, i))
                            pe.wait_ge(dn_v.sem, dn_v.at("M%d_%d" % (v, s), l, i))
                            for d, g, c in inst():
                                if v < LEVELS - 1:
                                    mm(ps[:, b + 1, c:c + P], XX[s][:, 1, d, g], MM[s][:, d, g], start=True, stop=True)
                                ins = mm(ps[:, b + 2, c:c + P], MM[s][:, d, g], XX[s][:, 1, d, g], start=True, stop=True)
                            odn.inc(ins, "b%d_%d" % (v, s))
                        each(right)

                    def state(s, b):
                        for x in range(2):
                            ins = mm(ps[:, b, 256 * x:256 * x + 256], kqv[s][:, 1 - x, 1],
                                     s0[:, bass.ds(i * 2 + s, 1)].rearrange("p h d v -> p (h d v)"), start=True, stop=True)
                        odn.inc(ins, "kS%d" % s)
                    each(state)

                    def values(s, b):
                        pe.wait_ge(dn_a.sem, dn_a.at("E%d_%d" % (LEVELS - 1, s), l, i))
                        pe.wait_ge(dn_v.sem, dn_v.at("R%d" % s, l, i))
                        for d, g, c in inst():
                            ins = mm(ps[:, b + 1, c:c + P], XX[s][:, 1, d, g], RP[s][:, d] if g else ktv[s][:, 1],
                                     start=True, stop=True)
                        odn.inc(ins, "V%d" % s)
                    each(values)

                    def out(s, b):
                        pe.wait_ge(dn_a.sem, dn_a.at("VN%d" % s, l, i))
                        for g in range(G):
                            for d in range(2):
                                ins = mm(ps[:, b + 2, g * P:(g + 1) * P], attn[s][:, d, g], VN[s][:, d, g],
                                         start=(d == 0), stop=(d == 1))
                        odn.inc(ins, "O%d" % s)
                    each(out)

                    def final(s, b):
                        pe.wait_ge(dn_v.sem, dn_v.at("VD%d" % s, l, i))
                        odn.inc(mm(ps[:, b + 1, 0:256], ktv[s][:, 0], VD[s].rearrange("p d v -> p (d v)"),
                                   start=True, stop=True), "SF%d" % s)
                    each(final)
                pe.wait_ge(rp_v.sem, rp_v.at("x2", l))
                pe.wait_ge(dn_v.sem, dn_v.at("y1", l, 3))
                pe.wait_ge(dn_a.sem, dn_a.at("sq1", l, 3))
                for v in range(HKV):
                    tr(ps[:, v, 0:P], tok[:, 0, T_K + v * P:T_K + (v + 1) * P])
                    tr(ps[:, v, P:2 * P], cache_k[:, v, :])
                    ins = tr(ps[:, v, 2 * P:3 * P], tok[:, 1, T_K + v * P:T_K + (v + 1) * P])
                okt.inc(ins, "k")
                pe.wait_ge(kt_a.sem, kt_a.at("o", l))
                with pe.Fori(0, 4) as i:
                    for s in range(2):
                        pe.wait_ge(at_g.sem, at_g.at("q%d" % s, l, i))
                        pe.wait_ge(at_a.sem, at_a.at("qe%d" % s, l, i - 1))
                        tr(ps[:, 4 * s, 0:P], qst[s][:, 0])
                        oat.inc(tr(ps[:, 4 * s, P:2 * P], qst[s][:, 1]), "qt%d" % s)
                    for s in range(2):
                        pe.wait_ge(at_a.sem, at_a.at("qe%d" % s, l, i))
                        pe.wait_ge(at_a.sem, at_a.at("P%d" % s, l, i - 1))
                        mm(ps[:, 4 * s + 1, 0:P], qT[s][:, 0], kTb[:, s, 0], start=True, stop=True)
                        oat.inc(mm(ps[:, 4 * s + 1, P:3 * P], qT[s][:, 1], kTb[:, s, 1:3].rearrange("p a b -> p (a b)"),
                                   start=True, stop=True), "sc%d" % s)
                    for s in range(2):
                        pe.wait_ge(at_a.sem, at_a.at("P%d" % s, l, i))
                        pe.wait_ge(at_a.sem, at_a.at("pe%d" % s, l, i - 1))
                        for k in range(3):
                            ins = tr(ps[:, 4 * s + 2, k * P:(k + 1) * P], pr[s][:, k])
                        oat.inc(ins, "pt%d" % s)
                    for s in range(2):
                        pe.wait_ge(at_a.sem, at_a.at("pe%d" % s, l, i))
                        pe.wait_ge(at_v.sem, at_v.at("o%d" % s, l, i - 1))
                        mm(ps[:, 4 * s + 3, 0:P], prT[s][:, 0], tok[:, 0, T_V + s * P:T_V + (s + 1) * P], start=True, stop=True)
                        mm(ps[:, 4 * s + 3, P:2 * P], prT[s][:, 1], cache_v[:, s, :], start=True, stop=False)
                        oat.inc(mm(ps[:, 4 * s + 3, P:2 * P], prT[s][:, 2], tok[:, 1, T_V + s * P:T_V + (s + 1) * P],
                                   start=False, stop=True), "pv%d" % s)
                pe.wait_ge(at_v.sem, at_v.at("o1", l, 3))
                for j in range(8):
                    b, g, h = j // 4, j // 2 % 2, j % 2
                    for k in range(4):
                        c = (0, T_Z)[b] + (4 * h + k) * P
                        ins = tr(ps[:, j, k * P:(k + 1) * P], tok[:, g, c:c + P])
                    oout.inc(ins, "tr%d" % j)
                pe.wait_ge(out_a.sem, out_a.at("ev7", l))
                u = [u_out[l]]

                def project(src, bank):
                    for n in range(2):
                        for h in range(2):
                            wait_unit(pe, u[0])
                            for k in range(4):
                                for g in range(G):
                                    ins = mm(ps[:, bank(n, g), :], src[:, 4 * h + k, g * P:(g + 1) * P],
                                             unit(u[0])[:, k * 512:(k + 1) * 512], start=(h + k == 0), stop=(h == 1 and k == 3))
                            used(ins)
                            u[0] += 1
                project(oaT, lambda n, g: 2 * n + g)
                project(obT, lambda n, g: 4 + 2 * n + g)
                pe.wait_ge(out_v.sem, out_v.at("m", l))
                for j in range(4):
                    g, h = j // 2, j % 2
                    for k in range(4):
                        c = T_GA + (4 * h + k) * P
                        ins = tr(ps[:, j, k * P:(k + 1) * P], tok[:, g, c:c + P])
                    oout.inc(ins, "mt%d" % j)
                pe.wait_ge(out_a.sem, out_a.at("me3", l))
                project(oaT, lambda n, g: 4 + 2 * g + n)

                def gate_rows(n):
                    for g in range(G):
                        ins = bcast(2 * g, (2, 5)[n], g)
                    ore.inc(ins, "gb")
                gate_rows(0)
                pe.wait_ge(res_v.sem, res_v.at("x", l, 0))
                norm_(l, 1)
                if l == 0:
                    def gate_up(u, i, f):
                        pe.wait_ge(ff_v.sem, ff_v.at("mu", 0, f - 1))
                        for x in range(2):
                            wait_unit(pe, u + x, i)
                            for g in range(G):
                                for k in range(KC):
                                    ins = mm(ps[:, g, 256 * x:256 * x + 256], h_t[:, k, g * P:(g + 1) * P],
                                             unit(u + x)[:, k * 256:(k + 1) * 256], start=(k == 0), stop=(k == KC - 1))
                            used(ins)

                    def down(u, i, f, s, at_=None):
                        pe.wait_ge(ff_v.sem, ff_v.at("mu", 0, f))
                        for k in range(4):
                            ins = tr(ps[:, 2 + s, k * P:(k + 1) * P], f_hid[s][:, k * P:(k + 1) * P])
                        off.inc(ins, "ht")
                        pe.wait_ge(ff_a.sem, ff_a.at("he", 0, f))
                        wait_unit(pe, u, i)
                        for k in range(2):
                            for g in range(G):
                                for n in range(2):
                                    ins = mm(ps[:, 4 + 2 * g + n, :], f_hT[s][:, 2 * g + k],
                                             unit(u)[:, k * 1024 + n * 512:k * 1024 + (n + 1) * 512],
                                             start=(at_ == 0 and k == 0), stop=(at_ == 1 and k == 1))
                        used(ins)
                    gate_up(u_ff, 0, 0)
                    gate_up(u_ff + 2, 0, 1)
                    down(u_ff + 4, 0, 0, 0, 0)
                    with pe.Fori(0, (FF_STEPS - 3) // 2) as i:
                        for j in range(2):
                            gate_up(u_ff + 5 + 3 * j, i, i * 2 + (2 + j))
                            down(u_ff + 7 + 3 * j, i, i * 2 + (1 + j), (1 + j) % 2)
                    w = u_ff + 3 * FF_STEPS - 4
                    gate_up(w, 0, FF_STEPS - 1)
                    down(w + 2, 0, FF_STEPS - 2, 1)
                    down(w + 3, 0, FF_STEPS - 1, 0, 1)
                else:
                    for g in range(G):
                        for k in range(KC):
                            ins = mm(ps[:, 0, NEXP * g:NEXP * (g + 1)], h_t[:, k, g * P:(g + 1) * P], wr[:, k, :],
                                     start=(k == 0), stop=(k == KC - 1))
                    ort.inc(ins, "lg")
                    pe.wait_ge(rt_v.sem, rt_v.at("mk"))
                    before = con[:, K_STR:K_STR + P]
                    mk = rt[6]
                    mm(ps[:, 1, 0:8], before, mk[:, 0], start=True, stop=True)
                    mm(ps[:, 1, 8:16], before, mk[:, 1], start=True, stop=False)
                    mm(ps[:, 1, 8:16], ones, mk[:, 0], start=False, stop=True)
                    mm(ps[:, 1, 16:24], ones, mk[:, 0], start=True, stop=False)
                    ort.inc(mm(ps[:, 1, 16:24], ones, mk[:, 1], start=False, stop=True), "pos")
                    pe.wait_ge(rt_v.sem, rt_v.at("pos"))

                    def expert(i):
                        r = i * (U_EXP // RING)
                        pe.wait_ge(moe_v.sem, moe_v.at("selc", 0, i))
                        pe.wait_ge(moe_v.sem, moe_v.at("add", 0, i - 1))
                        for g in range(G):
                            ins = tr(ps[:, 2, g * P:(g + 1) * P], selc[:, g])
                        omo.inc(ins, "sct")
                        for h in range(2):
                            for k in range(4):
                                for g in range(G):
                                    ins = mm(ps[:, 6 + h, k * P:(k + 1) * P], h_tok[:, g, (4 * h + k) * P:(4 * h + k + 1) * P],
                                             sel[:, g], start=(g == 0), stop=(g == 1))
                            omo.inc(ins, "ga%d" % h)
                        pe.wait_ge(moe_a.sem, moe_a.at("ge1", 0, i))
                        pe.wait_ge(moe_v.sem, moe_v.at("selT", 0, i))
                        u = u_moe
                        for f in range(FB + 1):
                            if f < FB:
                                pe.wait_ge(moe_v.sem, moe_v.at("mu%d" % (f - 1), 0, i) if f else moe_v.at("mu%d" % (FB - 1), 0, i - 1))
                                for x in range(2):
                                    for h in range(2):
                                        wait_unit(pe, u, r)
                                        for k in range(4):
                                            ins = mm(ps[:, x, :], hTe[:, 4 * h + k], unit(u)[:, k * 512:(k + 1) * 512],
                                                     start=(h + k == 0), stop=(h == 1 and k == 3))
                                        used(ins)
                                        u += 1
                            if f > 0:
                                b = (f - 1) % 2
                                pe.wait_ge(moe_v.sem, moe_v.at("mu%d" % (f - 1), 0, i))
                                for k in range(4):
                                    ins = tr(ps[:, 2 + b, k * P:(k + 1) * P], f_hid[b][:, k * P:(k + 1) * P])
                                omo.inc(ins, "ht%d" % (f - 1))
                                pe.wait_ge(moe_a.sem, moe_a.at("he%d" % (f - 1), 0, i))
                                for h in range(2):
                                    wait_unit(pe, u, r)
                                    for k in range(2):
                                        for n in range(2):
                                            ins = mm(ps[:, 4 + n, :], f_hT[b][:, 2 * h + k],
                                                     unit(u)[:, k * 1024 + n * 512:k * 1024 + (n + 1) * 512],
                                                     start=(f == 1 and h + k == 0), stop=(f == FB and h + k == 2))
                                    used(ins)
                                    u += 1
                        pe.wait_ge(moe_v.sem, moe_v.at("ye", 0, i))
                        for g in range(G):
                            for n in range(2):
                                ins = mm(ps[:, (6, 2)[g] + n, :], selT[:, g], ye[:, n * 512:(n + 1) * 512], start=True, stop=True)
                            omo.inc(ins, "sc%d" % g)

                    with pe.Fori(0, NEXP) as e:
                        expert(e)
                    second_blocks(pe, lambda e, x: expert(x + NEXP))
                pe.wait_ge(ffe_v.sem, ffe_v.at("y", l))
                gate_rows(1)

        @block.vector
        def _(dve):
            for s in V_STEPS:
                dve.sem_inc(s.sem, s.per)
            (oi, oad, orm, onr, oga, ocv, onl, ol2, odn, orp, oat, oout, ore, off, ofe, ort, omo) = (Order(s) for s in V_STEPS)
            TT, TS, STT, CP = dve.tensor_tensor, dve.tensor_scalar, dve.scalar_tensor_tensor, dve.tensor_copy

            def own(st, name, l=0, i=0):
                dve.wait_ge(st.sem, st.at(name, l, i))

            oi.inc(dve.memset(mhalf, -0.5), "half")
            dve.wait_ge(init_p.sem, init_p.at("condT"))
            oi.inc(CP(condT, ps[:, 0, 0:16].rearrange("p (k c) -> p k c", c=2)), "condT")

            def ms_(l, k):
                dve.wait_ge(rms_a.sem, rms_a.at("ss", l, k))
                if k or l:
                    dve.wait_ge(rms_g.sem, rms_g.at("rstd", l, k - 1))
                orm.inc(TS(ms, ss, 1.0 / D, EPS, ALU.mult, ALU.add), "ms")

            def norm_(l, n):
                ms_(l, 2 * n)
                dve.wait_ge(rms_g.sem, rms_g.at("rstd", l, 2 * n))
                for g in range(G):
                    dve.wait_ge(nrm_p.sem, nrm_p.at("bc%d" % g, l, n))
                    onr.inc(STT(h_tok[:, g, :], xt[:, g, :], rstd[:, g:g + 1],
                                ps[:, 4 * g:4 * g + 2, :].rearrange("p b c -> p (b c)"), ALU.mult, ALU.mult), "a%d" % g)
                    own(nrm_v, "a%d" % g, l, n)
                    onr.inc(TT(h_tok[:, g, :], h_tok[:, g, :], ps[:, 4 * g + 2:4 * g + 4, :].rearrange("p b c -> p (b c)"), ALU.add),
                            "h%d" % g)

            def resid(l, n):
                ms_(l, 2 * n + 1)
                dve.wait_ge(rms_g.sem, rms_g.at("rstd", l, 2 * n + 1))
                dve.wait_ge(res_p.sem, res_p.at("gb", l, n))
                for g in range(G):
                    ore.inc(STT(y_sb[:, g, :], y_sb[:, g, :], rstd[:, g:g + 1],
                                ps[:, 2 * g:2 * g + 2, :].rearrange("p b c -> p (b c)"), ALU.mult, ALU.mult), "t")
                own(res_v, "t", l, n)
                for g in range(G):
                    ore.inc(TT(xt[:, g, :], xt[:, g, :], y_sb[:, g, :], ALU.add), "x")

            for l in range(DEPTH):
                dve.wait_ge(s_lay, 16 * LAY_DMAS * (l + 1))
                for b in range(12):
                    q, c = MODS[b // 2]
                    wait_used(dve, u_ada[l] + 2 * b + 1)
                    m = mod_row(q, c, b % 2)
                    oad.inc(TT(m, ps[0:2, b % 3, :], m, ALU.add), "row")
                own(ada_v, "row", l)
                for m in GAIN:
                    q, c = MODS[m]
                    mo, gn = mod[32 * q:32 * q + 2, c, :], ngr[32 * q:32 * q + 2, c, :]
                    oad.inc(STT(mo, mo, 1.0 if m in (1, 4) else 0.0, gn, ALU.add, ALU.mult), "mod")
                norm_(l, 0)
                dve.wait_ge(gat_p.sem, gat_p.at("cw", l))
                oga.inc(CP(cw[:, 0:TAPS * QKV_CH], ps[:, 0, P:P + TAPS * QKV_CH]), "cw")
                oga.inc(CP(ba, ps[:, 0, 0:64].rearrange("p (g c) -> p g c", g=G)), "ba")
                own(gat_v, "ba", l)
                oga.inc(TT(ga[0], ba[:, :, 16:32], dtb.rearrange("p (o c) -> p o c", o=1).to_broadcast([P, G, 16]), ALU.add), "a")
                own(gat_v, "a", l)
                oga.inc(STT(ga[1], ga[0], -1.0, ga[0], ALU.mult, ALU.min), "na")
                dve.wait_ge(gat_a.sem, gat_a.at("el", l))
                oga.inc(TS(ga[2], ga[2], 1.0, None, ALU.add), "e1")
                dve.wait_ge(gat_a.sem, gat_a.at("ln", l))
                oga.inc(STT(ga[3], ga[0], 0.0, ga[3], ALU.max, ALU.add), "sp")
                own(gat_v, "sp", l)
                oga.inc(STT(ga[4], ga[3], -1.0, ealog.rearrange("p (o c) -> p o c", o=1).to_broadcast([P, G, 16]),
                            ALU.mult, ALU.mult), "g0")
                own(gat_v, "g0", l)

                def dgh(q):
                    return [GT[:, :, q, :, g].rearrange("p h d -> p d h") for g in range(G)]

                def split(x):
                    return x.rearrange("p g (d h) -> p g d h", d=2)

                def to_gt(q):
                    return GT[:, :, q, :, :].rearrange("p h d g -> p g d h")
                oga.inc(CP(to_gt(0), split(ga[4])), "gcol")
                dve.wait_ge(gat_p.sem, gat_p.at("gc", l))
                oga.inc(CP(gcs, ps[:, 1, 0:64]), "gcs")
                own(gat_v, "gcs", l)
                oga.inc(TT(gcs[:, 32:64], gcs[:, 32:64], gcs[:, 0:32], ALU.subtract), "kd")

                def dirs(x):
                    return x.rearrange("p (d g h) -> p d g h", d=2, g=G)

                def to_dirs(q):
                    return GT[:, :, q, :, :].rearrange("p h d g -> p d g h")
                oga.inc(CP(to_dirs(1), dirs(gcs[:, 0:32])), "gc")
                dve.wait_ge(gat_a.sem, gat_a.at("ex", l))
                oga.inc(CP(to_dirs(2), dirs(gex[:, 0:32])), "egc")
                oga.inc(TS(to_dirs(3), dirs(gex[:, 0:32]), -1.0, None, ALU.mult), "negc")
                oga.inc(CP(to_dirs(5), dirs(gex[:, 32:64])), "ekd")
                oga.inc(TS(eb, eb, 1.0, None, ALU.add), "b1")
                own(gat_v, "b1", l)
                oga.inc(dve.reciprocal(eb, eb), "rb")
                own(gat_v, "rb", l)
                oga.inc(CP(to_gt(4), split(eb)), "beta")
                dve.wait_ge(evac.sem, evac.at("b2", l, 1))
                own(gat_v, "cw", l)
                with dve.Fori(0, QKV_CH // 2) as i:
                    for j in range(TAPS):
                        for s in range(2):
                            x = qkv[:, bass.ds(i * 2 + s, 1), :, j:j + P].rearrange("p o g t -> p (o g) t")
                            w = cw[:, bass.ds(i * 2 + (j * QKV_CH + s), 1)]
                            if j == 0:
                                dve.wait_ge(cnv_a.sem, cnv_a.at("s%d" % s, l, i - 1))
                                ocv.inc(TS(acc[s], x, w, None, ALU.mult), "t%d%d" % (j, s))
                            else:
                                own(cnv_v, "t%d%d" % (j - 1, s), l, i)
                                ocv.inc(STT(acc[s], x, w, acc[s], ALU.mult, ALU.add), "t%d%d" % (j, s))
                with dve.Fori(0, 4) as i:
                    dve.wait_ge(l2_p.sem, l2_p.at("ss", l, i))
                    dve.wait_ge(l2_p.sem, l2_p.at("bc1", l, i - 1))
                    ol2.inc(TS(l2c, ps[:, 0, 0:8], EPS, None, ALU.add), "ep")
                    for s in range(2):
                        x = qkv[:, bass.ds(i * 2 + 8 * s, 2), :, PAD:PAD + P].rearrange("p a g t -> p (a g) t")
                        dve.wait_ge(l2_p.sem, l2_p.at("bc%d" % s, l, i))
                        ol2.inc(STT(x, x, SCALE if s == 0 else 1.0, ps[:, 6 + s, :].rearrange("p (a t) -> p a t", a=4),
                                    ALU.mult, ALU.mult), "nm%d" % s)
                dve.wait_ge(nl_a.sem, nl_a.at("z", l))
                z = tok[:, :, T_Z:T_Z + D].rearrange("p g (h v) -> p g h v", h=DH)
                onl.inc(TT(z, z, dng[:, :].rearrange("p (a b v) -> p a b v", a=1, b=1).to_broadcast([P, G, DH, P]), ALU.mult), "z")
                with dve.Fori(0, 4) as i:
                    def each(f):
                        for s in range(2):
                            f(s, 3 * s)

                    def w4(s, name):
                        own(dn_v, name % s, l, i)

                    def clamp(s, b):
                        dve.wait_ge(dn_p.sem, dn_p.at("gr%d" % s, l, i))
                        dve.wait_ge(dn_g.sem, dn_g.at("hc%d" % s, l, i))
                        for d in range(2):
                            for g in range(G):
                                c = (2 * d + g) * P
                                odn.inc(TS(ET[s][:, d, g], ps[:, b + 2, c:c + P], hc[s][:, 1, d, g:g + 1], 0.0,
                                           ALU.subtract, ALU.min), "t%d" % s)
                    each(clamp)

                    def pair(s, b, x):
                        return ps[:, b + 1, :].rearrange("p (o g x k) -> p o g x k", o=1, g=G, x=2)[:, :, :, x].to_broadcast([P, 2, G, P])

                    def attn_(s, b):
                        dve.wait_ge(dn_g.sem, dn_g.at("EM%d" % s, l, i))
                        dve.wait_ge(dn_p.sem, dn_p.at("G%d" % s, l, i))
                        dve.wait_ge(dn_p.sem, dn_p.at("O%d" % s, l, i - 1))
                        odn.inc(TT(attn[s], ET[s], pair(s, b, 0), ALU.mult), "at%d" % s)
                    each(attn_)

                    def w_(s, b):
                        odn.inc(TT(AT[s], ET[s], pair(s, b, 1), ALU.mult), "W%d" % s)
                    each(w_)

                    def a_(s, b):
                        w4(s, "W%d")
                        for d in range(2):
                            for g in range(G):
                                odn.inc(STT(AT[s][:, d, g], AT[s][:, d, g], hc[s][:, 4, d, g:g + 1],
                                            con[:, K_STR + d * P:K_STR + (d + 1) * P], ALU.mult, ALU.mult), "A%d" % s)
                    each(a_)

                    def ai(s, b):
                        w4(s, "A%d")
                        odn.inc(TT(AT[s], AT[s], ident.rearrange("p (a b k) -> p a b k", a=1, b=1).to_broadcast([P, 2, G, P]),
                                   ALU.add), "AI%d" % s)
                    each(ai)

                    def x_(s, b):
                        dve.wait_ge(dn_p.sem, dn_p.at("m%d" % s, l, i))
                        odn.inc(TT(XX[s][:, 0], ps[:, b, :].rearrange("p (d g k) -> p d g k", d=2, g=G), two(K_LEV), ALU.mult), "X%d" % s)
                    each(x_)
                    for v in lv:
                        def m_(s, b):
                            dve.wait_ge(dn_p.sem, dn_p.at("a%d_%d" % (v, s), l, i))
                            if v > 1:
                                dve.wait_ge(dn_p.sem, dn_p.at("b%d_%d" % (v - 1, s), l, i))
                            odn.inc(TT(MM[s], ps[:, b, :].rearrange("p (d g k) -> p d g k", d=2, g=G),
                                       two(K_LEV + 2 * v * P), ALU.mult), "M%d_%d" % (v, s))
                        each(m_)

                    def r_(s, b):
                        dve.wait_ge(dn_p.sem, dn_p.at("kS%d" % s, l, i))
                        for d in range(2):
                            odn.inc(STT(RP[s][:, d], ps[:, b, d * P:(d + 1) * P], hc[s][:, 3, d, 1:2], ktv[s][:, 2],
                                        ALU.mult, ALU.add), "R%d" % s)
                    each(r_)

                    def vd(s, b):
                        dve.wait_ge(dn_a.sem, dn_a.at("VN%d" % s, l, i))
                        for d in range(2):
                            odn.inc(TS(VD[s][:, d], VN[s][:, d, 0], hc[s][:, 5, d, 0:1], None, ALU.mult), "VD%d" % s)
                    each(vd)

                    def oc(s, b):
                        dve.wait_ge(dn_p.sem, dn_p.at("O%d" % s, l, i))
                        dve.wait_ge(dn_a.sem, dn_a.at("sq%d" % s, l, i - 1))
                        odn.inc(CP(osb[s].rearrange("p g v -> p (g v)"), ps[:, b + 2, 0:256]), "oc%d" % s)
                    each(oc)
                    for d in range(2):
                        def oa(s, b):
                            w4(s, ("oc%d", "oa%d")[d])
                            odn.inc(STT(osb[s][:, 1], ps[:, b, 256 + d * P:256 + (d + 1) * P], hc[s][:, 2, d, 1:2], osb[s][:, 1],
                                        ALU.mult, ALU.add), ("oa%d", "ob%d")[d] % s)
                        each(oa)

                    def msq(s, b):
                        dve.wait_ge(dn_a.sem, dn_a.at("sq%d" % s, l, i))
                        odn.inc(TS(oss[s], oss[s], 1.0 / P, EPS, ALU.mult, ALU.add), "ms%d" % s)
                    each(msq)

                    def y_(s, b):
                        dve.wait_ge(dn_g.sem, dn_g.at("rs%d" % s, l, i))
                        own(nl_v, "z", l)
                        for g in range(G):
                            zz = tok[:, g, bass.ds(i * 256 + (T_Z + P * s), P)]
                            odn.inc(STT(zz, osb[s][:, g], ors[s][:, g:g + 1], zz, ALU.mult, ALU.mult), "y%d" % s)
                    each(y_)
                own(dn_v, "y1", l, 3)
                dve.wait_ge(dn_p.sem, dn_p.at("SF1", l, 3))
                for s in range(2):
                    dve.wait_ge(s_state[s], 64 * (l + 1))
                xs = tok[:, 1, 0:1280].rearrange("p (h f x r) -> p h f x r", h=10, f=2, x=2)
                x1, x2 = xs[:, :, :, 0], xs[:, :, :, 1]
                cos, sin = (con[:, K_ROPE + 64 * j:K_ROPE + 64 * j + 64].rearrange("p (o f r) -> p o f r", o=1, f=2)
                            .to_broadcast([P, 10, 2, 32]) for j in range(2))
                for j, (a, b) in enumerate(((x1, cos), (x2, sin), (x2, cos), (x1, sin))):
                    orp.inc(TT(rope_t[j], a, b, ALU.mult), "m%d" % j)
                own(rp_v, "m3", l)
                orp.inc(TT(x1, rope_t[0], rope_t[1], ALU.subtract), "x1")
                orp.inc(TT(x2, rope_t[2], rope_t[3], ALU.add), "x2")
                with dve.Fori(0, 4) as i:
                    for s in range(2):
                        dve.wait_ge(at_p.sem, at_p.at("sc%d" % s, l, i))
                        dve.wait_ge(at_a.sem, at_a.at("P%d" % s, l, i - 1))
                        for g in range(G):
                            oat.inc(dve.tensor_reduce(am[s][0][:, g:g + 1], ps[:, 4 * s + 1, g * P:(1 + 2 * g) * P], AX_X, ALU.max),
                                    "mx%d" % s)
                    for s in range(2):
                        own(at_v, "mx%d" % s, l, i)
                        oat.inc(TS(am[s][1], am[s][0], sinkb[:, bass.ds(i + 4 * s, 1)], None, ALU.max), "mm%d" % s)
                    for s in range(2):
                        own(at_v, "mm%d" % s, l, i)
                        oat.inc(TS(am[s][2], am[s][1], -1.0, None, ALU.mult), "nm%d" % s)
                    for s in range(2):
                        own(at_v, "nm%d" % s, l, i)
                        dve.wait_ge(at_a.sem, at_a.at("se%d" % s, l, i - 1))
                        oat.inc(TS(am[s][4], am[s][2], sinkb[:, bass.ds(i + 4 * s, 1)], None, ALU.add), "sd%d" % s)
                    for s in range(2):
                        dve.wait_ge(at_a.sem, at_a.at("se%d" % s, l, i))
                        oat.inc(TT(am[s][5], am[s][5], am[s][3], ALU.add), "dn%d" % s)
                    for s in range(2):
                        own(at_v, "dn%d" % s, l, i)
                        oat.inc(dve.reciprocal(am[s][6], am[s][5]), "rc%d" % s)
                    for s in range(2):
                        own(at_v, "rc%d" % s, l, i)
                        dve.wait_ge(at_p.sem, at_p.at("pv%d" % s, l, i))
                        for g in range(G):
                            oat.inc(TS(tok[:, g, bass.ds(i * P + 4 * P * s, P)], ps[:, 4 * s + 3, g * P:(g + 1) * P],
                                       am[s][6][:, g:g + 1], None, ALU.mult), "o%d" % s)
                dve.wait_ge(nl_a.sem, nl_a.at("sig", l))
                for b, c0 in enumerate((T_GA, T_GB)):
                    for n in range(2):
                        wait_used(dve, u_out[l] + 4 * b + 2 * n + 1)
                        for g in range(G):
                            x = tok[:, g, c0 + 512 * n:c0 + 512 * n + 512]
                            oout.inc(TT(x, x, ps[:, 4 * b + 2 * n + g, :], ALU.mult), ("ga", "gb")[b])
                own(out_v, "gb", l)
                for g in range(G):
                    x = tok[:, g, T_GA:T_GA + D]
                    oout.inc(TT(x, x, tok[:, g, T_GB:T_GB + D], ALU.add), "m")
                wait_used(dve, u_out[l] + U_OUT - 1)
                for g in range(G):
                    oout.inc(CP(y_sb[:, g, :], ps[:, 4 + 2 * g:6 + 2 * g, :].rearrange("p b c -> p (b c)")), "y")
                resid(l, 0)
                own(res_v, "x", l, 0)
                norm_(l, 1)
                if l == 0:
                    def hidden(s, f, first=False):
                        dve.wait_ge(ff_a.sem, ff_a.at("si", 0, f))
                        for g in range(G):
                            off.inc(TT(f_hid[s][:, 256 * g:256 * g + 256], f_hs[0][:, 256 * g:256 * g + 256], ps[:, g, 256:512], ALU.mult), "mu")
                    dve.wait_ge(s_out, 32 * (l + 1))
                    hidden(0, 0)
                    with dve.Fori(0, (FF_STEPS - 1) // 2) as i:
                        for j in range(2):
                            hidden((1 + j) % 2, i * 2 + (1 + j))
                    wait_used(dve, u_ff + U_FF - 1)
                    for g in range(G):
                        ofe.inc(CP(y_sb[:, g, :], ps[:, 4 + 2 * g:6 + 2 * g, :].rearrange("p b c -> p (b c)")), "y")
                else:
                    lg, e1, c1, f1, l2, e2, mk, f2, c2, a1, a2, cmb = rt
                    m1, m2, dd, ex, x1_, rc, w2, _ = rcol
                    pos = cut(tokf, 8220, (24,))
                    dve.wait_ge(rt_p.sem, rt_p.at("lg"))

                    def r(ins, name):
                        ort.inc(ins, name)
                        if rt_v.at(name) == rt_v.per + ort.n or ort.n == 0:
                            own(rt_v, name)

                    def wide(x):
                        return x.to_broadcast([P, G, NEXP])
                    r(CP(lg, ps[:, 0, 0:16].rearrange("p (g e) -> p g e", g=G)), "lg")
                    r(dve.tensor_reduce(m1, lg, AX_X, ALU.max), "m1")
                    r(TT(e1, lg, wide(m1), ALU.is_equal), "e1")
                    for g in range(G):
                        r(dve.tensor_tensor_scan(c1[:, g], con[:, K_ONE:K_ONE + NEXP], e1[:, g], 0.0, ALU.mult, ALU.add), "c1")
                    r(STT(f1, c1, 1.0, e1, ALU.is_equal, ALU.mult), "f1")
                    r(STT(l2, f1, NEG, lg, ALU.mult, ALU.add), "l2")
                    r(dve.tensor_reduce(m2, l2, AX_X, ALU.max), "m2")
                    r(TT(e2, l2, wide(m2), ALU.is_equal), "e2")
                    for g in range(G):
                        r(dve.tensor_tensor_scan(c2[:, g], con[:, K_ONE:K_ONE + NEXP], e2[:, g], 0.0, ALU.mult, ALU.add), "c2")
                    r(STT(f2, c2, 1.0, e2, ALU.is_equal, ALU.mult), "f2")
                    r(TT(mk, f1, f2, ALU.add), "mk")
                    r(TT(dd, m2, m1, ALU.subtract), "d")
                    dve.wait_ge(rt_a.sem, rt_a.at("ex"))
                    r(TS(x1_, ex, 1.0, None, ALU.add), "x1")
                    r(dve.reciprocal(rc, x1_), "rc")
                    r(TT(w2, ex, rc, ALU.mult), "w2")
                    r(TT(a1, f1, wide(rc), ALU.mult), "a1")
                    r(TT(a2, f2, wide(w2), ALU.mult), "a2")
                    r(TT(cmb, a1, a2, ALU.add), "cmb")
                    dve.wait_ge(rt_p.sem, rt_p.at("pos"))
                    r(CP(pos, ps[:, 1, 0:24]), "pos")
                    r(dve.memset(f_acc, 0.0), "acc")

                    ov, cum, ovi, eq = (cut(tokf, 8244 + 8 * j, (NEXP,)) for j in range(4))
                    idf = cut(tokf, 8276, (EXTRA + 1,))
                    seen = cut(tokf, 8280, (1,))
                    r(TS(ov, pos[:, 16:24], P + 0.5, None, ALU.is_gt), "ov")
                    r(dve.tensor_tensor_scan(cum, con[:, K_ONE:K_ONE + NEXP], ov, 0.0, ALU.mult, ALU.add), "cum")
                    r(TT(ovi, ov, con[:, K_IOTA:K_IOTA + NEXP], ALU.mult), "ovi")
                    for j in range(EXTRA):
                        r(STT(eq, cum, float(j + 1), ovi, ALU.is_equal, ALU.mult), "eq%d" % j)
                        r(dve.tensor_reduce(idf[:, j:j + 1], eq, AX_X, ALU.add), "id%d" % j)
                    r(CP(idf[:, EXTRA:EXTRA + 1], cum[:, NEXP - 1:NEXP]), "n")
                    r(CP(over_tab[:, :], idf), "tab")

                    def expert(e, i, block_=0):
                        rr = i * (U_EXP // RING)
                        dve.wait_ge(moe_p.sem, moe_p.at("ga1", 0, i - 1))
                        for g in range(G):
                            omo.inc(TS(sel[:, g], con[:, K_IOTA + P * block_:K_IOTA + P * (block_ + 1)],
                                       pos[:, bass.ds(e + NEXP * g, 1)], mk.rearrange("p g e -> p (g e)")[:, bass.ds(e + NEXP * g, 1)],
                                       ALU.is_equal, ALU.mult), "sel")
                        own(moe_v, "sel", 0, i)
                        for g in range(G):
                            omo.inc(TS(selc[:, g], sel[:, g], cmb.rearrange("p g e -> p (g e)")[:, bass.ds(e + NEXP * g, 1)], None,
                                       ALU.mult), "selc")
                        dve.wait_ge(moe_p.sem, moe_p.at("sct", 0, i))
                        omo.inc(CP(selT.rearrange("p g t -> p (g t)"), ps[:, 2, 0:256]), "selT")
                        for f in range(FB):
                            dve.wait_ge(moe_a.sem, moe_a.at("si%d" % f, 0, i))
                            omo.inc(TT(f_hid[f % 2], f_hs[0], ps[:, 1, :], ALU.mult), "mu%d" % f)
                        wait_used(dve, u_moe + U_EXP - 1, rr)
                        omo.inc(CP(ye, ps[:, 4:6, :].rearrange("p b c -> p (b c)")), "ye")
                        for g in range(G):
                            dve.wait_ge(moe_p.sem, moe_p.at("sc%d" % g, 0, i))
                            omo.inc(TT(f_acc[:, g], f_acc[:, g], ps[:, (6, 2)[g]:(6, 2)[g] + 2, :].rearrange("p b c -> p (b c)"), ALU.add), "add")
                        own(moe_v, "add", 0, i)
                        omo.inc(dve.memset(seen, 1.0), "done")

                    with dve.Fori(0, NEXP) as e:
                        own(moe_v, "done", 0, e - 1)
                        expert(e, e)
                    own(moe_v, "done", 0, NEXP - 1)

                    def second(e, x):
                        expert(e, x + NEXP, 1)
                    second_blocks(dve, second)
                    for g in range(G):
                        ofe.inc(CP(y_sb[:, g, :], f_acc[:, g]), "y")
                resid(l, 1)


_W = ["w_ada", "b_ada", "norm_g", "w_in", "attn_sink", "conv_w", "dn_a_log", "dn_dt_bias", "dn_norm_g", "w_pa", "w_pb",
      "w_o", "w_ff_gate", "w_ff_up", "w_ff_down", "w_router", "w_e_gate", "w_e_up", "w_e_down", "x_prompt", "x_sample",
      "c", "c_ctx"]
_LAYER = {"cache_k%d": "cache_k_l%d", "cache_v%d": "cache_v_l%d", "state%d": "state_delta_l%d"}


def kernel(**inputs):
    import concourse.bacc as _bacc
    from concourse.bass_utils import run_bass_kernel_spmd as _run

    nc = _bacc.Bacc("TRN2", target_bir_lowering=False, num_devices=1)
    arrays, args = {}, {}

    def put(name, a):
        a = np.ascontiguousarray(a)
        arrays["in_" + name] = a
        args[name] = nc.dram_tensor("in_" + name, a.shape, mybir.dt.from_np(a.dtype), kind="ExternalInput").ap()

    for name in _W:
        put(name, inputs[name])
    for ours, theirs in _LAYER.items():
        for l in range(DEPTH):
            put(ours % l, inputs[theirs % l])
    put("consts", constants())
    outs = []

    def out(name, shape):
        args[name] = nc.dram_tensor("o_" + name, shape, F32, kind="ExternalOutput").ap()
        outs.append("o_" + name)

    out("y_out0", (1, P, D))
    out("y_out1", (1, P, D))
    for l in range(DEPTH):
        out("k_out%d" % l, (1, P, HKV, P))
        out("v_out%d" % l, (1, P, HKV, P))
        out("s_out%d" % l, (1, 2, DH, P, P))
    program(nc, args)
    r = _run(nc, [arrays], core_ids=[0])
    return tuple(r.results[0][n] for n in outs)
```

```python
from contextlib import ExitStack

import numpy as np

import concourse.bass as bass
from concourse import mybir

F32 = mybir.dt.float32
F32R = mybir.dt.float32r
I32 = mybir.dt.int32
ACT = mybir.ActivationFunctionType
ALU = mybir.AluOpType
AX_X = mybir.AxisListType.X

P = 128
G = 2
D = 1024
KC = D // P
DEPTH = 2
HQ, HKV = 8, 2
DH = 8
TAPS = 5
PAD = TAPS // 2
TP = P + 2 * PAD
QKV_CH = 3 * DH
DFF = 2816
NEXP = 8
DEXP = 3584
EPS = 1e-6
IN_W = 7712
C_QKVB, C_Z, C_BA, C_GATES = 1536, 4608, 5632, 5664
COLS = 4608
T_K, T_V, T_Z, T_GA, T_GB = 1024, 1280, 1536, 2560, 3584
UNIT = 2048
RING = 4
WRING = 3
LOOP = 12
LEVELS = 7
FF_STEPS = DFF // 256
FB = DEXP // 512
EXTRA = 3
NEG = -3.0e38
SCALE = float(P) ** -0.5

K_ID = 0
K_TRI = K_ID + P
K_STR = K_TRI + 2 * P
K_ONE = K_STR + 2 * P
K_ROPE = K_ONE + P
K_IOTA = K_ROPE + 128
K_SEL = K_IOTA + 256
K_ALL = K_SEL + 2 * P
PAIRS = [0, 4, 1, 5, 2, 6, 3, 7, 8, 9, 10, 11]


def constants():
    c = np.zeros((P, K_ALL), np.float32)
    r, k = np.arange(P)[:, None], np.arange(P)[None, :]
    c[:, K_ID:K_ID + P] = r == k
    c[:, K_TRI:K_TRI + P] = r <= k
    c[:, K_TRI + P:K_TRI + 2 * P] = r >= k
    c[:, K_STR:K_STR + P] = r < k
    c[:, K_STR + P:K_STR + 2 * P] = r > k
    c[:, K_ONE:K_ONE + P] = 1.0
    lev = np.zeros((P, LEVELS * 2 * P), np.float32)
    for n in range(LEVELS):
        s = 1 << n
        same = (r // (2 * s)) == (k // (2 * s))
        low = same & (r % (2 * s) >= s) & (k % (2 * s) < s)
        m = (r == k).astype(np.float32)
        lev[:, 2 * n * P:(2 * n + 1) * P] = m - low
        lev[:, (2 * n + 1) * P:(2 * n + 2) * P] = m - low.T
    inv = 10000.0 ** (-np.arange(32, dtype=np.float32) / 32)
    ang = np.stack([(np.arange(P) // 64)[:, None] * inv, (np.arange(P) % 64)[:, None] * inv], 1)
    ang = ang.astype(np.float32).reshape(P, 64)
    c[:, K_ROPE:K_ROPE + 64] = np.cos(ang)
    c[:, K_ROPE + 64:K_ROPE + 128] = np.sin(ang)
    c[:, K_IOTA:K_IOTA + 256] = np.arange(256)[None, :]
    for g in range(G):
        c[:, K_SEL + g * P:K_SEL + (g + 1) * P] = (np.arange(P) % 32 == g)[:, None]
    return c, lev


class Steps:

    def __init__(self, sem, iters, names):
        self.sem, self.iters, self.off = sem, iters, {}
        n = 0
        for x in names:
            name, k = x if isinstance(x, tuple) else (x, 1)
            assert name not in self.off
            n += k
            self.off[name] = n
        self.per = n

    def at(self, name, l=0, i=0):
        return i * self.per + ((l * self.iters + 1) * self.per + self.off[name])


class Order:

    def __init__(self, steps):
        self.s, self.n = steps, 0

    def inc(self, ins, name):
        self.n += 1
        lo = 0
        for k, v in self.s.off.items():
            if lo < self.n <= v:
                assert k == name, (k, name)
            lo = v
        ins.then_inc(self.s.sem, 1)
        if self.n == self.s.per:
            self.n = 0


def program(nc, A):
    ctx = ExitStack()
    with ctx:
        def sb(name, shape, dt=F32):
            return ctx.enter_context(nc.sbuf_tensor(name, shape, dt))

        def sem(name):
            return ctx.enter_context(nc.semaphore(name))

        def steps(name, iters, names):
            return Steps(sem(name), iters, names)

        ring = sb("ring", [P, RING, UNIT])
        con = sb("con", [P, K_ALL])
        xt = sb("xt", [P, G, D])
        hreg = sb("hreg", [P, G * D])
        tok = sb("tok", [P, G, COLS])
        mod = sb("mod", [P, 2, D])
        cache_k = sb("cache_k", [P, HKV, P])
        cache_v = sb("cache_v", [P, HKV, P])
        small = sb("small", [P, 1024])
        wba = sb("wba", [P, KC, 32])
        ps = ctx.enter_context(nc.psum_tensor("ps", [P, 8, 512], F32))
        with nc.sbuf_tensor("bT", [P, 2, KC, G * P], F32R) as bT:
            pass
        qreg = sb("qreg", [P, QKV_CH * G * TP])
        turn_ = ExitStack()
        wsp = turn_.enter_context(nc.sbuf_tensor("wsp", [P, WRING, 2, UNIT], F32R))
        hT = turn_.enter_context(nc.sbuf_tensor("hT", [P, 2, KC, G * P], F32R))
        fT = turn_.enter_context(nc.sbuf_tensor("fT", [P, 2, 2, 4, P], F32R))
        turn_.close()
        dnx = sb("dnx", [P, WRING * 2 * UNIT + 2 * 2048 + 2048])

        def cut(t, at, shape):
            n = 1
            for k in shape:
                n *= k
            flat = t[:, at:at + n]
            names = "abcd"[:len(shape)]
            if len(shape) == 1:
                return flat
            return flat.rearrange("p (%s) -> p %s" % (" ".join(names), " ".join(names)),
                                  **{names[j]: shape[j] for j in range(len(shape))})

        ident = con[:, K_ID:K_ID + P]
        ones = con[:, K_ONE:K_ONE + P]

        def tri(d):
            return con[:, K_TRI + d * P:K_TRI + (d + 1) * P]

        def two(t):
            return t.rearrange("p (d o k) -> p d o k", d=2, o=1).to_broadcast([P, 2, G, P])

        h_tok = cut(hreg, 0, (G, D))
        qkv = cut(qreg, 0, (QKV_CH, G, TP))

        at = [0]

        def slot(shape):
            n = int(np.prod(shape))
            r = [cut(dnx, at[0] + n * s, shape) for s in range(2)]
            at[0] += 2 * n
            return r

        kqv = slot((3, G, P))
        XX = slot((2, 2, G, P))
        ktv = slot((3, P))
        ET = slot((2, G, P))
        attn = slot((2, G, P))
        AT = slot((2, G, P))
        MM = slot((2, G, P))
        RP = slot((2, P))
        VN = slot((2, G, P))
        VD = slot((2, P))
        osb = slot((G, P))
        sfo = slot((2, P))
        junk = slot((G, P))
        s0 = cut(dnx, at[0], (DH, 2, P))
        lev = cut(dnx, at[0] + 2048, (LEVELS, 2 * P))
        assert at[0] + 2048 + LEVELS * 2 * P <= dnx.shape[1]
        acc = [cut(hreg, 256 * s, (G, P)) for s in range(2)]
        l2s = [cut(hreg, 512 + 512 * s, (2, G, P)) for s in range(2)]
        l2c = cut(hreg, 1536, (8,))
        at[0] = 0
        qst = slot((G, P))
        qT = slot((G, P))
        pr = slot((3, P))
        prT = slot((3, P))
        kTb = cut(dnx, at[0], (HKV, 3, P))
        at[0] += 768
        rope_t = [cut(dnx, at[0] + 640 * j, (10, 2, 32)) for j in range(4)]
        y_sb = cut(qreg, 4096, (G, D))
        ngr = cut(qreg, 0, (2, D))
        sqj = cut(hreg, 0, (D,))
        tokf = tok[:, :, :].rearrange("p g c -> p (g c)")
        f_hs = [cut(tokf, 512 * s, (512,)) for s in range(2)]
        f_hid = [cut(tokf, 1024 + 512 * s, (512,)) for s in range(2)]
        sel = cut(tokf, 4096, (G, P))
        selc = cut(tokf, 4352, (G, P))
        selT = cut(tokf, 4608, (G, P))
        ye = cut(tokf, 4864, (D,))
        f_acc = cut(tokf, 5888, (G, D))
        sm = [0]

        def col(n):
            sm[0] += n
            assert sm[0] <= 1024
            return small[:, sm[0] - n:sm[0]]

        condT = col(2 * KC).rearrange("p (k c) -> p k c", c=2)
        ss, ms, rstd = col(2), col(2), col(2)
        mhalf = col(16)
        ba = col(64).rearrange("p (g c) -> p g c", g=G)
        eb = col(32).rearrange("p (g c) -> p g c", g=G)
        ga = [col(32).rearrange("p (g c) -> p g c", g=G) for _ in range(5)]
        dtb, alog, ealog = col(16), col(16), col(16)
        gcs, gex = col(64), col(64)
        GT = col(192).rearrange("p (h q d g) -> p h q d g", h=DH, q=6, d=2)
        cw = col(128)
        hc = [col(24).rearrange("p (q d g) -> p q d g", q=6, d=2) for _ in range(2)]
        oss = [col(2) for _ in range(2)]
        ors = [col(2) for _ in range(2)]
        sinkb = col(8)
        am = [[col(2) for _ in range(7)] for _ in range(2)]
        cwr = sb("cwr", [P, P])
        dng = sb("dng", [P, P])
        cond = hreg[0:2, 0:D]
        condS = hreg[0:2, D:2 * D]
        condR = [hT[:, x].rearrange("p a b -> p (a b)")[:, 0:KC * P].rearrange("p (k m) -> p k m", k=KC) for x in range(2)]
        hTe = [hT[:, x].rearrange("p a b -> p (a b)")[:, 0:KC * P].rearrange("p (k m) -> p k m", k=KC) for x in range(2)]
        wr = sb("wr", [P, KC, NEXP])
        over_tab = sb("over_tab", [P, EXTRA + 1], I32)
        rt = [cut(tokf, 8000 + 16 * j, (G, NEXP)) for j in range(12)]
        rcol = [cut(tokf, 8192 + 2 * j, (G, 1)) for j in range(8)]

        ready = [sem("unit_ready%d" % j) for j in range(RING)]
        unit_used = sem("unit_used")
        unit_hi = sem("unit_high")
        unit_lo = sem("unit_low")
        s_in = sem("inputs_in")
        s_out = sem("outputs_out")
        s_state = [sem("state_out%d" % s) for s in range(2)]
        s_lay = sem("layer_small_in")
        LAY_DMAS = 18
        s_lev = sem("levels_in")
        s_st = sem("states_in")
        init_a = steps("init_act", 1, ["cond"])
        init_p = steps("init_pe", 1, ["condT"])
        init_v = steps("init_dve", 1, ["half", "condT"])
        lay_g = steps("layer_pool", 1, [("pads", 2)])
        cnd_a = steps("cond_act", 1, ["hi"])
        cnd_v = steps("cond_dve", 1, ["lo"])
        ada_v = steps("ada_dve", 1, [("row", 12), ("mod", 4)])
        rms_a = steps("rms_act", 4, [("ss", 2)])
        rms_v = steps("rms_dve", 4, ["ms"])
        rms_g = steps("rms_pool", 4, ["rstd"])
        nrm_p = steps("norm_pe", 2, ["bc0", "bc1", "t00", "t01", "t10", "t11"])
        nrm_v = steps("norm_dve", 2, ["a0", "h0", "a1", "h1", "l00", "l01", "l10", "l11"])
        nrm_a = steps("norm_act", 2, ["e00", "e01", "e10", "e11"])
        evac = steps("proj_evac", 1, ["b%d" % j for j in range(12)] + ["t%d" % j for j in range(9)])
        gat_p = steps("gates_pe", 1, ["ba", "cw", "gc"])
        gat_v = steps("gates_dve", 1, ["cw", "ba", "a", "na", "e1", "sp", "g0", "gcol", "gcs", "kd",
                                       "gc", "egc", "negc", "ekd", "b1", "rb", "beta"])
        gat_a = steps("gates_act", 1, ["eb", "ea", "el", "ln", ("ex", 2)])
        cnv_v = steps("conv_dve", QKV_CH // 2, ["t%d%d" % (j, s) for j in range(TAPS) for s in range(2)])
        cnv_a = steps("conv_act", QKV_CH // 2, ["s0", "s1"])
        nl_a = steps("gate_act", 1, ["sig"])
        nl_v = steps("gate_dve", 1, ["z"])
        l2_g = steps("l2_pool", 4, ["sq0", "sq1", "pw"])
        l2_p = steps("l2_pe", 4, ["ss", "bc0", "bc1"])
        l2_v = steps("l2_dve", 4, ["ep", "nm0", "nm1"])

        def both(names):
            return [(x[0] % s, x[1]) if isinstance(x, tuple) else x % s for x in names for s in range(2)]

        lv = range(1, LEVELS)
        dn_g = steps("dn_pool", 4, both(["kqv%d", "hc%d", "EM%d", ("XT%d", 2), "rs%d"]))
        dn_p = steps("dn_pe", 4, both(["tr%d", "G%d", "gr%d", "m%d"])
                     + [x for v in lv for x in both(["a%d_%%d" % v, "b%d_%%d" % v])]
                     + both(["kS%d", "V%d", "O%d", "SF%d"]))
        dn_v = steps("dn_dve", 4, both([("t%d", 4), "at%d", "W%d", ("A%d", 4), "AI%d", "X%d"])
                     + [x for v in lv for x in both(["M%d_%%d" % v])]
                     + both([("R%d", 2), ("VD%d", 2), "oc%d", "oa%d", "ob%d", "ms%d", ("y%d", 2)]))
        dn_a = steps("dn_act", 4, both(["tok%d", "ET%d"]) + [x for v in lv for x in both(["E%d_%%d" % v])]
                     + both([("VN%d", 4), "Sf%d", ("sq%d", 2)]))
        rp_v = steps("rope_dve", 1, ["m0", "m1", "m2", "m3", "x1", "x2"])
        kt_p = steps("keys_pe", 1, ["k"])
        kt_a = steps("keys_act", 1, ["k", "o"])
        at_g = steps("attn_pool", 4, both(["q%d"]))
        at_p = steps("attn_pe", 4, both(["qt%d", "sc%d", "pt%d", "pv%d"]))
        at_v = steps("attn_dve", 4, both([("mx%d", 2), "mm%d", "nm%d", "sd%d", "dn%d", "rc%d", ("o%d", 2)]))
        at_a = steps("attn_act", 4, both(["qe%d", ("P%d", 2), "se%d", "pe%d"]))
        out_p = steps("out_pe", 1, ["tr%d" % j for j in range(8)] + ["mt%d" % j for j in range(4)])
        out_a = steps("out_act", 1, ["ev%d" % j for j in range(8)] + ["me%d" % j for j in range(4)])
        out_v = steps("out_dve", 1, ["lv%d" % j for j in range(8)] + [("ga", 4), ("gb", 4), ("m", 2)] + ["ml%d" % j for j in range(4)] + [("y", 2)])
        res_p = steps("resid_pe", 2, ["gb"])
        res_v = steps("resid_dve", 2, [("t", 2), ("x", 2)])
        ff_a = steps("ff_act", FF_STEPS, [("si", 2)])
        ff_h = steps("ff_hidden", FF_STEPS, ["he"])
        ff_v = steps("ff_dve", FF_STEPS, [("mu", 2)])
        ff_l = steps("ff_low", FF_STEPS, ["hl"])
        ff_p = steps("ff_pe", FF_STEPS, ["ht"])
        ffe_v = steps("ff_end", 1, [("y", 2)])
        rt_p = steps("router_pe", 1, ["lg", "pos"])
        rt_v = steps("router_dve", 1, ["lg", "m1", "e1", ("c1", 2), "f1", "l2", "m2", "e2", ("c2", 2), "f2",
                                       "mk", "d", "x1", "rc", "w2", "a1", "a2", "cmb", "pos", "acc",
                                       "ov", "cum", "ovi"] + [x % j for j in range(EXTRA) for x in ("eq%d", "id%d")]
                     + ["n", "tab"])
        rt_a = steps("router_act", 1, ["ex"])
        moe_v = steps("moe_dve", NEXP + EXTRA, [("sel", 2), ("selc", 2), "selT", "gl0", "gl1"]
                      + ["mu0"] + [x for f in range(1, FB) for x in ("hl%d" % (f - 1), "mu%d" % f)] + ["hl%d" % (FB - 1)]
                      + ["ye", ("add", 2), "done"])
        moe_a = steps("moe_act", NEXP + EXTRA, ["ge0", "ge1", "si0"]
                      + [x for f in range(1, FB) for x in ("he%d" % (f - 1), "si%d" % f)] + ["he%d" % (FB - 1)])
        moe_p = steps("moe_pe", NEXP + EXTRA, ["sct", "ga0", "ga1"] + ["ht%d" % f for f in range(FB)] + ["sc0", "sc1"])

        V_STEPS = [init_v, cnd_v, ada_v, rms_v, nrm_v, gat_v, cnv_v, nl_v, l2_v, dn_v, rp_v, at_v, out_v, res_v,
                   ff_v, ff_l, ffe_v, rt_v, moe_v]
        A_STEPS = [init_a, cnd_a, rms_a, nrm_a, evac, gat_a, cnv_a, nl_a, dn_a, kt_a, at_a, out_a, ff_a, ff_h, rt_a, moe_a]
        P_STEPS = [init_p, nrm_p, gat_p, l2_p, dn_p, kt_p, at_p, out_p, res_p, ff_p, rt_p, moe_p]
        G_STEPS = [lay_g, rms_g, l2_g, dn_g, at_g]

        U_ADA, U_PROJ, U_OUT, U_FF, U_EXP = 24, 30, 12, 3 * FF_STEPS, 6 * FB
        u_ada = [0, U_ADA + U_PROJ + U_OUT + U_FF]
        u_proj = [u + U_ADA for u in u_ada]
        u_out = [u + U_PROJ for u in u_proj]
        u_ff = u_out[0] + U_OUT
        u_moe = u_out[1] + U_OUT

        def unit(u):
            return ring[:, u % RING, :]

        def part(u, x):
            return wsp[:, u % WRING, x, :]

        def wait_used(eng, u, i=0):
            eng.wait_ge(unit_used, i * LOOP + (u + 1 + WRING))

        def high(act, u, i=0):
            act.wait_ge(ready[u % RING], i * (16 * LOOP // RING) + (16 * (u // RING) + 16))
            wait_used(act, u - WRING, i)
            act.activation(part(u, 0), unit(u), ACT.Copy).then_inc(unit_hi, 1)

        def low(dve, u, i=0):
            dve.wait_ge(unit_hi, i * LOOP + (u + 1))
            dve.tensor_tensor(part(u, 1), unit(u), part(u, 0).bitcast(F32), ALU.subtract).then_inc(unit_lo, 1)

        def wait_hi(pe, u, i=0):
            pe.wait_ge(unit_hi, i * LOOP + (u + 1))

        def wait_lo(eng, u, i=0):
            eng.wait_ge(unit_lo, i * LOOP + (u + 1 + RING))

        def mod_row(q, c, n):
            return mod[32 * q:32 * q + 2, c, 512 * n:512 * n + 512]

        def gu_last(f):
            return 6 * f + 1 if f else 3

        def second_blocks(eng, body):
            eng.wait_ge(rt_v.sem, rt_v.at("tab"))
            n = eng.value_load(over_tab[0:1, EXTRA:EXTRA + 1], min_val=0, max_val=EXTRA)
            for x in range(EXTRA):
                with eng.If(n > x):
                    e = eng.value_load(over_tab[0:1, x:x + 1], min_val=0, max_val=NEXP - 1)
                    body(e, x)

        MODS = [(0, 0), (1, 0), (2, 0), (3, 0), (0, 1), (1, 1)]
        GAIN = {1: 0, 2: 1, 4: 2, 5: 3}

        x_in = [A["x_prompt"], A["x_sample"]]
        block = ctx.enter_context(nc.Block())

        @block.sync
        def _(sp):
            def load(u, src, dst=None, i=0):
                wait_lo(sp, u - RING, i)
                d = unit(u) if dst is None else dst
                sp.dma_start(d, src).then_inc(ready[u % RING], 16)

            def rows(u, w, k0, c0, i=0, kn=4, cn=512):
                src = w[k0:k0 + kn, :, bass.ds(c0, cn)].rearrange("k p n -> p k n")
                load(u, src, unit(u)[:, 0:kn * cn].rearrange("p (k n) -> p k n", k=kn), i)

            sp.sem_inc(unit_used, WRING)
            sp.sem_inc(unit_lo, RING)
            for l in range(DEPTH):
                w = A["w_ada"][l].rearrange("(k p) n -> k p n", p=P)
                with sp.Fori(0, U_ADA // LOOP) as i:
                    for j in range(LOOP // 2):
                        for h in range(2):
                            rows(u_ada[l] + 2 * j + h, w, 4 * h, i * (LOOP * 256) + 512 * j, i)
                w = A["w_in"][l].rearrange("(k p) n -> k p n", p=P)
                for j, pr_ in enumerate(PAIRS):
                    rows(u_proj[l] + j, w, 0, C_QKVB + 256 * pr_, 0, 8, 256)
                cols = [512 * j for j in range(3)] + [C_Z, C_Z + 512] + [C_GATES + 512 * j for j in range(4)]
                for j, c in enumerate(cols):
                    for h in range(2):
                        rows(u_proj[l] + 12 + 2 * j + h, w, 4 * h, c)
                u = u_out[l]
                for name in ("w_pa", "w_pb", "w_o"):
                    w = A[name][l].rearrange("(k p) n -> k p n", p=P)
                    for n in range(2):
                        for h in range(2):
                            rows(u, w, 4 * h, 512 * n)
                            u += 1
                if l == 0:
                    wg, wu = (A[n][0].rearrange("(k p) n -> k p n", p=P) for n in ("w_ff_gate", "w_ff_up"))
                    wd = A["w_ff_down"][0].rearrange("(f k p) n -> f p k n", p=P, k=2)

                    def ff_gu(u, f, i=0):
                        rows(u, wg, 0, f * 256, i, 8, 256)
                        rows(u + 1, wu, 0, f * 256, i, 8, 256)

                    def ff_d(u, f, i=0):
                        load(u, wd[bass.ds(f, 1)].rearrange("f p k n -> p (f k) n"),
                             unit(u).rearrange("p (k n) -> p k n", k=2), i)

                    ff_gu(u_ff, 0)
                    ff_gu(u_ff + 2, 1)
                    ff_d(u_ff + 4, 0)
                    with sp.Fori(0, (FF_STEPS - 3) // 4) as i:
                        for j in range(4):
                            ff_gu(u_ff + 5 + 3 * j, i * 4 + (2 + j), i)
                            ff_d(u_ff + 7 + 3 * j, i * 4 + (1 + j), i)
                    u = u_ff + 3 * FF_STEPS - 4
                    ff_gu(u, FF_STEPS - 1)
                    ff_d(u + 2, FF_STEPS - 2)
                    ff_d(u + 3, FF_STEPS - 1)
                else:
                    def expert(e, u, i=0):
                        we = [A[n][0, bass.ds(e, 1)].rearrange("e (k p) n -> (e k) p n", p=P)
                              for n in ("w_e_gate", "w_e_up")]
                        wd = A["w_e_down"][0, bass.ds(e, 1)].rearrange("e (f k p) n -> (e f) p k n", p=P, k=2)
                        for f in range(FB + 1):
                            if f < FB:
                                for w in we:
                                    for h in range(2):
                                        rows(u, w, 4 * h, 512 * f, i)
                                        u += 1
                            if f > 0:
                                for h in range(2):
                                    load(u, wd[2 * (f - 1) + h], unit(u).rearrange("p (k n) -> p k n", k=2), i)
                                    u += 1

                    with sp.Fori(0, NEXP // 2) as i:
                        for j in range(2):
                            expert(i * 2 + j, u_moe + j * U_EXP, i * (2 * U_EXP // LOOP))
                    second_blocks(sp, lambda e, x: expert(e, u_moe + (NEXP + x) * U_EXP))

        @block.gpsimd
        def _(pool):
            for s in G_STEPS:
                pool.sem_inc(s.sem, s.per)
            D0 = pool.dma_start
            D0(con[:, :], A["consts"]).then_inc(s_in, 16)
            D0(cond[0:1, :], A["c_ctx"].rearrange("(a n) -> a n", a=1)).then_inc(s_in, 16)
            D0(cond[1:2, :], A["c"]).then_inc(s_in, 16)
            for g in range(G):
                D0(xt[:, g, :], x_in[g][0]).then_inc(s_in, 16)

            D0(wr[:, :, :], A["w_router"][0].rearrange("(k p) e -> p k e", p=P)).then_inc(s_in, 16)

            def bc(row, n):
                return row.rearrange("(a n) -> a n", a=1).to_broadcast([n, row.shape[0]])

            def rstd_(l, k):
                pool.wait_ge(rms_v.sem, rms_v.at("ms", l, k))
                pool.wait_ge(init_v.sem, init_v.at("half"))
                rg.inc(pool.tensor_tensor(rstd[:, :], ms[:, :], mhalf[:, 0:2], ALU.pow), "rstd")

            lg, rg, l2g, dg, ag = (Order(s) for s in G_STEPS)
            for l in range(DEPTH):
                if l:
                    pool.wait_ge(res_v.sem, res_v.at("x", 0, 1))
                for m, (q, c) in enumerate(MODS):
                    pool.dma_start(mod[32 * q:32 * q + 2, c, :], bc(A["b_ada"][l, m * D:(m + 1) * D], 2)).then_inc(s_lay, 16)
                for m, r in GAIN.items():
                    q, c = MODS[m]
                    pool.dma_start(ngr[32 * q:32 * q + 2, c, :], bc(A["norm_g"][l, r], 2)).then_inc(s_lay, 16)
                pool.dma_start(wba[:, :, :], A["w_in"][l, :, C_BA:C_BA + 32].rearrange("(k p) n -> p k n", p=P)).then_inc(s_lay, 16)
                pool.dma_start(cwr[0:TAPS * QKV_CH, :], A["conv_w"][l].rearrange("j (c p) -> (j c) p", p=P)).then_inc(s_lay, 16)
                pool.dma_start(dtb, bc(A["dn_dt_bias"][l].rearrange("d h -> (d h)"), P)).then_inc(s_lay, 16)
                pool.dma_start(alog, bc(A["dn_a_log"][l].rearrange("d h -> (d h)"), P)).then_inc(s_lay, 16)
                pool.dma_start(dng[:, :], bc(A["dn_norm_g"][l], P)).then_inc(s_lay, 16)
                pool.dma_start(sinkb, bc(A["attn_sink"][l], P)).then_inc(s_lay, 16)
                pool.dma_start(cache_k[:, :, :], A["cache_k%d" % l][0]).then_inc(s_lay, 16)
                pool.dma_start(cache_v[:, :, :], A["cache_v%d" % l][0]).then_inc(s_lay, 16)
                rstd_(l, 0)
                pool.wait_ge(ada_v.sem, ada_v.at("mod", l))
                lg.inc(pool.memset(qkv[:, :, :, 0:PAD], 0.0), "pads")
                lg.inc(pool.memset(qkv[:, :, :, PAD + P:TP], 0.0), "pads")
                for i in range(4):
                    pool.wait_ge(cnv_a.sem, cnv_a.at("s1", l, 2 * i + 1))
                    pool.wait_ge(l2_p.sem, l2_p.at("ss", l, i - 1))
                    for s in range(2):
                        x = qkv[:, 2 * i + 8 * s:2 * i + 8 * s + 2, :, PAD:PAD + P]
                        l2g.inc(pool.tensor_tensor(l2s[s], x, x, ALU.mult), "sq%d" % s)
                    pool.wait_ge(l2_v.sem, l2_v.at("ep", l, i))
                    l2g.inc(pool.tensor_tensor(l2c, l2c, mhalf[:, 0:8], ALU.pow), "pw")
                wait_used(pool, u_proj[l] + U_PROJ - 1)
                pool.dma_start(lev.rearrange("p a b -> p (a b)"), A["levels"]).then_inc(s_lev, 16)
                for d in range(2):
                    pool.dma_start(s0[:, :, d, :], A["state%d" % l][0, d].rearrange("h k v -> k h v")).then_inc(s_st, 16)
                with pool.Fori(0, 4) as i:
                    for s in range(2):
                        if s == 0:
                            pool.wait_ge(l2_v.sem, l2_v.at("nm1", l, 3))
                        pool.wait_ge(dn_p.sem, dn_p.at("kS%d" % s, l, i - 1))
                        src = qkv[:, bass.ds(i * 2 + s, 17), :, PAD:PAD + P][:, 0:17:8]
                        dg.inc(pool.tensor_copy(kqv[s], src), "kqv%d" % s)
                    for s in range(2):
                        if s == 0:
                            pool.wait_ge(gat_v.sem, gat_v.at("beta", l))
                        pool.wait_ge(dn_v.sem, dn_v.at("ob%d" % s, l, i - 1))
                        pool.wait_ge(dn_a.sem, dn_a.at("VN%d" % s, l, i - 1))
                        dg.inc(pool.tensor_copy(hc[s].rearrange("p q d g -> p (q d g)"),
                                                GT[:, bass.ds(i * 2 + s, 1)].rearrange("p h q d g -> p (h q d g)")),
                               "hc%d" % s)
                    for s in range(2):
                        pool.wait_ge(dn_a.sem, dn_a.at("ET%d" % s, l, i))
                        dg.inc(pool.tensor_tensor(ET[s], ET[s], two(con[:, K_TRI:K_TRI + 2 * P]), ALU.mult), "EM%d" % s)
                    for s in range(2):
                        pool.wait_ge(dn_v.sem, dn_v.at("AI%d" % s, l, i))
                        pool.wait_ge(s_lev, 16 * (l + 1))
                        pool.wait_ge(dn_p.sem, dn_p.at("V%d" % s, l, i - 1))
                        for d in range(2):
                            dg.inc(pool.tensor_tensor(XX[s][:, 1, d], AT[s][:, d],
                                                     lev[:, 0, (1 - d) * P:(2 - d) * P]
                                                     .rearrange("p (o k) -> p o k", o=1).to_broadcast([P, G, P]), ALU.mult), "XT%d" % s)
                    for s in range(2):
                        pool.wait_ge(dn_v.sem, dn_v.at("ms%d" % s, l, i))
                        dg.inc(pool.tensor_tensor(ors[s], oss[s], mhalf[:, 0:2], ALU.pow), "rs%d" % s)
                        pool.wait_ge(dn_a.sem, dn_a.at("Sf%d" % s, l, i))
                        pool.dma_start(A["s_out%d" % l][0, :, bass.ds(i * 2 + s, 1)].rearrange("d h k v -> k (d h) v"),
                                       sfo[s]).then_inc(s_state[s], 16)
                with pool.Fori(0, 4) as i:
                    for s in range(2):
                        if s == 0:
                            pool.wait_ge(rp_v.sem, rp_v.at("x2", l))
                            pool.wait_ge(dn_v.sem, dn_v.at("y1", l, 3))
                        pool.wait_ge(at_p.sem, at_p.at("qt%d" % s, l, i - 1))
                        ag.inc(pool.tensor_copy(qst[s], tok[:, :, bass.ds(i * P + 4 * P * s, P)]), "q%d" % s)
                pool.wait_ge(evac.sem, evac.at("t2", l))
                for n, c in (("k", T_K), ("v", T_V)):
                    pool.dma_start(A["%s_out%d" % (n, l)][0], tok[:, 0, c:c + 256].rearrange("p (h d) -> p h d", h=HKV))\
                        .then_inc(s_out, 16)
                rstd_(l, 1)
                rstd_(l, 2)
                rstd_(l, 3)
            for s in range(2):
                pool.wait_ge(s_state[s], 16 * 4 * DEPTH)
            pool.wait_ge(res_v.sem, res_v.at("x", 1, 1))
            for g in range(G):
                pool.dma_start(A["y_out%d" % g][0], xt[:, g, :]).then_inc(s_out, 16)
            pool.wait_ge(s_out, 32 * DEPTH + 32)

        @block.scalar
        def _(act):
            for s in A_STEPS:
                act.sem_inc(s.sem, s.per)
            (oi, ocd, orr, onr, oev, oga, ocv, onl, odn, okt, oat, oout, off, ofh, ort, omo) = (Order(s) for s in A_STEPS)
            AC = act.activation
            act.wait_ge(s_in, 16 * 6)
            oi.inc(AC(condS, cond, ACT.Silu), "cond")

            def ss_(l, k, src, ready_):
                for g in range(G):
                    ready_(g)
                    if g or l or k:
                        act.wait_ge(rms_a.sem, rms_a.at("ss", l, k) - 2 + g)
                    orr.inc(AC(sqj, src(g), ACT.Square, accum_out=ss[:, g:g + 1]), "ss")

            def norm_(l, n):
                for g in range(G):
                    for h in range(2):
                        act.wait_ge(nrm_p.sem, nrm_p.at("t%d%d" % (g, h), l, n))
                        onr.inc(AC(hT[:, 0, 4 * h:4 * h + 4, g * P:(g + 1) * P],
                                   ps[:, 4 * g + h, :].rearrange("p (k t) -> p k t", k=4), ACT.Copy), "e%d%d" % (g, h))

            for l in range(DEPTH):
                act.wait_ge(init_v.sem, init_v.at("condT"))
                if l:
                    act.wait_ge(res_v.sem, res_v.at("x", l - 1, 1))
                cT = condT.rearrange("p k (o c) -> p k o c", o=1).to_broadcast([P, KC, P // 2, 2])
                ocd.inc(AC(condR[0].rearrange("p k (o c) -> p k o c", c=2), cT, ACT.Copy), "hi")
                with act.Fori(0, U_ADA // LOOP) as i:
                    for j in range(LOOP):
                        high(act, u_ada[l] + j, i)
                def x_there(g):
                    if l:
                        act.wait_ge(res_v.sem, res_v.at("x", 0, 1) - 1 + g)
                ss_(l, 0, lambda g: xt[:, g, :], x_there)
                norm_(l, 0)
                up = u_proj[l]

                def silu(p):
                    for s in range(2):
                        act.wait_ge(cnv_v.sem, cnv_v.at("t%d%d" % (TAPS - 1, s), l, p))
                        ocv.inc(AC(qkv[:, 2 * PAIRS[p] + s, :, PAD:PAD + P], acc[s], ACT.Silu), "s%d" % s)

                act.wait_ge(s_lay, 16 * LAY_DMAS * (l + 1))
                act.wait_ge(lay_g.sem, lay_g.at("pads", l))
                for n in range(U_PROJ + 2):
                    if n < U_PROJ:
                        high(act, up + n)
                    if n == 2:
                        act.wait_ge(gat_v.sem, gat_v.at("ba", l))
                        oga.inc(AC(eb, ba[:, :, 0:16], ACT.Exp, scale=-1.0), "eb")
                        oga.inc(AC(ealog, alog, ACT.Exp), "ea")
                        act.wait_ge(gat_v.sem, gat_v.at("na", l))
                        oga.inc(AC(ga[2], ga[1], ACT.Exp), "el")
                        act.wait_ge(gat_v.sem, gat_v.at("e1", l))
                        oga.inc(AC(ga[3], ga[2], ACT.Ln), "ln")
                    if n == 6:
                        act.wait_ge(gat_v.sem, gat_v.at("kd", l))
                        oga.inc(AC(gex[:, 0:32], gcs[:, 0:32], ACT.Exp), "ex")
                        oga.inc(AC(gex[:, 32:64], gcs[:, 32:64], ACT.Exp), "ex")
                    m = n - 2
                    if 0 <= m < 12:
                        wait_used(act, up + m)
                        oev.inc(AC(qkv[:, 2 * PAIRS[m]:2 * PAIRS[m] + 2, :, PAD:PAD + P],
                                   ps[:, 2 + m % 6, :].rearrange("p (c g t) -> p c g t", c=2, g=G), ACT.Copy), "b%d" % m)
                    elif m >= 12 and m % 2:
                        j = (m - 12) // 2
                        wait_used(act, up + m)
                        oev.inc(AC(tok[:, :, 512 * j:512 * j + 512], ps[:, 2 + 2 * (j % 3):4 + 2 * (j % 3), :],
                                   ACT.Silu if j in (3, 4) else ACT.Copy), "t%d" % j)
                    if n >= 5 and n % 2 and (n - 5) // 2 < 12:
                        silu((n - 5) // 2)
                gt = tok[:, :, T_GA:COLS]
                act.wait_ge(evac.sem, evac.at("t8", l))
                onl.inc(AC(gt, gt, ACT.Sigmoid), "sig")
                with act.Fori(0, 4) as i:
                    for s in range(2):
                        act.wait_ge(dn_p.sem, dn_p.at("tr%d" % s, l, i))
                        act.wait_ge(dn_p.sem, dn_p.at("SF%d" % s, l, i - 1))
                        if s == 0:
                            act.wait_ge(l2_v.sem, l2_v.at("nm1", l, 3))
                        odn.inc(AC(ktv[s], ps[:, 3 * s, 0:384].rearrange("p (a b) -> p a b", a=3), ACT.Copy), "tok%d" % s)
                    for s in range(2):
                        act.wait_ge(dn_v.sem, dn_v.at("t%d" % s, l, i))
                        odn.inc(AC(ET[s], ET[s], ACT.Exp), "ET%d" % s)
                    for v in lv:
                        for s in range(2):
                            act.wait_ge(dn_p.sem, dn_p.at("b%d_%d" % (v, s), l, i))
                            if v < LEVELS - 1:
                                odn.inc(AC(XX[s].rearrange("p x d g t -> p x (d g t)"), ps[:, 3 * s + 1:3 * s + 3, :], ACT.Copy),
                                        "E%d_%d" % (v, s))
                            else:
                                odn.inc(AC(XX[s][:, 1].rearrange("p d g t -> p (d g t)"), ps[:, 3 * s + 2, :], ACT.Copy),
                                        "E%d_%d" % (v, s))
                    for s in range(2):
                        act.wait_ge(dn_p.sem, dn_p.at("V%d" % s, l, i))
                        for d in range(2):
                            for g in range(G):
                                odn.inc(AC(VN[s][:, d, g], ps[:, 3 * s + 1, (2 * d + g) * P:(2 * d + g + 1) * P], ACT.Copy,
                                           scale=hc[s][:, 4, d, g:g + 1]), "VN%d" % s)
                    for s in range(2):
                        act.wait_ge(dn_p.sem, dn_p.at("SF%d" % s, l, i))
                        act.wait_ge(s_state[s], i * 16 + 64 * l)
                        odn.inc(AC(sfo[s], ps[:, 3 * s + 1, 0:256].rearrange("p (a b) -> p a b", a=2), ACT.Copy), "Sf%d" % s)
                    for s in range(2):
                        act.wait_ge(dn_v.sem, dn_v.at("ob%d" % s, l, i))
                        for g in range(G):
                            odn.inc(AC(junk[s][:, g], osb[s][:, g], ACT.Square, accum_out=oss[s][:, g:g + 1]), "sq%d" % s)
                act.wait_ge(kt_p.sem, kt_p.at("k", l))
                okt.inc(AC(kTb[:, 0], ps[:, 0, 0:384].rearrange("p (a b) -> p a b", a=3), ACT.Copy), "k")
                okt.inc(AC(kTb[:, 1], ps[:, 1, 0:384].rearrange("p (a b) -> p a b", a=3), ACT.Copy), "o")
                with act.Fori(0, 4) as i:
                    for s in range(2):
                        act.wait_ge(at_p.sem, at_p.at("qt%d" % s, l, i))
                        act.wait_ge(at_p.sem, at_p.at("sc%d" % s, l, i - 1))
                        oat.inc(AC(qT[s], ps[:, 4 * s, 0:256].rearrange("p (a b) -> p a b", a=2), ACT.Copy, scale=SCALE), "qe%d" % s)
                    for s in range(2):
                        act.wait_ge(at_v.sem, at_v.at("nm%d" % s, l, i))
                        act.wait_ge(at_p.sem, at_p.at("pt%d" % s, l, i - 1))
                        for g in range(G):
                            oat.inc(AC(pr[s][:, g:1 + 2 * g], ps[:, 4 * s + 1, g * P:(1 + 2 * g) * P]
                                       .rearrange("p (a b) -> p a b", b=P), ACT.Exp, bias=am[s][2][:, g:g + 1],
                                       accum_out=am[s][3][:, g:g + 1]), "P%d" % s)
                    for s in range(2):
                        act.wait_ge(at_v.sem, at_v.at("sd%d" % s, l, i))
                        oat.inc(AC(am[s][5][:, 0:2], am[s][4][:, 0:2], ACT.Exp), "se%d" % s)
                    for s in range(2):
                        act.wait_ge(at_p.sem, at_p.at("pt%d" % s, l, i))
                        act.wait_ge(at_p.sem, at_p.at("pv%d" % s, l, i - 1))
                        oat.inc(AC(prT[s], ps[:, 4 * s + 2, 0:384].rearrange("p (a b) -> p a b", a=3), ACT.Copy), "pe%d" % s)
                for j in range(8):
                    b, g, h = j // 4, j // 2 % 2, j % 2
                    act.wait_ge(out_p.sem, out_p.at("tr%d" % j, l))
                    oout.inc(AC((hT, bT)[b][:, 0, 4 * h:4 * h + 4, g * P:(g + 1) * P],
                                ps[:, j, :].rearrange("p (k t) -> p k t", k=4), ACT.Copy), "ev%d" % j)
                for j in range(11):
                    high(act, u_out[l] + j)
                for j in range(4):
                    g, h = j // 2, j % 2
                    act.wait_ge(out_p.sem, out_p.at("mt%d" % j, l))
                    oout.inc(AC(hT[:, 0, 4 * h:4 * h + 4, g * P:(g + 1) * P],
                                ps[:, j, :].rearrange("p (k t) -> p k t", k=4), ACT.Copy), "me%d" % j)
                high(act, u_out[l] + 11)
                ss_(l, 1, lambda g: y_sb[:, g, :], lambda g: act.wait_ge(out_v.sem, out_v.at("y", l) - 1 + g))
                ss_(l, 2, lambda g: xt[:, g, :], lambda g: act.wait_ge(res_v.sem, res_v.at("x", l, 0) - 1 + g))
                norm_(l, 1)
                act.wait_ge(s_out, 32 * (l + 1))
                if l == 0:
                    def silus(f, first=False):
                        if first:
                            wait_used(act, u_ff + 1)
                        else:
                            act.wait_ge(unit_used, f * 3 + (u_ff + 1 + WRING))
                        act.wait_ge(ff_v.sem, ff_v.at("mu", 0, f - 1))
                        for g in range(G):
                            off.inc(AC(f_hs[0][:, 256 * g:256 * g + 256], ps[:, g, 0:256], ACT.Silu), "si")

                    def hiddenT(f, s):
                        act.wait_ge(ff_p.sem, ff_p.at("ht", 0, f))
                        ofh.inc(AC(fT[:, s, 0].rearrange("p a b -> p (a b)"), ps[:, 2 + s, :], ACT.Copy), "he")

                    high(act, u_ff)
                    high(act, u_ff + 1)
                    high(act, u_ff + 2)
                    silus(0, True)
                    high(act, u_ff + 3)
                    high(act, u_ff + 4)
                    hiddenT(0, 0)
                    silus(1)
                    with act.Fori(0, (FF_STEPS - 3) // 4) as i:
                        for j in range(4):
                            for x in range(3):
                                high(act, u_ff + 5 + 3 * j + x, i)
                            hiddenT(i * 4 + (1 + j), (1 + j) % 2)
                            silus(i * 4 + (2 + j))
                    for x in range(3):
                        high(act, u_ff + 29 + x)
                    hiddenT(FF_STEPS - 2, 1)
                    silus(FF_STEPS - 1)
                    high(act, u_ff + 32)
                    hiddenT(FF_STEPS - 1, 0)
                else:
                    act.wait_ge(rt_v.sem, rt_v.at("d"))
                    ort.inc(AC(rcol[3], rcol[2], ACT.Exp), "ex")

                    def expert(i, u, r=0):
                        high(act, u, r)
                        high(act, u + 1, r)
                        for h in range(2):
                            act.wait_ge(moe_p.sem, moe_p.at("ga%d" % h, 0, i))
                            omo.inc(AC(hTe[0][:, 4 * h:4 * h + 4], ps[:, 6 + h, :].rearrange("p (k t) -> p k t", k=4), ACT.Copy),
                                    "ge%d" % h)
                        n = 2
                        for f in range(FB + 1):
                            last = gu_last(f) if f < FB else U_EXP - 3
                            while n <= last + (1 if f else 0):
                                high(act, u + n, r)
                                n += 1
                            if f:
                                act.wait_ge(moe_p.sem, moe_p.at("ht%d" % (f - 1), 0, i))
                                omo.inc(AC(fT[:, (f - 1) % 2, 0].rearrange("p a b -> p (a b)"), ps[:, 2 + (f - 1) % 2, :], ACT.Copy),
                                        "he%d" % (f - 1))
                                high(act, u + n, r)
                                n += 1
                            if f < FB:
                                wait_used(act, u + gu_last(f), r)
                                act.wait_ge(moe_v.sem, moe_v.at("mu%d" % (f - 1), 0, i) if f else moe_v.at("mu%d" % (FB - 1), 0, i - 1))
                                omo.inc(AC(f_hs[0], ps[:, 0, :], ACT.Silu), "si%d" % f)
                        assert n == U_EXP

                    with act.Fori(0, NEXP // 2) as i:
                        for j in range(2):
                            expert(i * 2 + j, u_moe + j * U_EXP, i * (2 * U_EXP // LOOP))
                    second_blocks(act, lambda e, x: expert(NEXP + x, u_moe + (NEXP + x) * U_EXP))
                ss_(l, 3, lambda g: y_sb[:, g, :], lambda g: act.wait_ge(ffe_v.sem, ffe_v.at("y", l) - 1 + g))

        @block.tensor
        def _(pe):
            for s in P_STEPS:
                pe.sem_inc(s.sem, s.per)
            (oi, onr, oga, ol2, odn, okt, oat, oout, ore, off, ort, omo) = (Order(s) for s in P_STEPS)
            mm = pe.matmul

            def tr(out, src, n=P):
                return pe.transpose(out, src, con[0:n, K_ID:K_ID + n])

            pe.wait_ge(init_a.sem, init_a.at("cond"))
            for k in range(KC):
                ins = tr(ps[:, 0, 2 * k:2 * k + 2], condS[:, k * P:(k + 1) * P], 2)
            oi.inc(ins, "condT")
            pe.wait_ge(init_v.sem, init_v.at("condT"))

            def used(ins):
                ins.then_inc(unit_used, 1)

            def prod(u, i, outs, wide=512):
                wait_hi(pe, u, i)
                for x in range(2):
                    for o, hi, lo, c, first, _ in outs:
                        mm(o, (hi, lo)[x], part(u, 0)[:, c:c + wide], start=(first and x == 0), stop=False)
                wait_lo(pe, u, i)
                for o, hi, lo, c, _, last in outs:
                    ins = mm(o, hi, part(u, 1)[:, c:c + wide], start=False, stop=last)
                used(ins)

            def bcast(bank, m, g):
                q, c = MODS[m]
                for n in range(2):
                    ins = mm(ps[:, bank + n, :], con[32 * q:32 * q + 2, K_SEL + g * P:K_SEL + (g + 1) * P],
                             mod_row(q, c, n), start=True, stop=True)
                return ins

            def norm_(l, n):
                for g in range(G):
                    bcast(4 * g, (1, 4)[n], g)
                    onr.inc(bcast(4 * g + 2, (0, 3)[n], g), "bc%d" % g)
                for g in range(G):
                    pe.wait_ge(nrm_v.sem, nrm_v.at("h%d" % g, l, n))
                    for h in range(2):
                        for k in range(4):
                            ins = tr(ps[:, 4 * g + h, k * P:(k + 1) * P], h_tok[:, g, (4 * h + k) * P:(4 * h + k + 1) * P])
                        onr.inc(ins, "t%d%d" % (g, h))
                pe.wait_ge(nrm_v.sem, nrm_v.at("l11", l, n))

            for l in range(DEPTH):
                if l:
                    pe.wait_ge(res_v.sem, res_v.at("x", l - 1, 1))
                pe.wait_ge(cnd_v.sem, cnd_v.at("lo", l))
                with pe.Fori(0, U_ADA // LOOP) as i:
                    for j in range(LOOP // 2):
                        pe.wait_ge(ada_v.sem, i * (LOOP // 2) + (ada_v.at("row", l) - 12 + j - 2))
                        for h in range(2):
                            prod(u_ada[l] + 2 * j + h, i,
                                 [(ps[:, j % 3, :], condR[0][:, 4 * h + k], condR[1][:, 4 * h + k], k * 512, h + k == 0, h == 1 and k == 3)
                                  for k in range(4)])
                pe.wait_ge(ada_v.sem, ada_v.at("mod", l))
                if l:
                    pe.wait_ge(res_v.sem, res_v.at("x", l - 1, 1))
                norm_(l, 0)
                pe.wait_ge(s_lay, 16 * LAY_DMAS * (l + 1))
                for g in range(G):
                    for k in range(KC):
                        for x in range(2):
                            ins = mm(ps[:, 0, 32 * g:32 * g + 32], hT[:, x, k, g * P:(g + 1) * P].bitcast(F32), wba[:, k, :],
                                     start=(k + x == 0), stop=(k == KC - 1 and x == 1))
                oga.inc(ins, "ba")
                oga.inc(tr(ps[:, 0, P:P + TAPS * QKV_CH], cwr[0:TAPS * QKV_CH, :], TAPS * QKV_CH), "cw")
                up = u_proj[l]
                for n in range(12):
                    if n >= 6:
                        pe.wait_ge(evac.sem, evac.at("b%d" % (n - 6), l))
                    elif n == 0:
                        pe.wait_ge(nrm_v.sem, nrm_v.at("l11", l, 0))
                    wait_hi(pe, up + n)
                    wait_lo(pe, up + n)
                    for c in range(2):
                        for k in range(KC):
                            for y, x in ((0, 0), (0, 1), (1, 0)):
                                ins = mm(ps[:, 2 + n % 6, 256 * c:256 * c + 256], part(up + n, y)[:, k * 256 + c * P:k * 256 + (c + 1) * P],
                                         hT[:, x, k, :], start=(k + x + y == 0), stop=(k == KC - 1 and y == 1))
                    used(ins)
                    if n == 3:
                        pe.wait_ge(gat_v.sem, gat_v.at("g0", l))
                        for d in range(2):
                            gd = ga[4][:, :, 8 * d:8 * d + 8]
                            mm(ps[:, 1, 16 * d:16 * d + 16], tri(d), gd, start=True, stop=True)
                            ins = mm(ps[:, 1, 32 + 16 * d:48 + 16 * d], ones, gd, start=True, stop=True)
                        oga.inc(ins, "gc")
                    l2_pe = {4 * i + 9: (0, i) for i in range(4)}
                    l2_pe.update({4 * i + 12: (1, i) for i in range(4)})

                    def l2_(n):
                        if n not in l2_pe:
                            return
                        what, i = l2_pe[n]
                        if what == 0:
                            pe.wait_ge(l2_g.sem, l2_g.at("sq1", l, i))
                            pe.wait_ge(l2_v.sem, l2_v.at("nm1", l, i - 1))
                            if i == 0:
                                pe.wait_ge(gat_v.sem, gat_v.at("ba", l))
                            for s in range(2):
                                for c in range(2):
                                    for g in range(G):
                                        ins = mm(ps[:, 0, 4 * s + 2 * c + g:4 * s + 2 * c + g + 1], l2s[s][:, c, g], ones[:, 0:1],
                                                 start=True, stop=True)
                            ol2.inc(ins, "ss")
                        else:
                            pe.wait_ge(l2_g.sem, l2_g.at("pw", l, i))
                            if i == 0:
                                pe.wait_ge(gat_v.sem, gat_v.at("gcs", l))
                            for s in range(2):
                                for x in range(4):
                                    ins = mm(ps[:, 1 - s, x * P:(x + 1) * P], l2c[:, 4 * s + x:4 * s + x + 1].to_broadcast([P, P]),
                                             ident, start=True, stop=True)
                                ol2.inc(ins, "bc%d" % s)
                    l2_(n)
                for n in range(12, U_PROJ):
                    j, h = (n - 12) // 2, n % 2
                    if h == 0:
                        for m in ([6 + 2 * j, 7 + 2 * j] if j < 3 else []):
                            pe.wait_ge(evac.sem, evac.at("b%d" % m, l))
                        if j >= 3:
                            pe.wait_ge(evac.sem, evac.at("t%d" % (j - 3), l))
                    prod(up + n, 0, [(ps[:, 2 + 2 * (j % 3) + g, :], hT[:, 0, 4 * h + k, g * P:(g + 1) * P],
                                      hT[:, 1, 4 * h + k, g * P:(g + 1) * P], k * 512, h + k == 0, h == 1 and k == 3)
                                     for k in range(4) for g in range(G)])
                    l2_(n)
                pe.wait_ge(evac.sem, evac.at("t8", l))
                pe.wait_ge(l2_v.sem, l2_v.at("nm1", l, 3))
                with pe.Fori(0, 4) as i:
                    def each(f):
                        for s in range(2):
                            f(s, 3 * s)

                    def inst():
                        return [(d, g, (2 * d + g) * P) for d in range(2) for g in range(G)]

                    def turn(s, b):
                        pe.wait_ge(dn_g.sem, dn_g.at("kqv%d" % s, l, i))
                        pe.wait_ge(dn_v.sem, dn_v.at("ob%d" % s, l, i - 1))
                        tr(ps[:, b, 0:P], kqv[s][:, 1, 0])
                        tr(ps[:, b, P:2 * P], kqv[s][:, 2, 0])
                        odn.inc(tr(ps[:, b, 2 * P:3 * P], kqv[s][:, 2, 1]), "tr%d" % s)
                    each(turn)

                    def gram(s, b):
                        pe.wait_ge(dn_a.sem, dn_a.at("Sf%d" % s, l, i - 1))
                        for g in range(G):
                            ins = mm(ps[:, b + 1, 256 * g:256 * g + 256], kqv[s][:, 1, g], kqv[s][:, 0:2, g, :], start=True, stop=True)
                        odn.inc(ins, "G%d" % s)
                    each(gram)

                    def decay(s, b):
                        pe.wait_ge(dn_g.sem, dn_g.at("hc%d" % s, l, i))
                        pe.wait_ge(dn_v.sem, dn_v.at("oc%d" % s, l, i - 1))
                        for d, g, c in inst():
                            ins = mm(ps[:, b + 2, c:c + P], hc[s][:, 0, d, g:g + 1].to_broadcast([P, P]), tri(d), start=True, stop=True)
                        odn.inc(ins, "gr%d" % s)
                    each(decay)

                    def first(s, b):
                        pe.wait_ge(dn_v.sem, dn_v.at("AI%d" % s, l, i))
                        pe.wait_ge(dn_a.sem, dn_a.at("tok%d" % s, l, i))
                        for d, g, c in inst():
                            ins = tr(ps[:, b, c:c + P], AT[s][:, d, g])
                        odn.inc(ins, "m%d" % s)
                    each(first)
                    for v in lv:
                        def left(s, b):
                            if v == 1:
                                pe.wait_ge(dn_v.sem, dn_v.at("X%d" % s, l, i))
                            else:
                                pe.wait_ge(dn_a.sem, dn_a.at("E%d_%d" % (v - 1, s), l, i))
                            for d, g, c in inst():
                                ins = mm(ps[:, b, c:c + P], AT[s][:, d, g], XX[s][:, 0, d, g], start=True, stop=True)
                            odn.inc(ins, "a%d_%d" % (v, s))
                        each(left)

                        def right(s, b):
                            if v == 1:
                                pe.wait_ge(dn_g.sem, dn_g.at("XT%d" % s, l, i))
                                pe.wait_ge(dn_v.sem, dn_v.at("AI%d" % s, l, i))
                            pe.wait_ge(dn_v.sem, dn_v.at("M%d_%d" % (v, s), l, i))
                            for d, g, c in inst():
                                if v < LEVELS - 1:
                                    mm(ps[:, b + 1, c:c + P], XX[s][:, 1, d, g], MM[s][:, d, g], start=True, stop=True)
                                ins = mm(ps[:, b + 2, c:c + P], MM[s][:, d, g], XX[s][:, 1, d, g], start=True, stop=True)
                            odn.inc(ins, "b%d_%d" % (v, s))
                        each(right)

                    def state(s, b):
                        pe.wait_ge(s_st, 32 * (l + 1))
                        for x in range(2):
                            ins = mm(ps[:, b, 256 * x:256 * x + 256], kqv[s][:, 1 - x, 1],
                                     s0[:, bass.ds(i * 2 + s, 1)].rearrange("p h d v -> p (h d v)"), start=True, stop=True)
                        odn.inc(ins, "kS%d" % s)
                    each(state)

                    def values(s, b):
                        pe.wait_ge(dn_a.sem, dn_a.at("E%d_%d" % (LEVELS - 1, s), l, i))
                        pe.wait_ge(dn_v.sem, dn_v.at("R%d" % s, l, i))
                        for d, g, c in inst():
                            ins = mm(ps[:, b + 1, c:c + P], XX[s][:, 1, d, g], RP[s][:, d] if g else ktv[s][:, 1],
                                     start=True, stop=True)
                        odn.inc(ins, "V%d" % s)
                    each(values)

                    def out(s, b):
                        pe.wait_ge(dn_a.sem, dn_a.at("VN%d" % s, l, i))
                        for g in range(G):
                            for d in range(2):
                                ins = mm(ps[:, b + 2, g * P:(g + 1) * P], attn[s][:, d, g], VN[s][:, d, g],
                                         start=(d == 0), stop=(d == 1))
                        odn.inc(ins, "O%d" % s)
                    each(out)

                    def final(s, b):
                        pe.wait_ge(dn_v.sem, dn_v.at("VD%d" % s, l, i))
                        odn.inc(mm(ps[:, b + 1, 0:256], ktv[s][:, 0], VD[s].rearrange("p d v -> p (d v)"),
                                   start=True, stop=True), "SF%d" % s)
                    each(final)
                pe.wait_ge(rp_v.sem, rp_v.at("x2", l))
                pe.wait_ge(dn_v.sem, dn_v.at("y1", l, 3))
                pe.wait_ge(dn_a.sem, dn_a.at("sq1", l, 3))
                for v in range(HKV):
                    tr(ps[:, v, 0:P], tok[:, 0, T_K + v * P:T_K + (v + 1) * P])
                    tr(ps[:, v, P:2 * P], cache_k[:, v, :])
                    ins = tr(ps[:, v, 2 * P:3 * P], tok[:, 1, T_K + v * P:T_K + (v + 1) * P])
                okt.inc(ins, "k")
                pe.wait_ge(kt_a.sem, kt_a.at("o", l))
                with pe.Fori(0, 4) as i:
                    for s in range(2):
                        pe.wait_ge(at_g.sem, at_g.at("q%d" % s, l, i))
                        pe.wait_ge(at_a.sem, at_a.at("qe%d" % s, l, i - 1))
                        tr(ps[:, 4 * s, 0:P], qst[s][:, 0])
                        oat.inc(tr(ps[:, 4 * s, P:2 * P], qst[s][:, 1]), "qt%d" % s)
                    for s in range(2):
                        pe.wait_ge(at_a.sem, at_a.at("qe%d" % s, l, i))
                        pe.wait_ge(at_a.sem, at_a.at("P%d" % s, l, i - 1))
                        mm(ps[:, 4 * s + 1, 0:P], qT[s][:, 0], kTb[:, s, 0], start=True, stop=True)
                        oat.inc(mm(ps[:, 4 * s + 1, P:3 * P], qT[s][:, 1], kTb[:, s, 1:3].rearrange("p a b -> p (a b)"),
                                   start=True, stop=True), "sc%d" % s)
                    for s in range(2):
                        pe.wait_ge(at_a.sem, at_a.at("P%d" % s, l, i))
                        pe.wait_ge(at_a.sem, at_a.at("pe%d" % s, l, i - 1))
                        for k in range(3):
                            ins = tr(ps[:, 4 * s + 2, k * P:(k + 1) * P], pr[s][:, k])
                        oat.inc(ins, "pt%d" % s)
                    for s in range(2):
                        pe.wait_ge(at_a.sem, at_a.at("pe%d" % s, l, i))
                        pe.wait_ge(at_v.sem, at_v.at("o%d" % s, l, i - 1))
                        mm(ps[:, 4 * s + 3, 0:P], prT[s][:, 0], tok[:, 0, T_V + s * P:T_V + (s + 1) * P], start=True, stop=True)
                        mm(ps[:, 4 * s + 3, P:2 * P], prT[s][:, 1], cache_v[:, s, :], start=True, stop=False)
                        oat.inc(mm(ps[:, 4 * s + 3, P:2 * P], prT[s][:, 2], tok[:, 1, T_V + s * P:T_V + (s + 1) * P],
                                   start=False, stop=True), "pv%d" % s)
                pe.wait_ge(at_v.sem, at_v.at("o1", l, 3))
                for j in range(8):
                    b, g, h = j // 4, j // 2 % 2, j % 2
                    for k in range(4):
                        c = (0, T_Z)[b] + (4 * h + k) * P
                        ins = tr(ps[:, j, k * P:(k + 1) * P], tok[:, g, c:c + P])
                    oout.inc(ins, "tr%d" % j)
                pe.wait_ge(out_v.sem, out_v.at("lv7", l))
                u = [u_out[l]]

                def project(src, bank):
                    for n in range(2):
                        for h in range(2):
                            prod(u[0], 0, [(ps[:, bank(n, g), :], src[:, 0, 4 * h + k, g * P:(g + 1) * P],
                                            src[:, 1, 4 * h + k, g * P:(g + 1) * P], k * 512, h + k == 0, h == 1 and k == 3)
                                           for k in range(4) for g in range(G)])
                            u[0] += 1
                project(hT, lambda n, g: 2 * n + g)
                project(bT, lambda n, g: 4 + 2 * n + g)
                pe.wait_ge(out_v.sem, out_v.at("m", l))
                for j in range(4):
                    g, h = j // 2, j % 2
                    for k in range(4):
                        c = T_GA + (4 * h + k) * P
                        ins = tr(ps[:, j, k * P:(k + 1) * P], tok[:, g, c:c + P])
                    oout.inc(ins, "mt%d" % j)
                pe.wait_ge(out_v.sem, out_v.at("ml3", l))
                project(hT, lambda n, g: 4 + 2 * g + n)

                def gate_rows(n):
                    for g in range(G):
                        ins = bcast(2 * g, (2, 5)[n], g)
                    ore.inc(ins, "gb")
                gate_rows(0)
                pe.wait_ge(res_v.sem, res_v.at("x", l, 0))
                norm_(l, 1)
                if l == 0:
                    def gate_up(u, i, f):
                        pe.wait_ge(ff_v.sem, ff_v.at("mu", 0, f - 1))
                        for x in range(2):
                            prod(u + x, i, [(ps[:, g, 256 * x:256 * x + 256], hT[:, 0, k, g * P:(g + 1) * P],
                                             hT[:, 1, k, g * P:(g + 1) * P], k * 256, k == 0, k == KC - 1)
                                            for k in range(KC) for g in range(G)], 256)

                    def down(u, i, f, s, at_=None):
                        pe.wait_ge(ff_v.sem, ff_v.at("mu", 0, f))
                        for k in range(4):
                            ins = tr(ps[:, 2 + s, k * P:(k + 1) * P], f_hid[s][:, k * P:(k + 1) * P])
                        off.inc(ins, "ht")
                        pe.wait_ge(ff_l.sem, ff_l.at("hl", 0, f))
                        prod(u, i, [(ps[:, 4 + 2 * g + n, :], fT[:, s, 0, 2 * g + k], fT[:, s, 1, 2 * g + k],
                                     k * 1024 + n * 512, at_ == 0 and k == 0, at_ == 1 and k == 1)
                                    for k in range(2) for g in range(G) for n in range(2)])
                    gate_up(u_ff, 0, 0)
                    gate_up(u_ff + 2, 0, 1)
                    down(u_ff + 4, 0, 0, 0, 0)
                    with pe.Fori(0, (FF_STEPS - 3) // 4) as i:
                        for j in range(4):
                            gate_up(u_ff + 5 + 3 * j, i, i * 4 + (2 + j))
                            down(u_ff + 7 + 3 * j, i, i * 4 + (1 + j), (1 + j) % 2)
                    w = u_ff + 3 * FF_STEPS - 4
                    gate_up(w, 0, FF_STEPS - 1)
                    down(w + 2, 0, FF_STEPS - 2, 1)
                    down(w + 3, 0, FF_STEPS - 1, 0, 1)
                else:
                    for g in range(G):
                        for k in range(KC):
                            for x in range(2):
                                ins = mm(ps[:, 0, NEXP * g:NEXP * (g + 1)], hT[:, x, k, g * P:(g + 1) * P].bitcast(F32), wr[:, k, :],
                                         start=(k + x == 0), stop=(k == KC - 1 and x == 1))
                    ort.inc(ins, "lg")
                    pe.wait_ge(rt_v.sem, rt_v.at("mk"))
                    before = con[:, K_STR:K_STR + P]
                    mk = rt[6]
                    mm(ps[:, 1, 0:8], before, mk[:, 0], start=True, stop=True)
                    mm(ps[:, 1, 8:16], before, mk[:, 1], start=True, stop=False)
                    mm(ps[:, 1, 8:16], ones, mk[:, 0], start=False, stop=True)
                    mm(ps[:, 1, 16:24], ones, mk[:, 0], start=True, stop=False)
                    ort.inc(mm(ps[:, 1, 16:24], ones, mk[:, 1], start=False, stop=True), "pos")
                    pe.wait_ge(rt_v.sem, rt_v.at("pos"))

                    def expert(i, u, r=0):
                        pe.wait_ge(moe_v.sem, moe_v.at("selc", 0, i))
                        pe.wait_ge(moe_v.sem, moe_v.at("add", 0, i - 1))
                        for g in range(G):
                            ins = tr(ps[:, 2, g * P:(g + 1) * P], selc[:, g])
                        omo.inc(ins, "sct")
                        for h in range(2):
                            for k in range(4):
                                for g in range(G):
                                    ins = mm(ps[:, 6 + h, k * P:(k + 1) * P], h_tok[:, g, (4 * h + k) * P:(4 * h + k + 1) * P],
                                             sel[:, g], start=(g == 0), stop=(g == 1))
                            omo.inc(ins, "ga%d" % h)
                        pe.wait_ge(moe_v.sem, moe_v.at("gl1", 0, i))
                        for f in range(FB + 1):
                            if f < FB:
                                pe.wait_ge(moe_v.sem, moe_v.at("mu%d" % (f - 1), 0, i) if f else moe_v.at("mu%d" % (FB - 1), 0, i - 1))
                                for x in range(2):
                                    for h in range(2):
                                        prod(u, r, [(ps[:, x, :], hTe[0][:, 4 * h + k], hTe[1][:, 4 * h + k], k * 512,
                                                     h + k == 0, h == 1 and k == 3) for k in range(4)])
                                        u += 1
                            if f > 0:
                                b = (f - 1) % 2
                                pe.wait_ge(moe_v.sem, moe_v.at("mu%d" % (f - 1), 0, i))
                                for k in range(4):
                                    ins = tr(ps[:, 2 + b, k * P:(k + 1) * P], f_hid[b][:, k * P:(k + 1) * P])
                                omo.inc(ins, "ht%d" % (f - 1))
                                pe.wait_ge(moe_v.sem, moe_v.at("hl%d" % (f - 1), 0, i))
                                for h in range(2):
                                    prod(u, r, [(ps[:, 4 + n, :], fT[:, b, 0, 2 * h + k], fT[:, b, 1, 2 * h + k],
                                                 k * 1024 + n * 512, f == 1 and h + k == 0, f == FB and h + k == 2)
                                                for k in range(2) for n in range(2)])
                                    u += 1
                        pe.wait_ge(moe_v.sem, moe_v.at("ye", 0, i))
                        for g in range(G):
                            for n in range(2):
                                ins = mm(ps[:, (6, 2)[g] + n, :], selT[:, g], ye[:, n * 512:(n + 1) * 512], start=True, stop=True)
                            omo.inc(ins, "sc%d" % g)

                    with pe.Fori(0, NEXP // 2) as i:
                        for j in range(2):
                            expert(i * 2 + j, u_moe + j * U_EXP, i * (2 * U_EXP // LOOP))
                    second_blocks(pe, lambda e, x: expert(NEXP + x, u_moe + (NEXP + x) * U_EXP))
                pe.wait_ge(ffe_v.sem, ffe_v.at("y", l))
                gate_rows(1)

        @block.vector
        def _(dve):
            for s in V_STEPS:
                dve.sem_inc(s.sem, s.per)
            (oi, ocd, oad, orm, onr, oga, ocv, onl, ol2, odn, orp, oat, oout, ore, off, ofl, ofe, ort, omo) = (Order(s) for s in V_STEPS)
            TT, TS, STT, CP = dve.tensor_tensor, dve.tensor_scalar, dve.scalar_tensor_tensor, dve.tensor_copy

            def own(st, name, l=0, i=0):
                dve.wait_ge(st.sem, st.at(name, l, i))

            oi.inc(dve.memset(mhalf, -0.5), "half")
            dve.wait_ge(init_p.sem, init_p.at("condT"))
            oi.inc(CP(condT, ps[:, 0, 0:16].rearrange("p (k c) -> p k c", c=2)), "condT")

            def ms_(l, k):
                dve.wait_ge(rms_a.sem, rms_a.at("ss", l, k))
                if k or l:
                    dve.wait_ge(rms_g.sem, rms_g.at("rstd", l, k - 1))
                orm.inc(TS(ms, ss, 1.0 / D, EPS, ALU.mult, ALU.add), "ms")

            def rest(dst, h, g, bank):
                hi, lo = (dst[:, x, 4 * h:4 * h + 4, g * P:(g + 1) * P] for x in range(2))
                return TT(lo, ps[:, bank, :].rearrange("p (k t) -> p k t", k=4), hi.bitcast(F32), ALU.subtract)

            def norm_(l, n):
                ms_(l, 2 * n)
                dve.wait_ge(rms_g.sem, rms_g.at("rstd", l, 2 * n))
                for g in range(G):
                    dve.wait_ge(nrm_p.sem, nrm_p.at("bc%d" % g, l, n))
                    onr.inc(STT(h_tok[:, g, :], xt[:, g, :], rstd[:, g:g + 1],
                                ps[:, 4 * g:4 * g + 2, :].rearrange("p b c -> p (b c)"), ALU.mult, ALU.mult), "a%d" % g)
                    own(nrm_v, "a%d" % g, l, n)
                    onr.inc(TT(h_tok[:, g, :], h_tok[:, g, :], ps[:, 4 * g + 2:4 * g + 4, :].rearrange("p b c -> p (b c)"), ALU.add),
                            "h%d" % g)
                for g in range(G):
                    for h in range(2):
                        dve.wait_ge(nrm_a.sem, nrm_a.at("e%d%d" % (g, h), l, n))
                        onr.inc(rest(hT, h, g, 4 * g + h), "l%d%d" % (g, h))

            def resid(l, n):
                ms_(l, 2 * n + 1)
                dve.wait_ge(rms_g.sem, rms_g.at("rstd", l, 2 * n + 1))
                dve.wait_ge(res_p.sem, res_p.at("gb", l, n))
                for g in range(G):
                    ore.inc(STT(y_sb[:, g, :], y_sb[:, g, :], rstd[:, g:g + 1],
                                ps[:, 2 * g:2 * g + 2, :].rearrange("p b c -> p (b c)"), ALU.mult, ALU.mult), "t")
                own(res_v, "t", l, n)
                for g in range(G):
                    ore.inc(TT(xt[:, g, :], xt[:, g, :], y_sb[:, g, :], ALU.add), "x")

            for l in range(DEPTH):
                dve.wait_ge(cnd_a.sem, cnd_a.at("hi", l))
                cT = condT.rearrange("p k (o c) -> p k o c", o=1).to_broadcast([P, KC, P // 2, 2])
                c0, c1 = (x.rearrange("p k (o c) -> p k o c", c=2) for x in condR)
                own(init_v, "condT")
                ocd.inc(TT(c1, cT, c0.bitcast(F32), ALU.subtract), "lo")
                for b in range(13):
                    if b < 12:
                        low(dve, u_ada[l] + 2 * b)
                        low(dve, u_ada[l] + 2 * b + 1)
                    if b == 0:
                        dve.wait_ge(s_lay, 16 * LAY_DMAS * (l + 1))
                    else:
                        b -= 1
                        q, c = MODS[b // 2]
                        wait_used(dve, u_ada[l] + 2 * b + 1)
                        m = mod_row(q, c, b % 2)
                        oad.inc(TT(m, ps[0:2, b % 3, :], m, ALU.add), "row")
                own(ada_v, "row", l)
                for m in GAIN:
                    q, c = MODS[m]
                    mo, gn = mod[32 * q:32 * q + 2, c, :], ngr[32 * q:32 * q + 2, c, :]
                    oad.inc(STT(mo, mo, 1.0 if m in (1, 4) else 0.0, gn, ALU.add, ALU.mult), "mod")
                norm_(l, 0)
                up = u_proj[l]

                def split(x):
                    return x.rearrange("p g (d h) -> p g d h", d=2)

                def to_gt(q):
                    return GT[:, :, q, :, :].rearrange("p h d g -> p g d h")

                def dirs(x):
                    return x.rearrange("p (d g h) -> p d g h", d=2, g=G)

                def to_dirs(q):
                    return GT[:, :, q, :, :].rearrange("p h d g -> p d g h")

                def decay_in():
                    dve.wait_ge(gat_p.sem, gat_p.at("cw", l))
                    oga.inc(CP(cw[:, 0:TAPS * QKV_CH], ps[:, 0, P:P + TAPS * QKV_CH]), "cw")
                    oga.inc(CP(ba, ps[:, 0, 0:64].rearrange("p (g c) -> p g c", g=G)), "ba")
                    own(gat_v, "ba", l)
                    oga.inc(TT(ga[0], ba[:, :, 16:32], dtb.rearrange("p (o c) -> p o c", o=1).to_broadcast([P, G, 16]), ALU.add), "a")
                    own(gat_v, "a", l)
                    oga.inc(STT(ga[1], ga[0], -1.0, ga[0], ALU.mult, ALU.min), "na")
                    dve.wait_ge(gat_a.sem, gat_a.at("el", l))
                    oga.inc(TS(ga[2], ga[2], 1.0, None, ALU.add), "e1")
                    dve.wait_ge(gat_a.sem, gat_a.at("ln", l))
                    oga.inc(STT(ga[3], ga[0], 0.0, ga[3], ALU.max, ALU.add), "sp")
                    own(gat_v, "sp", l)
                    oga.inc(STT(ga[4], ga[3], -1.0, ealog.rearrange("p (o c) -> p o c", o=1).to_broadcast([P, G, 16]),
                                ALU.mult, ALU.mult), "g0")
                    own(gat_v, "g0", l)
                    oga.inc(CP(to_gt(0), split(ga[4])), "gcol")

                def decay_sums():
                    dve.wait_ge(gat_p.sem, gat_p.at("gc", l))
                    oga.inc(CP(gcs, ps[:, 1, 0:64]), "gcs")
                    own(gat_v, "gcs", l)
                    oga.inc(TT(gcs[:, 32:64], gcs[:, 32:64], gcs[:, 0:32], ALU.subtract), "kd")
                    oga.inc(CP(to_dirs(1), dirs(gcs[:, 0:32])), "gc")

                def decay_out():
                    dve.wait_ge(gat_a.sem, gat_a.at("ex", l))
                    oga.inc(CP(to_dirs(2), dirs(gex[:, 0:32])), "egc")
                    oga.inc(TS(to_dirs(3), dirs(gex[:, 0:32]), -1.0, None, ALU.mult), "negc")
                    oga.inc(CP(to_dirs(5), dirs(gex[:, 32:64])), "ekd")
                    oga.inc(TS(eb, eb, 1.0, None, ALU.add), "b1")
                    own(gat_v, "b1", l)
                    oga.inc(dve.reciprocal(eb, eb), "rb")
                    own(gat_v, "rb", l)
                    oga.inc(CP(to_gt(4), split(eb)), "beta")

                def conv(p):
                    dve.wait_ge(evac.sem, evac.at("b%d" % p, l))
                    own(gat_v, "cw", l)
                    for j in range(TAPS):
                        for s in range(2):
                            c = 2 * PAIRS[p] + s
                            x, w = qkv[:, c, :, j:j + P], cw[:, j * QKV_CH + c:j * QKV_CH + c + 1]
                            if j == 0:
                                dve.wait_ge(cnv_a.sem, cnv_a.at("s%d" % s, l, p - 1))
                                ocv.inc(TS(acc[s], x, w, None, ALU.mult), "t%d%d" % (j, s))
                            else:
                                own(cnv_v, "t%d%d" % (j - 1, s), l, p)
                                ocv.inc(STT(acc[s], x, w, acc[s], ALU.mult, ALU.add), "t%d%d" % (j, s))

                def norm_in(i):
                    dve.wait_ge(l2_p.sem, l2_p.at("ss", l, i))
                    dve.wait_ge(l2_p.sem, l2_p.at("bc1", l, i - 1))
                    ol2.inc(TS(l2c, ps[:, 0, 0:8], EPS, None, ALU.add), "ep")

                def norm_out(i):
                    for s in range(2):
                        x = qkv[:, 2 * i + 8 * s:2 * i + 8 * s + 2, :, PAD:PAD + P].rearrange("p a g t -> p (a g) t")
                        dve.wait_ge(l2_p.sem, l2_p.at("bc%d" % s, l, i))
                        ol2.inc(STT(x, x, SCALE if s == 0 else 1.0, ps[:, 1 - s, :].rearrange("p (a t) -> p a t", a=4),
                                    ALU.mult, ALU.mult), "nm%d" % s)

                for n in range(U_PROJ):
                    low(dve, up + n)
                    if n == 2:
                        decay_in()
                    if n == 5:
                        decay_sums()
                    if n == 7:
                        decay_out()
                    if n >= 3 and n % 2 and (n - 3) // 2 < 12:
                        conv((n - 3) // 2)
                    if n >= 10 and (n - 10) % 4 == 0 and (n - 10) // 4 < 4:
                        norm_in((n - 10) // 4)
                    if n >= 13 and (n - 13) % 4 == 0 and (n - 13) // 4 < 4:
                        norm_out((n - 13) // 4)
                dve.wait_ge(evac.sem, evac.at("t4", l))
                z = tok[:, :, T_Z:T_Z + D].rearrange("p g (h v) -> p g h v", h=DH)
                onl.inc(TT(z, z, dng[:, :].rearrange("p (a b v) -> p a b v", a=1, b=1).to_broadcast([P, G, DH, P]), ALU.mult), "z")
                with dve.Fori(0, 4) as i:
                    def each(f):
                        for s in range(2):
                            f(s, 3 * s)

                    def w4(s, name):
                        own(dn_v, name % s, l, i)

                    def clamp(s, b):
                        dve.wait_ge(dn_p.sem, dn_p.at("gr%d" % s, l, i))
                        dve.wait_ge(dn_g.sem, dn_g.at("hc%d" % s, l, i))
                        for d in range(2):
                            for g in range(G):
                                c = (2 * d + g) * P
                                odn.inc(TS(ET[s][:, d, g], ps[:, b + 2, c:c + P], hc[s][:, 1, d, g:g + 1], 0.0,
                                           ALU.subtract, ALU.min), "t%d" % s)
                    each(clamp)

                    def pair(s, b, x):
                        return ps[:, b + 1, :].rearrange("p (o g x k) -> p o g x k", o=1, g=G, x=2)[:, :, :, x].to_broadcast([P, 2, G, P])

                    def attn_(s, b):
                        dve.wait_ge(dn_g.sem, dn_g.at("EM%d" % s, l, i))
                        dve.wait_ge(dn_p.sem, dn_p.at("G%d" % s, l, i))
                        dve.wait_ge(dn_p.sem, dn_p.at("O%d" % s, l, i - 1))
                        odn.inc(TT(attn[s], ET[s], pair(s, b, 0), ALU.mult), "at%d" % s)
                    each(attn_)

                    def w_(s, b):
                        odn.inc(TT(AT[s], ET[s], pair(s, b, 1), ALU.mult), "W%d" % s)
                    each(w_)

                    def a_(s, b):
                        w4(s, "W%d")
                        for d in range(2):
                            for g in range(G):
                                odn.inc(STT(AT[s][:, d, g], AT[s][:, d, g], hc[s][:, 4, d, g:g + 1],
                                            con[:, K_STR + d * P:K_STR + (d + 1) * P], ALU.mult, ALU.mult), "A%d" % s)
                    each(a_)

                    def ai(s, b):
                        w4(s, "A%d")
                        odn.inc(TT(AT[s], AT[s], ident.rearrange("p (a b k) -> p a b k", a=1, b=1).to_broadcast([P, 2, G, P]),
                                   ALU.add), "AI%d" % s)
                    each(ai)

                    def x_(s, b):
                        dve.wait_ge(s_lev, 16 * (l + 1))
                        dve.wait_ge(dn_p.sem, dn_p.at("m%d" % s, l, i))
                        odn.inc(TT(XX[s][:, 0], ps[:, b, :].rearrange("p (d g k) -> p d g k", d=2, g=G), two(lev[:, 0]), ALU.mult), "X%d" % s)
                    each(x_)
                    for v in lv:
                        def m_(s, b):
                            dve.wait_ge(dn_p.sem, dn_p.at("a%d_%d" % (v, s), l, i))
                            if v > 1:
                                dve.wait_ge(dn_p.sem, dn_p.at("b%d_%d" % (v - 1, s), l, i))
                            odn.inc(TT(MM[s], ps[:, b, :].rearrange("p (d g k) -> p d g k", d=2, g=G),
                                       two(lev[:, v]), ALU.mult), "M%d_%d" % (v, s))
                        each(m_)

                    def r_(s, b):
                        dve.wait_ge(dn_p.sem, dn_p.at("kS%d" % s, l, i))
                        for d in range(2):
                            odn.inc(STT(RP[s][:, d], ps[:, b, d * P:(d + 1) * P], hc[s][:, 3, d, 1:2], ktv[s][:, 2],
                                        ALU.mult, ALU.add), "R%d" % s)
                    each(r_)

                    def vd(s, b):
                        dve.wait_ge(dn_a.sem, dn_a.at("VN%d" % s, l, i))
                        for d in range(2):
                            odn.inc(TS(VD[s][:, d], VN[s][:, d, 0], hc[s][:, 5, d, 0:1], None, ALU.mult), "VD%d" % s)
                    each(vd)

                    def oc(s, b):
                        dve.wait_ge(dn_p.sem, dn_p.at("O%d" % s, l, i))
                        dve.wait_ge(dn_a.sem, dn_a.at("sq%d" % s, l, i - 1))
                        odn.inc(CP(osb[s].rearrange("p g v -> p (g v)"), ps[:, b + 2, 0:256]), "oc%d" % s)
                    each(oc)
                    for d in range(2):
                        def oa(s, b):
                            w4(s, ("oc%d", "oa%d")[d])
                            odn.inc(STT(osb[s][:, 1], ps[:, b, 256 + d * P:256 + (d + 1) * P], hc[s][:, 2, d, 1:2], osb[s][:, 1],
                                        ALU.mult, ALU.add), ("oa%d", "ob%d")[d] % s)
                        each(oa)

                    def msq(s, b):
                        dve.wait_ge(dn_a.sem, dn_a.at("sq%d" % s, l, i))
                        odn.inc(TS(oss[s], oss[s], 1.0 / P, EPS, ALU.mult, ALU.add), "ms%d" % s)
                    each(msq)

                    def y_(s, b):
                        dve.wait_ge(dn_g.sem, dn_g.at("rs%d" % s, l, i))
                        own(nl_v, "z", l)
                        for g in range(G):
                            zz = tok[:, g, bass.ds(i * 256 + (T_Z + P * s), P)]
                            odn.inc(STT(zz, osb[s][:, g], ors[s][:, g:g + 1], zz, ALU.mult, ALU.mult), "y%d" % s)
                    each(y_)
                own(dn_v, "y1", l, 3)
                dve.wait_ge(dn_p.sem, dn_p.at("SF1", l, 3))
                for s in range(2):
                    dve.wait_ge(s_state[s], 64 * (l + 1))
                xs = tok[:, 1, 0:1280].rearrange("p (h f x r) -> p h f x r", h=10, f=2, x=2)
                x1, x2 = xs[:, :, :, 0], xs[:, :, :, 1]
                cos, sin = (con[:, K_ROPE + 64 * j:K_ROPE + 64 * j + 64].rearrange("p (o f r) -> p o f r", o=1, f=2)
                            .to_broadcast([P, 10, 2, 32]) for j in range(2))
                for j, (a, b) in enumerate(((x1, cos), (x2, sin), (x2, cos), (x1, sin))):
                    orp.inc(TT(rope_t[j], a, b, ALU.mult), "m%d" % j)
                own(rp_v, "m3", l)
                orp.inc(TT(x1, rope_t[0], rope_t[1], ALU.subtract), "x1")
                orp.inc(TT(x2, rope_t[2], rope_t[3], ALU.add), "x2")
                with dve.Fori(0, 4) as i:
                    for s in range(2):
                        dve.wait_ge(at_p.sem, at_p.at("sc%d" % s, l, i))
                        dve.wait_ge(at_a.sem, at_a.at("P%d" % s, l, i - 1))
                        for g in range(G):
                            oat.inc(dve.tensor_reduce(am[s][0][:, g:g + 1], ps[:, 4 * s + 1, g * P:(1 + 2 * g) * P], AX_X, ALU.max),
                                    "mx%d" % s)
                    for s in range(2):
                        own(at_v, "mx%d" % s, l, i)
                        oat.inc(TS(am[s][1], am[s][0], sinkb[:, bass.ds(i + 4 * s, 1)], None, ALU.max), "mm%d" % s)
                    for s in range(2):
                        own(at_v, "mm%d" % s, l, i)
                        oat.inc(TS(am[s][2], am[s][1], -1.0, None, ALU.mult), "nm%d" % s)
                    for s in range(2):
                        own(at_v, "nm%d" % s, l, i)
                        dve.wait_ge(at_a.sem, at_a.at("se%d" % s, l, i - 1))
                        oat.inc(TS(am[s][4], am[s][2], sinkb[:, bass.ds(i + 4 * s, 1)], None, ALU.add), "sd%d" % s)
                    for s in range(2):
                        dve.wait_ge(at_a.sem, at_a.at("se%d" % s, l, i))
                        oat.inc(TT(am[s][5], am[s][5], am[s][3], ALU.add), "dn%d" % s)
                    for s in range(2):
                        own(at_v, "dn%d" % s, l, i)
                        oat.inc(dve.reciprocal(am[s][6], am[s][5]), "rc%d" % s)
                    for s in range(2):
                        own(at_v, "rc%d" % s, l, i)
                        dve.wait_ge(at_p.sem, at_p.at("pv%d" % s, l, i))
                        for g in range(G):
                            oat.inc(TS(tok[:, g, bass.ds(i * P + 4 * P * s, P)], ps[:, 4 * s + 3, g * P:(g + 1) * P],
                                       am[s][6][:, g:g + 1], None, ALU.mult), "o%d" % s)
                for j in range(8):
                    b, g, h = j // 4, j // 2 % 2, j % 2
                    dve.wait_ge(out_a.sem, out_a.at("ev%d" % j, l))
                    oout.inc(rest((hT, bT)[b], h, g, j), "lv%d" % j)
                dve.wait_ge(nl_a.sem, nl_a.at("sig", l))
                for j in range(3):
                    low(dve, u_out[l] + j)
                for b, c0 in enumerate((T_GA, T_GB)):
                    for n in range(2):
                        for j in range(2):
                            low(dve, u_out[l] + 4 * b + 2 * n + 3 + j)
                        wait_used(dve, u_out[l] + 4 * b + 2 * n + 1)
                        for g in range(G):
                            x = tok[:, g, c0 + 512 * n:c0 + 512 * n + 512]
                            oout.inc(TT(x, x, ps[:, 4 * b + 2 * n + g, :], ALU.mult), ("ga", "gb")[b])
                own(out_v, "gb", l)
                for g in range(G):
                    x = tok[:, g, T_GA:T_GA + D]
                    oout.inc(TT(x, x, tok[:, g, T_GB:T_GB + D], ALU.add), "m")
                for j in range(4):
                    dve.wait_ge(out_a.sem, out_a.at("me%d" % j, l))
                    oout.inc(rest(hT, j % 2, j // 2, j), "ml%d" % j)
                low(dve, u_out[l] + 11)
                wait_used(dve, u_out[l] + U_OUT - 1)
                for g in range(G):
                    oout.inc(CP(y_sb[:, g, :], ps[:, 4 + 2 * g:6 + 2 * g, :].rearrange("p b c -> p (b c)")), "y")
                resid(l, 0)
                own(res_v, "x", l, 0)
                norm_(l, 1)
                if l == 0:
                    def hidden(s, f, first=False):
                        dve.wait_ge(ff_a.sem, ff_a.at("si", 0, f))
                        for g in range(G):
                            off.inc(TT(f_hid[s][:, 256 * g:256 * g + 256], f_hs[0][:, 256 * g:256 * g + 256], ps[:, g, 256:512], ALU.mult), "mu")
                    dve.wait_ge(s_out, 32 * (l + 1))

                    def hl(f, s):
                        dve.wait_ge(ff_h.sem, ff_h.at("he", 0, f))
                        ofl.inc(TT(fT[:, s, 1].rearrange("p a b -> p (a b)"), ps[:, 2 + s, :],
                                   fT[:, s, 0].rearrange("p a b -> p (a b)").bitcast(F32), ALU.subtract), "hl")

                    low(dve, u_ff)
                    low(dve, u_ff + 1)
                    low(dve, u_ff + 2)
                    hidden(0, 0)
                    low(dve, u_ff + 3)
                    low(dve, u_ff + 4)
                    hl(0, 0)
                    hidden(1, 1)
                    with dve.Fori(0, (FF_STEPS - 3) // 4) as i:
                        for j in range(4):
                            for x in range(3):
                                low(dve, u_ff + 5 + 3 * j + x, i)
                            hl(i * 4 + (1 + j), (1 + j) % 2)
                            hidden(j % 2, i * 4 + (2 + j))
                    for x in range(3):
                        low(dve, u_ff + 29 + x)
                    hl(FF_STEPS - 2, 1)
                    hidden(0, FF_STEPS - 1)
                    low(dve, u_ff + 32)
                    hl(FF_STEPS - 1, 0)
                    wait_used(dve, u_ff + U_FF - 1)
                    for g in range(G):
                        ofe.inc(CP(y_sb[:, g, :], ps[:, 4 + 2 * g:6 + 2 * g, :].rearrange("p b c -> p (b c)")), "y")
                else:
                    lg, e1, c1, f1, l2, e2, mk, f2, c2, a1, a2, cmb = rt
                    m1, m2, dd, ex, x1_, rc, w2, _ = rcol
                    pos = cut(tokf, 8220, (24,))
                    dve.wait_ge(rt_p.sem, rt_p.at("lg"))

                    def r(ins, name):
                        ort.inc(ins, name)
                        if rt_v.at(name) == rt_v.per + ort.n or ort.n == 0:
                            own(rt_v, name)

                    def wide(x):
                        return x.to_broadcast([P, G, NEXP])
                    r(CP(lg, ps[:, 0, 0:16].rearrange("p (g e) -> p g e", g=G)), "lg")
                    r(dve.tensor_reduce(m1, lg, AX_X, ALU.max), "m1")
                    r(TT(e1, lg, wide(m1), ALU.is_equal), "e1")
                    for g in range(G):
                        r(dve.tensor_tensor_scan(c1[:, g], con[:, K_ONE:K_ONE + NEXP], e1[:, g], 0.0, ALU.mult, ALU.add), "c1")
                    r(STT(f1, c1, 1.0, e1, ALU.is_equal, ALU.mult), "f1")
                    r(STT(l2, f1, NEG, lg, ALU.mult, ALU.add), "l2")
                    r(dve.tensor_reduce(m2, l2, AX_X, ALU.max), "m2")
                    r(TT(e2, l2, wide(m2), ALU.is_equal), "e2")
                    for g in range(G):
                        r(dve.tensor_tensor_scan(c2[:, g], con[:, K_ONE:K_ONE + NEXP], e2[:, g], 0.0, ALU.mult, ALU.add), "c2")
                    r(STT(f2, c2, 1.0, e2, ALU.is_equal, ALU.mult), "f2")
                    r(TT(mk, f1, f2, ALU.add), "mk")
                    r(TT(dd, m2, m1, ALU.subtract), "d")
                    dve.wait_ge(rt_a.sem, rt_a.at("ex"))
                    r(TS(x1_, ex, 1.0, None, ALU.add), "x1")
                    r(dve.reciprocal(rc, x1_), "rc")
                    r(TT(w2, ex, rc, ALU.mult), "w2")
                    r(TT(a1, f1, wide(rc), ALU.mult), "a1")
                    r(TT(a2, f2, wide(w2), ALU.mult), "a2")
                    r(TT(cmb, a1, a2, ALU.add), "cmb")
                    dve.wait_ge(rt_p.sem, rt_p.at("pos"))
                    r(CP(pos, ps[:, 1, 0:24]), "pos")
                    r(dve.memset(f_acc, 0.0), "acc")

                    ov, cum, ovi, eq = (cut(tokf, 8244 + 8 * j, (NEXP,)) for j in range(4))
                    idf = cut(tokf, 8276, (EXTRA + 1,))
                    seen = cut(tokf, 8280, (1,))
                    r(TS(ov, pos[:, 16:24], P + 0.5, None, ALU.is_gt), "ov")
                    r(dve.tensor_tensor_scan(cum, con[:, K_ONE:K_ONE + NEXP], ov, 0.0, ALU.mult, ALU.add), "cum")
                    r(TT(ovi, ov, con[:, K_IOTA:K_IOTA + NEXP], ALU.mult), "ovi")
                    for j in range(EXTRA):
                        r(STT(eq, cum, float(j + 1), ovi, ALU.is_equal, ALU.mult), "eq%d" % j)
                        r(dve.tensor_reduce(idf[:, j:j + 1], eq, AX_X, ALU.add), "id%d" % j)
                    r(CP(idf[:, EXTRA:EXTRA + 1], cum[:, NEXP - 1:NEXP]), "n")
                    r(CP(over_tab[:, :], idf), "tab")

                    def expert(e, i, u, rr=0, block_=0):
                        dve.wait_ge(moe_p.sem, moe_p.at("ga1", 0, i - 1))
                        for g in range(G):
                            omo.inc(TS(sel[:, g], con[:, K_IOTA + P * block_:K_IOTA + P * (block_ + 1)],
                                       pos[:, bass.ds(e + NEXP * g, 1)], mk.rearrange("p g e -> p (g e)")[:, bass.ds(e + NEXP * g, 1)],
                                       ALU.is_equal, ALU.mult), "sel")
                        own(moe_v, "sel", 0, i)
                        for g in range(G):
                            omo.inc(TS(selc[:, g], sel[:, g], cmb.rearrange("p g e -> p (g e)")[:, bass.ds(e + NEXP * g, 1)], None,
                                       ALU.mult), "selc")
                        dve.wait_ge(moe_p.sem, moe_p.at("sct", 0, i))
                        omo.inc(CP(selT.rearrange("p g t -> p (g t)"), ps[:, 2, 0:256]), "selT")
                        low(dve, u, rr)
                        for h in range(2):
                            dve.wait_ge(moe_a.sem, moe_a.at("ge%d" % h, 0, i))
                            omo.inc(TT(hTe[1][:, 4 * h:4 * h + 4], ps[:, 6 + h, :].rearrange("p (k t) -> p k t", k=4),
                                       hTe[0][:, 4 * h:4 * h + 4].bitcast(F32), ALU.subtract), "gl%d" % h)
                        n = 1
                        for f in range(FB + 1):
                            last = gu_last(f) if f < FB else U_EXP - 3
                            while n <= last + (1 if f else 0):
                                low(dve, u + n, rr)
                                n += 1
                            if f:
                                dve.wait_ge(moe_a.sem, moe_a.at("he%d" % (f - 1), 0, i))
                                omo.inc(TT(fT[:, (f - 1) % 2, 1].rearrange("p a b -> p (a b)"), ps[:, 2 + (f - 1) % 2, :],
                                           fT[:, (f - 1) % 2, 0].rearrange("p a b -> p (a b)").bitcast(F32), ALU.subtract), "hl%d" % (f - 1))
                                low(dve, u + n, rr)
                                n += 1
                            if f < FB:
                                dve.wait_ge(moe_a.sem, moe_a.at("si%d" % f, 0, i))
                                omo.inc(TT(f_hid[f % 2], f_hs[0], ps[:, 1, :], ALU.mult), "mu%d" % f)
                        assert n == U_EXP
                        wait_used(dve, u + U_EXP - 1, rr)
                        omo.inc(CP(ye, ps[:, 4:6, :].rearrange("p b c -> p (b c)")), "ye")
                        for g in range(G):
                            dve.wait_ge(moe_p.sem, moe_p.at("sc%d" % g, 0, i))
                            omo.inc(TT(f_acc[:, g], f_acc[:, g], ps[:, (6, 2)[g]:(6, 2)[g] + 2, :].rearrange("p b c -> p (b c)"), ALU.add), "add")
                        own(moe_v, "add", 0, i)
                        omo.inc(dve.memset(seen, 1.0), "done")

                    with dve.Fori(0, NEXP // 2) as i:
                        for j in range(2):
                            own(moe_v, "done", 0, i * 2 + (j - 1))
                            expert(i * 2 + j, i * 2 + j, u_moe + j * U_EXP, i * (2 * U_EXP // LOOP))
                    own(moe_v, "done", 0, NEXP - 1)

                    def second(e, x):
                        expert(e, NEXP + x, u_moe + (NEXP + x) * U_EXP, 0, 1)
                    second_blocks(dve, second)
                    for g in range(G):
                        ofe.inc(CP(y_sb[:, g, :], f_acc[:, g]), "y")
                resid(l, 1)


_W = ["w_ada", "b_ada", "norm_g", "w_in", "attn_sink", "conv_w", "dn_a_log", "dn_dt_bias", "dn_norm_g", "w_pa", "w_pb",
      "w_o", "w_ff_gate", "w_ff_up", "w_ff_down", "w_router", "w_e_gate", "w_e_up", "w_e_down", "x_prompt", "x_sample",
      "c", "c_ctx"]
_LAYER = {"cache_k%d": "cache_k_l%d", "cache_v%d": "cache_v_l%d", "state%d": "state_delta_l%d"}


def kernel(**inputs):
    import concourse.bacc as _bacc
    from concourse.bass_utils import run_bass_kernel_spmd as _run

    nc = _bacc.Bacc("TRN2", target_bir_lowering=False, num_devices=1)
    arrays, args = {}, {}

    def put(name, a):
        a = np.ascontiguousarray(a)
        arrays["in_" + name] = a
        args[name] = nc.dram_tensor("in_" + name, a.shape, mybir.dt.from_np(a.dtype), kind="ExternalInput").ap()

    for name in _W:
        put(name, inputs[name])
    for ours, theirs in _LAYER.items():
        for l in range(DEPTH):
            put(ours % l, inputs[theirs % l])
    con, lev = constants()
    put("consts", con)
    put("levels", lev)
    outs = []

    def out(name, shape):
        args[name] = nc.dram_tensor("o_" + name, shape, F32, kind="ExternalOutput").ap()
        outs.append("o_" + name)

    out("y_out0", (1, P, D))
    out("y_out1", (1, P, D))
    for l in range(DEPTH):
        out("k_out%d" % l, (1, P, HKV, P))
        out("v_out%d" % l, (1, P, HKV, P))
        out("s_out%d" % l, (1, 2, DH, P, P))
    program(nc, args)
    r = _run(nc, [arrays], core_ids=[0])
    return tuple(r.results[0][n] for n in outs)
```

```python
from contextlib import ExitStack

import numpy as np

import concourse.bass as bass
from concourse import mybir

F32 = mybir.dt.float32
F32R = mybir.dt.float32r
I32 = mybir.dt.int32
ACT = mybir.ActivationFunctionType
ALU = mybir.AluOpType
AX_X = mybir.AxisListType.X

P = 128
G = 2
D = 1024
KC = D // P
DEPTH = 2
HQ, HKV = 8, 2
DH = 8
TAPS = 5
PAD = TAPS // 2
TP = P + 2 * PAD
QKV_CH = 3 * DH
DFF = 2816
NEXP = 8
DEXP = 3584
EPS = 1e-6
IN_W = 7712
C_QKVB, C_Z, C_BA, C_GATES = 1536, 4608, 5632, 5664
COLS = 4608
T_K, T_V, T_Z, T_GA, T_GB = 1024, 1280, 1536, 2560, 3584
UNIT = 2048
RING = 4
WRING = 3
LOOP = 12
LEVELS = 7
LEV_W = (2 * LEVELS - 1) * P
FF_STEPS = DFF // 256
FB = DEXP // 512
EXTRA = 3
NEG = -3.0e38
SCALE = float(P) ** -0.5

K_ID = 0
K_TRI = K_ID + P
K_STR = K_TRI + 2 * P
K_ONE = K_STR + 2 * P
K_ROPE = K_ONE + P
K_IOTA = K_ROPE + 128
K_SEL = K_IOTA + 256
K_ALL = K_SEL + 2 * P
PAIRS = [0, 4, 1, 5, 2, 6, 3, 7, 8, 9, 10, 11]


def constants():
    c = np.zeros((P, K_ALL), np.float32)
    r, k = np.arange(P)[:, None], np.arange(P)[None, :]
    c[:, K_ID:K_ID + P] = r == k
    c[:, K_TRI:K_TRI + P] = r <= k
    c[:, K_TRI + P:K_TRI + 2 * P] = r >= k
    c[:, K_STR:K_STR + P] = r < k
    c[:, K_STR + P:K_STR + 2 * P] = r > k
    c[:, K_ONE:K_ONE + P] = 1.0
    lev = np.zeros((P, LEV_W), np.float32)
    for v in range(LEVELS):
        n = 1 << v
        lev[:, v * P:(v + 1) * P] = -1.0 * ((r // (2 * n) == k // (2 * n)) & (r // n != k // n))
        if v:
            odd = (r // n) % 2 == 1
            lev[:, (LEVELS + v - 1) * P:(LEVELS + v) * P] = np.where(odd, r <= k, r >= k)
    inv = 10000.0 ** (-np.arange(32, dtype=np.float32) / 32)
    ang = np.stack([(np.arange(P) // 64)[:, None] * inv, (np.arange(P) % 64)[:, None] * inv], 1)
    ang = ang.astype(np.float32).reshape(P, 64)
    c[:, K_ROPE:K_ROPE + 64] = np.cos(ang)
    c[:, K_ROPE + 64:K_ROPE + 128] = np.sin(ang)
    c[:, K_IOTA:K_IOTA + 256] = np.arange(256)[None, :]
    for g in range(G):
        c[:, K_SEL + g * P:K_SEL + (g + 1) * P] = (np.arange(P) % 32 == g)[:, None]
    return c, lev


class Steps:

    def __init__(self, sem, iters, names):
        self.sem, self.iters, self.off = sem, iters, {}
        n = 0
        for x in names:
            name, k = x if isinstance(x, tuple) else (x, 1)
            assert name not in self.off
            n += k
            self.off[name] = n
        self.per = n

    def at(self, name, l=0, i=0):
        return i * self.per + ((l * self.iters + 1) * self.per + self.off[name])


class Order:

    def __init__(self, steps):
        self.s, self.n = steps, 0

    def inc(self, ins, name):
        self.n += 1
        lo = 0
        for k, v in self.s.off.items():
            if lo < self.n <= v:
                assert k == name, (k, name)
            lo = v
        ins.then_inc(self.s.sem, 1)
        if self.n == self.s.per:
            self.n = 0


def program(nc, A):
    ctx = ExitStack()
    with ctx:
        def sb(name, shape, dt=F32):
            return ctx.enter_context(nc.sbuf_tensor(name, shape, dt))

        def sem(name):
            return ctx.enter_context(nc.semaphore(name))

        def steps(name, iters, names):
            return Steps(sem(name), iters, names)

        ring = sb("ring", [P, RING, UNIT])
        con = sb("con", [P, K_ALL])
        xt = sb("xt", [P, G, D])
        hreg = sb("hreg", [P, G * D])
        mod_hi = [None, None]
        with nc.sbuf_tensor("tok_pad", [P, 1536], F32), nc.sbuf_tensor("mod_hi1", [P, D], F32R) as mod_hi[1]:
            pass
        tok = sb("tok", [P, G, COLS])
        with nc.sbuf_tensor("mod_lo", [P, 2, D], F32R) as mod_lo:
            pass
        mod = sb("mod", [P, 2, D])
        cache_k = sb("cache_k", [P, HKV, P])
        cache_v = sb("cache_v", [P, HKV, P])
        small = sb("small", [P, 1024])
        wba = sb("wba", [P, KC, 32])
        ps = ctx.enter_context(nc.psum_tensor("ps", [P, 8, 512], F32))
        with nc.sbuf_tensor("bT", [P, 2, KC, G * P], F32R) as bT:
            pass
        with nc.sbuf_tensor("qreg_pad", [P, 4096], F32), nc.sbuf_tensor("mod_hi0", [P, D], F32R) as mod_hi[0]:
            pass
        qreg = sb("qreg", [P, QKV_CH * G * TP])
        turn_ = ExitStack()
        wsp = turn_.enter_context(nc.sbuf_tensor("wsp", [P, WRING, 2, UNIT], F32R))
        hT = turn_.enter_context(nc.sbuf_tensor("hT", [P, 2, KC, G * P], F32R))
        fT = turn_.enter_context(nc.sbuf_tensor("fT", [P, 2, 2, 4, P], F32R))
        turn_.close()
        dnx = sb("dnx", [P, WRING * 2 * UNIT + 2 * 2048 + 2048])

        def cut(t, at, shape):
            n = 1
            for k in shape:
                n *= k
            flat = t[:, at:at + n]
            names = "abcd"[:len(shape)]
            if len(shape) == 1:
                return flat
            return flat.rearrange("p (%s) -> p %s" % (" ".join(names), " ".join(names)),
                                  **{names[j]: shape[j] for j in range(len(shape))})

        ident = con[:, K_ID:K_ID + P]
        ones = con[:, K_ONE:K_ONE + P]

        def tri(d):
            return con[:, K_TRI + d * P:K_TRI + (d + 1) * P]

        def two(t):
            return t.rearrange("p (d o k) -> p d o k", d=2, o=1).to_broadcast([P, 2, G, P])

        h_tok = cut(hreg, 0, (G, D))
        qkv = cut(qreg, 0, (QKV_CH, G, TP))

        at = [0]

        def slot(shape):
            n = int(np.prod(shape))
            r = [cut(dnx, at[0] + n * s, shape) for s in range(2)]
            at[0] += 2 * n
            return r

        kqv = slot((3, G, P))
        XX = slot((2, 2, G, P))
        ktv = slot((3, P))
        ET = slot((2, G, P))
        attn = slot((2, G, P))
        AT = slot((2, G, P))
        SS = slot((2, G, P))
        MM = slot((2, G, P))
        RP = slot((2, P))
        VN = slot((2, G, P))
        VD = slot((2, P))
        osb = slot((G, P))
        sfo = slot((2, P))
        junk = slot((G, P))
        s0 = cut(dnx, at[0], (DH, 2, P))
        lev = cut(dnx, at[0] + 2048, (LEV_W,))
        assert at[0] + 2048 + LEV_W <= dnx.shape[1]
        acc = [cut(hreg, 256 * s, (G, P)) for s in range(2)]
        l2s = [cut(hreg, 512 + 512 * s, (2, G, P)) for s in range(2)]
        l2c = cut(hreg, 1536, (8,))
        at[0] = 0
        qst = [wba[:, :, :].rearrange("p k c -> p (k c)").rearrange("p (g t) -> p g t", g=G), cut(hreg, 1792, (G, P))]
        qT = slot((G, P))
        pr = slot((3, P))
        prT = slot((3, P))
        kTb = cut(hreg, 1024, (HKV, 3, P))
        rope_t = [cut(hreg, 1024 + 256 * j, (4, 2, 32)) for j in range(4)]
        ROPE = [(0, 4), (4, 8), (8, 10)]
        y_sb = cut(qreg, 4096, (G, D))
        ngr = cut(qreg, 0, (2, D))
        ngh = cut(hreg, 0, (D,))
        sqj = cut(hreg, 0, (D,))
        tokf = tok[:, :, :].rearrange("p g c -> p (g c)")
        f_hs = [cut(tokf, 0, (512,))]
        f_hid = [cut(tokf, 512 + 512 * s, (512,)) for s in range(2)]
        sel = cut(tokf, 4096, (G, P))
        selc = cut(tokf, 4352, (G, P))
        selT = [cut(tokf, 2560 + 256 * s, (G, P)) for s in range(2)]
        ye = cut(tokf, 4864, (D,))
        f_acc = cut(tokf, 5888, (G, D))
        sm = [0]

        def col(n):
            sm[0] += n
            assert sm[0] <= 1024
            return small[:, sm[0] - n:sm[0]]

        condT = col(2 * KC).rearrange("p (k c) -> p k c", c=2)
        ss, ms, rstd = col(2), col(2), col(2)
        mhalf = col(16)
        ba = col(64).rearrange("p (g c) -> p g c", g=G)
        eb = col(32).rearrange("p (g c) -> p g c", g=G)
        ga = [col(32).rearrange("p (g c) -> p g c", g=G) for _ in range(5)]
        dtb, alog, ealog = col(16), col(16), col(16)
        gcs, gex = col(64), col(64)
        GT = col(192).rearrange("p (h q d g) -> p h q d g", h=DH, q=6, d=2)
        cw = col(128)
        hc = [col(24).rearrange("p (q d g) -> p q d g", q=6, d=2) for _ in range(2)]
        oss = [col(2) for _ in range(2)]
        ors = [col(2) for _ in range(2)]
        sinkb = col(8)
        am = [[col(2) for _ in range(7)] for _ in range(2)]
        cwr = sb("cwr", [P, P])
        dng = sb("dng", [P, P])
        cond = hreg[0:2, 0:D]
        condS = hreg[0:2, D:2 * D]
        condR = [hT[:, x].rearrange("p a b -> p (a b)")[:, 0:KC * P].rearrange("p (k m) -> p k m", k=KC) for x in range(2)]
        hTe = [[hT[:, x].rearrange("p a b -> p (a b)")[:, s * D:(s + 1) * D].rearrange("p (k m) -> p k m", k=KC) for x in range(2)]
               for s in range(2)]
        wr = sb("wr", [P, KC, NEXP])
        selR = sb("selR", [P, 2 * P], F32R)
        over_tab = sb("over_tab", [P, EXTRA + 1], I32)
        rt = [cut(tokf, 8000 + 16 * j, (G, NEXP)) for j in range(12)]
        rcol = [cut(tokf, 8192 + 2 * j, (G, 1)) for j in range(8)]

        ready = [sem("unit_ready%d" % j) for j in range(RING)]
        unit_used = sem("unit_used")
        unit_hi = sem("unit_high")
        unit_lo = sem("unit_low")
        s_cond = sem("conditions_in")
        s_in = sem("inputs_in")
        s_out = sem("outputs_out")
        s_state = [sem("state_out%d" % s) for s in range(2)]
        s_mod = sem("first_bias_in")
        s_lay = sem("layer_small_in")
        MOD_DMAS, LAY_DMAS = 3, 12
        s_gain = sem("gains_in")
        s_lev = sem("levels_in")
        s_st = sem("states_in")
        init_a = steps("init_act", 1, ["cond", "sel"])
        init_p = steps("init_pe", 1, ["condT"])
        clr_v = steps("mod_cleared", 1, ["mod"])
        init_v = steps("init_dve", 1, ["half", "condT"])
        lay_g = steps("layer_pool", 1, [("pads", 2)])
        cnd_a = steps("cond_act", 1, ["hi"])
        cnd_v = steps("cond_dve", 1, ["lo"])
        ada_v = steps("ada_dve", 1, [("row", 4), "mod"])
        adb_v = steps("adb_dve", 4, ["r%d" % q for q in range(4)])
        adm_v = steps("gains_dve", 1, [("mod", 3)])
        rms_a = steps("rms_act", 4, [("ss", 2)])
        rms_v = steps("rms_dve", 4, ["ms"])
        rms_g = steps("rms_pool", 4, ["rstd"])
        nrm_p = steps("norm_pe", 2, ["bc0", "bc1", "t00", "t01", "t10", "t11"])
        nrm_v = steps("norm_dve", 2, ["a0", "h0", "a1", "h1", "l00", "l01", "l10", "l11"])
        nrm_a = steps("norm_act", 2, ["e00", "e01", "e10", "e11"])
        evac = steps("proj_evac", 1, ["b%d" % j for j in range(12)] + ["t%d" % j for j in range(9)])
        gat_p = steps("gates_pe", 1, ["ba", "cw", "gc"])
        gat_v = steps("gates_dve", 1, ["cw", "ba", "a", "na", "e1", "sp", "g0", "gcol", "gcs", "kd",
                                       "gc", "egc", "negc", "ekd", "b1", "rb", "beta"])
        gat_a = steps("gates_act", 1, ["eb", "ea", "el", "ln", ("ex", 2)])
        cnv_v = steps("conv_dve", QKV_CH // 2, ["t%d%d" % (j, s) for j in range(TAPS) for s in range(2)])
        cnv_a = steps("conv_act", QKV_CH // 2, ["s0", "s1"])
        nl_a = steps("gate_act", 1, ["sig"])
        nl_v = steps("gate_dve", 1, ["z"])
        l2_g = steps("l2_pool", 4, ["sq0", "sq1", "pw"])
        l2_p = steps("l2_pe", 4, ["ss", "bc0", "bc1"])
        l2_v = steps("l2_dve", 4, ["ep", "nm0", "nm1"])

        def both(names):
            return [(x[0] % s, x[1]) if isinstance(x, tuple) else x % s for x in names for s in range(2)]

        lv = range(1, LEVELS)
        dn_g = steps("dn_pool", 4, both(["Et2_%d", "EM%d"]) + [x for v in range(3, LEVELS) for x in both(["Et%d_%%d" % v])]
                     + both(["rs%d"]))
        dq_g = steps("dn_in_pool", 4, both(["kqv%d", "hc%d"]))
        dn_p = steps("dn_pe", 4, both(["tr%d", "G%d", "gr%d", "m%d"])
                     + [x for v in lv for x in both(["a%d_%%d" % v, "b%d_%%d" % v])]
                     + both(["kS%d", "V%d", "O%d", "SF%d"]))
        dn_v = steps("dn_dve", 4, both([("t%d", 4), "W%d", ("A%d", 4), "B%d", "S%d", "I%d", ("E1_%d", 2), "at%d"])
                     + [x for v in lv for x in both(["T%d_%%d" % v])
                        + [y % (v + z, s) for s in range(2) for z, y in ((0, "D%d_%d"), (1, "E%d_%d"), (0, "F%d_%d"))
                           if y[0] != "F" or v < LEVELS - 1]]
                     + both([("R%d", 2), ("VD%d", 2), "oc%d", "oa%d", "ob%d", "ms%d", ("y%d", 2)]))
        dn_a = steps("dn_act", 4, both(["tok%d", "ET%d", "X%d"])
                     + both([("VN%d", 4), "Sf%d", ("sq%d", 2)]))
        rp_v = steps("rope_dve", 3, ["m0", "m1", "m2", "m3", "x1", "x2"])
        kt_p = steps("keys_pe", 1, ["k"])
        kt_a = steps("keys_act", 1, ["k", "o"])
        at_g = steps("attn_pool", 4, both(["q%d"]))
        at_p = steps("attn_pe", 4, both(["qt%d", "sc%d", "pt%d", "pv%d"]))
        at_v = steps("attn_dve", 4, both([("mx%d", 2), "mm%d", "nm%d", "sd%d", "dn%d", "rc%d", ("o%d", 2)]))
        at_a = steps("attn_act", 4, both(["qe%d", ("P%d", 2), "se%d", "pe%d"]))
        out_p = steps("out_pe", 1, ["tr%d" % j for j in range(8)] + ["mt%d" % j for j in range(4)])
        out_a = steps("out_act", 1, ["ev%d" % j for j in range(8)] + ["me%d" % j for j in range(4)])
        out_v = steps("out_dve", 1, ["lv%d" % j for j in range(8)] + [("ga", 4), ("gb0", 2), ("m0", 2), ("gb1", 2), ("m1", 2)] + ["ml%d" % j for j in range(4)] + [("y", 2)])
        res_p = steps("resid_pe", 2, ["gb"])
        res_v = steps("resid_dve", 2, [("t", 2), ("x", 2)])
        ff_a = steps("ff_act", FF_STEPS, [("si", 2)])
        ff_h = steps("ff_hidden", FF_STEPS, ["he"])
        ff_v = steps("ff_dve", FF_STEPS, [("mu", 2)])
        ff_l = steps("ff_low", FF_STEPS, ["hl"])
        ff_p = steps("ff_pe", FF_STEPS, ["ht"])
        ffe_v = steps("ff_end", 1, [("y", 2)])
        rt_p = steps("router_pe", 1, ["lg", "pos"])
        rt_v = steps("router_dve", 1, ["lg", "m1", "e1", ("c1", 2), "f1", "l2", "m2", "e2", ("c2", 2), "f2",
                                       "mk", "d", "x1", "rc", "w2", "a1", "a2", "cmb", "pos", "acc",
                                       "ov", "cum", "ovi"] + [x % j for j in range(EXTRA) for x in ("eq%d", "id%d")]
                     + ["n", "tab"])
        rt_a = steps("router_act", 1, ["ex"])
        N = NEXP + EXTRA
        moe_v = steps("moe_dve", N, ["mu0"] + [x for f in range(1, FB) for x in ("hl%d" % (f - 1), "mu%d" % f)] + ["hl%d" % (FB - 1)])
        moe_a = steps("moe_act", N, ["si0"] + [x for f in range(1, FB) for x in ("he%d" % (f - 1), "si%d" % f)] + ["he%d" % (FB - 1)])
        moe_p = steps("moe_pe", N, ["ht%d" % f for f in range(FB)])
        pre_v = steps("fetch_dve", N, [("sel", 2), ("selc", 2), "selT", "gl0", "gl1"])
        pre_a = steps("fetch_act", N, ["ge0", "ge1"])
        pre_p = steps("fetch_pe", N, ["sct", "ga0", "ga1"])
        post_v = steps("back_dve", N, ["ye", "add0", "add1", "done"])
        post_p = steps("back_pe", N, ["sc0", "sc1"])

        mdh_a = steps("mod_high", 2, ["h"])
        mdl_v = steps("mod_low", 2, ["l"])
        V_STEPS = [init_v, cnd_v, ada_v, rms_v, nrm_v, gat_v, cnv_v, nl_v, l2_v, dn_v, rp_v, at_v, out_v, res_v,
                   ff_v, ff_l, ffe_v, rt_v, moe_v, pre_v, post_v, adb_v, adm_v, mdl_v, clr_v]
        A_STEPS = [init_a, cnd_a, rms_a, nrm_a, evac, gat_a, cnv_a, nl_a, dn_a, kt_a, at_a, out_a, ff_a, ff_h, rt_a, moe_a, pre_a, mdh_a]
        P_STEPS = [init_p, nrm_p, gat_p, l2_p, dn_p, kt_p, at_p, out_p, res_p, ff_p, rt_p, moe_p, pre_p, post_p]
        G_STEPS = [lay_g, rms_g, l2_g, dn_g, at_g, dq_g]

        U_ADA, U_PROJ, U_ADB, U_OUT, U_FF, U_EXP = 8, 30, 16, 12, 3 * FF_STEPS, 6 * FB
        u_ada = [0, U_ADA + U_PROJ + U_ADB + U_OUT + U_FF]
        u_proj = [u + U_ADA for u in u_ada]
        u_adb = [u + U_PROJ for u in u_proj]
        u_out = [u + U_ADB for u in u_adb]
        u_ff = u_out[0] + U_OUT
        u_moe = u_out[1] + U_OUT

        def unit(u):
            return ring[:, u % RING, :]

        def sp_(u):
            return u - U_ADB * sum(u >= a + U_ADB for a in u_adb)

        def part(u, x):
            return wsp[:, sp_(u) % WRING, x, :]

        def wait_used(eng, u, i=0):
            eng.wait_ge(unit_used, i * LOOP + (sp_(u) + 1 + WRING))

        def wait_in(eng, u, i=0, per=LOOP):
            eng.wait_ge(ready[u % RING], i * (16 * per // RING) + (16 * (u // RING) + 16))

        def high(act, u, i=0):
            wait_in(act, u, i)
            act.wait_ge(unit_used, i * LOOP + (sp_(u) + 1))
            act.activation(part(u, 0), unit(u), ACT.Copy).then_inc(unit_hi, 1)

        def low(dve, u, i=0):
            dve.wait_ge(unit_hi, i * LOOP + (sp_(u) + 1))
            dve.tensor_tensor(part(u, 1), unit(u), part(u, 0).bitcast(F32), ALU.subtract).then_inc(unit_lo, 1)

        def wait_hi(pe, u, i=0):
            pe.wait_ge(unit_hi, i * LOOP + (sp_(u) + 1))

        def wait_lo(eng, u, i=0, per=LOOP):
            eng.wait_ge(unit_lo, i * per + (u + 1 + RING))

        def mod_row(q, c, n):
            return mod[32 * q:32 * q + 2, c, 512 * n:512 * n + 512]

        def gu(f):
            return 6 * f - 2 if f else 0

        def experts(eng, fetch, body, back):
            def at_(i, j, u, r, prev=True, next_=True):
                def hook(f):
                    if prev and f in (0, 1, 2, 3):
                        back(i - 1 if isinstance(i, int) else i + (-1), 1 - j, f)
                    if next_ and f in (2, 3, 4, 5):
                        fetch(i + 1, i + 1, 1 - j, f)
                body(i, j, u, r, hook)
            for f in (2, 3, 4, 5):
                fetch(0, 0, 0, f)
            at_(0, 0, u_moe, 0, prev=False)
            with eng.Fori(0, NEXP // 2 - 1) as i:
                for j in (1, 2):
                    at_(i * 2 + j, j % 2, u_moe + j * U_EXP, i * (2 * U_EXP // LOOP))
            at_(NEXP - 1, 1, u_moe + (NEXP - 1) * U_EXP, 0, next_=False)
            for f in (0, 1, 2, 3):
                back(NEXP - 1, 1, f)

            def second(e, x):
                i = NEXP + x
                for f in (2, 3, 4, 5):
                    fetch(i, e, x % 2, f, 1)
                body(i, x % 2, u_moe + i * U_EXP, 0, lambda f: None)
                for f in (0, 1, 2, 3):
                    back(i, x % 2, f)
            second_blocks(eng, second)

        def second_blocks(eng, body):
            eng.wait_ge(rt_v.sem, rt_v.at("tab"))
            n = eng.value_load(over_tab[0:1, EXTRA:EXTRA + 1], min_val=0, max_val=EXTRA)
            for x in range(EXTRA):
                with eng.If(n > x):
                    e = eng.value_load(over_tab[0:1, x:x + 1], min_val=0, max_val=NEXP - 1)
                    body(e, x)

        MODS = [(0, 0), (1, 0), (0, 1), (1, 1), (2, 1), (3, 1)]
        GAIN = {1: 0, 2: 1, 4: 2, 5: 3}

        def y_ps(g):
            return ps[:, 4 + 2 * g:6 + 2 * g, :].rearrange("p b c -> p (b c)")

        x_in = [A["x_prompt"], A["x_sample"]]
        block = ctx.enter_context(nc.Block())

        @block.sync
        def _(sp):
            def load(u, src, dst=None, i=0, per=LOOP):
                wait_lo(sp, u - RING, i, per)
                d = unit(u) if dst is None else dst
                sp.dma_start(d, src).then_inc(ready[u % RING], 16)

            def rows(u, w, k0, c0, i=0, kn=4, cn=512, per=LOOP):
                src = w[k0:k0 + kn, :, bass.ds(c0, cn)].rearrange("k p n -> p k n")
                load(u, src, unit(u)[:, 0:kn * cn].rearrange("p (k n) -> p k n", k=kn), i, per)

            sp.sem_inc(unit_used, WRING)
            sp.sem_inc(unit_lo, RING)
            sp.dma_start(cond[0:1, :], A["c_ctx"].rearrange("(a n) -> a n", a=1)).then_inc(s_cond, 16)
            sp.dma_start(cond[1:2, :], A["c"]).then_inc(s_cond, 16)
            sp.dma_start(con[:, :], A["consts"]).then_inc(s_cond, 16)
            for l in range(DEPTH):
                wa = A["w_ada"][l].rearrange("(k p) n -> k p n", p=P)
                for j in range(U_ADA // 2):
                    for h in range(2):
                        rows(u_ada[l] + 2 * j + h, wa, 4 * h, 512 * j)
                w = A["w_in"][l].rearrange("(k p) n -> k p n", p=P)
                for j, pr_ in enumerate(PAIRS):
                    rows(u_proj[l] + j, w, 0, C_QKVB + 256 * pr_, 0, 8, 256)
                cols = [512 * j for j in range(3)] + [C_Z, C_Z + 512] + [C_GATES + 512 * j for j in range(4)]
                for j, c in enumerate(cols):
                    for h in range(2):
                        rows(u_proj[l] + 12 + 2 * j + h, w, 4 * h, c)
                with sp.Fori(0, 4) as i:
                    for q in range(4):
                        rows(u_adb[l] + q, wa, 0, i * 256 + (2 + q) * D, i, KC, 256, 4)
                u = u_out[l]
                for name in ("w_pa", "w_pb", "w_o"):
                    w = A[name][l].rearrange("(k p) n -> k p n", p=P)
                    for n in range(2):
                        for h in range(2):
                            rows(u, w, 4 * h, 512 * n)
                            u += 1
                if l == 0:
                    wg, wu = (A[n][0].rearrange("(k p) n -> k p n", p=P) for n in ("w_ff_gate", "w_ff_up"))
                    wd = A["w_ff_down"][0].rearrange("(f k p) n -> f p k n", p=P, k=2)

                    def ff_gu(u, f, i=0):
                        rows(u, wg, 0, f * 256, i, 8, 256)
                        rows(u + 1, wu, 0, f * 256, i, 8, 256)

                    def ff_d(u, f, i=0):
                        load(u, wd[bass.ds(f, 1)].rearrange("f p k n -> p (f k) n"),
                             unit(u).rearrange("p (k n) -> p k n", k=2), i)

                    ff_gu(u_ff, 0)
                    ff_gu(u_ff + 2, 1)
                    ff_d(u_ff + 4, 0)
                    with sp.Fori(0, (FF_STEPS - 3) // 4) as i:
                        for j in range(4):
                            ff_gu(u_ff + 5 + 3 * j, i * 4 + (2 + j), i)
                            ff_d(u_ff + 7 + 3 * j, i * 4 + (1 + j), i)
                    u = u_ff + 3 * FF_STEPS - 4
                    ff_gu(u, FF_STEPS - 1)
                    ff_d(u + 2, FF_STEPS - 2)
                    ff_d(u + 3, FF_STEPS - 1)
                else:
                    def expert(e, u, i=0):
                        we = [A[n][0, bass.ds(e, 1)].rearrange("e (k p) n -> (e k) p n", p=P)
                              for n in ("w_e_gate", "w_e_up")]
                        wd = A["w_e_down"][0, bass.ds(e, 1)].rearrange("e (f k p) n -> (e f) p k n", p=P, k=2)
                        for f in range(FB + 1):
                            if f < FB:
                                for w in we:
                                    for h in range(2):
                                        rows(u, w, 4 * h, 512 * f, i)
                                        u += 1
                            if f > 0:
                                for h in range(2):
                                    load(u, wd[2 * (f - 1) + h], unit(u).rearrange("p (k n) -> p k n", k=2), i)
                                    u += 1

                    with sp.Fori(0, NEXP // 2) as i:
                        for j in range(2):
                            expert(i * 2 + j, u_moe + j * U_EXP, i * (2 * U_EXP // LOOP))
                    second_blocks(sp, lambda e, x: expert(e, u_moe + (NEXP + x) * U_EXP))

        @block.gpsimd
        def _(pool):
            for s in G_STEPS:
                pool.sem_inc(s.sem, s.per)
            D0 = pool.dma_start
            for g in range(G):
                D0(xt[:, g, :], x_in[g][0]).then_inc(s_in, 16)

            D0(wr[:, :, :], A["w_router"][0].rearrange("(k p) e -> p k e", p=P)).then_inc(s_in, 16)

            def bc(row, n):
                return row.rearrange("(a n) -> a n", a=1).to_broadcast([n, row.shape[0]])

            def rstd_(l, k):
                pool.wait_ge(rms_v.sem, rms_v.at("ms", l, k))
                pool.wait_ge(init_v.sem, init_v.at("half"))
                rg.inc(pool.tensor_tensor(rstd[:, :], ms[:, :], mhalf[:, 0:2], ALU.pow), "rstd")

            lg, rg, l2g, dg, ag, dqg = (Order(s) for s in G_STEPS)
            for l in range(DEPTH):
                if l:
                    pool.wait_ge(res_v.sem, res_v.at("x", 0, 1))
                pool.wait_ge(clr_v.sem, clr_v.at("mod", l))
                for m, (q, c) in enumerate(MODS[:2]):
                    pool.dma_start(mod[32 * q:32 * q + 2, c, :], bc(A["b_ada"][l, m * D:(m + 1) * D], 2)).then_inc(s_mod, 16)
                pool.dma_start(ngr[32:34, 0, :], bc(A["norm_g"][l, GAIN[1]], 2)).then_inc(s_mod, 16)
                for m in range(2, 6):
                    q, c = MODS[m]
                    pool.dma_start(mod[32 * q:32 * q + 2, c, :], bc(A["b_ada"][l, m * D:(m + 1) * D], 2)).then_inc(s_lay, 16)
                pool.dma_start(wba[:, :, :], A["w_in"][l, :, C_BA:C_BA + 32].rearrange("(k p) n -> p k n", p=P)).then_inc(s_lay, 16)
                pool.dma_start(cwr[0:TAPS * QKV_CH, :], A["conv_w"][l].rearrange("j (c p) -> (j c) p", p=P)).then_inc(s_lay, 16)
                pool.dma_start(dtb, bc(A["dn_dt_bias"][l].rearrange("d h -> (d h)"), P)).then_inc(s_lay, 16)
                pool.dma_start(alog, bc(A["dn_a_log"][l].rearrange("d h -> (d h)"), P)).then_inc(s_lay, 16)
                pool.dma_start(dng[:, :], bc(A["dn_norm_g"][l], P)).then_inc(s_lay, 16)
                pool.dma_start(sinkb, bc(A["attn_sink"][l], P)).then_inc(s_lay, 16)
                pool.dma_start(cache_k[:, :, :], A["cache_k%d" % l][0]).then_inc(s_lay, 16)
                pool.dma_start(cache_v[:, :, :], A["cache_v%d" % l][0]).then_inc(s_lay, 16)
                rstd_(l, 0)
                pool.wait_ge(nrm_p.sem, nrm_p.at("bc1", l, 0))
                lg.inc(pool.memset(qkv[:, :, :, 0:PAD], 0.0), "pads")
                lg.inc(pool.memset(qkv[:, :, :, PAD + P:TP], 0.0), "pads")
                for i in range(4):
                    pool.wait_ge(cnv_a.sem, cnv_a.at("s1", l, 2 * i + 1))
                    pool.wait_ge(l2_p.sem, l2_p.at("ss", l, i - 1))
                    for s in range(2):
                        x = qkv[:, 2 * i + 8 * s:2 * i + 8 * s + 2, :, PAD:PAD + P]
                        l2g.inc(pool.tensor_tensor(l2s[s], x, x, ALU.mult), "sq%d" % s)
                    pool.wait_ge(l2_v.sem, l2_v.at("ep", l, i))
                    l2g.inc(pool.tensor_tensor(l2c, l2c, mhalf[:, 0:8], ALU.pow), "pw")
                def dn_in(i, i1):
                    for s in range(2):
                        pool.wait_ge(dn_p.sem, dn_p.at("kS%d" % s, l, i1))
                        src = qkv[:, bass.ds(i * 2 + s, 17), :, PAD:PAD + P][:, 0:17:8]
                        dqg.inc(pool.tensor_copy(kqv[s], src), "kqv%d" % s)
                    for s in range(2):
                        pool.wait_ge(dn_v.sem, dn_v.at("ob%d" % s, l, i1))
                        pool.wait_ge(dn_a.sem, dn_a.at("VN%d" % s, l, i1))
                        dqg.inc(pool.tensor_copy(hc[s].rearrange("p q d g -> p (q d g)"),
                                                 GT[:, bass.ds(i * 2 + s, 1)].rearrange("p h q d g -> p (h q d g)")),
                                "hc%d" % s)

                def dn_masks(i):
                    for v in range(2, LEVELS):
                        for s in range(2):
                            pool.wait_ge(dn_v.sem, dn_v.at("F%d_%d" % (v - 1, s), l, i))
                            dg.inc(pool.tensor_tensor(XX[s][:, 0, 1], SS[s][:, 1],
                                                     lev[:, (LEVELS + v - 1) * P:(LEVELS + v) * P].rearrange("p (o k) -> p o k", o=1)
                                                     .to_broadcast([P, G, P]), ALU.mult), "Et%d_%d" % (v, s))
                        if v == 2:
                            attn_masks(i)

                def attn_masks(i):
                    for s in range(2):
                        pool.wait_ge(dn_v.sem, dn_v.at("at%d" % s, l, i))
                        dg.inc(pool.tensor_tensor(attn[s], attn[s], two(con[:, K_TRI:K_TRI + 2 * P]), ALU.mult), "EM%d" % s)

                def dn_end(i):
                    for s in range(2):
                        pool.wait_ge(dn_v.sem, dn_v.at("ms%d" % s, l, i))
                        dg.inc(pool.tensor_tensor(ors[s], oss[s], mhalf[:, 0:2], ALU.pow), "rs%d" % s)
                        pool.wait_ge(dn_a.sem, dn_a.at("Sf%d" % s, l, i))
                        src = i * 2 + s if isinstance(i, int) else bass.ds(i * 2 + s, 1)
                        src = slice(src, src + 1) if isinstance(i, int) else src
                        pool.dma_start(A["s_out%d" % l][0, :, src].rearrange("d h k v -> k (d h) v"),
                                       sfo[s]).then_inc(s_state[s], 16)

                pool.wait_ge(gat_v.sem, gat_v.at("beta", l))
                pool.wait_ge(l2_v.sem, l2_v.at("nm1", l, 3))
                wait_used(pool, u_proj[l] + U_PROJ - 1)
                dn_in(0, -1)
                pool.dma_start(lev, A["levels"]).then_inc(s_lev, 16)
                for d in range(2):
                    pool.dma_start(s0[:, :, d, :], A["state%d" % l][0, d].rearrange("h k v -> k h v")).then_inc(s_st, 16)
                pool.wait_ge(cnv_a.sem, cnv_a.at("s1", l, QKV_CH // 2 - 1))
                for m in (2, 4, 5):
                    q = MODS[m][0]
                    pool.dma_start(ngh[32 * q:32 * q + 2, :], bc(A["norm_g"][l, GAIN[m]], 2)).then_inc(s_gain, 16)

                with pool.Fori(0, 3) as i:
                    dn_masks(i)
                    dn_in(i + 1, i)
                    dn_end(i)
                dn_masks(3)
                dn_end(3)
                with pool.Fori(0, 4) as i:
                    for s in range(2):
                        if s == 0:
                            pool.wait_ge(rp_v.sem, rp_v.at("x2", l, 2))
                        pool.wait_ge(at_p.sem, at_p.at("qt%d" % s, l, i - 1))
                        ag.inc(pool.tensor_copy(qst[s], tok[:, :, bass.ds(i * P + 4 * P * s, P)]), "q%d" % s)
                pool.wait_ge(evac.sem, evac.at("t2", l))
                for n, c in (("k", T_K), ("v", T_V)):
                    pool.dma_start(A["%s_out%d" % (n, l)][0], tok[:, 0, c:c + 256].rearrange("p (h d) -> p h d", h=HKV))\
                        .then_inc(s_out, 16)
                rstd_(l, 1)
                rstd_(l, 2)
                rstd_(l, 3)
            for s in range(2):
                pool.wait_ge(s_state[s], 16 * 4 * DEPTH)
            pool.wait_ge(res_v.sem, res_v.at("x", 1, 1))
            for g in range(G):
                pool.dma_start(A["y_out%d" % g][0], xt[:, g, :]).then_inc(s_out, 16)
            pool.wait_ge(s_out, 32 * DEPTH + 32)

        @block.scalar
        def _(act):
            for s in A_STEPS:
                act.sem_inc(s.sem, s.per)
            (oi, ocd, orr, onr, oev, oga, ocv, onl, odn, okt, oat, oout, off, ofh, ort, omo, opr, omh) = (Order(s) for s in A_STEPS)
            AC = act.activation
            act.wait_ge(s_cond, 16 * 3)
            oi.inc(AC(condS, cond, ACT.Silu), "cond")
            oi.inc(AC(selR[:, :], con[:, K_SEL:K_SEL + 2 * P], ACT.Copy), "sel")

            def ss_(l, k, src, ready_):
                for g in range(G):
                    ready_(g)
                    if not (g or l or k):
                        act.wait_ge(s_in, 16 * 3)
                        act.wait_ge(init_a.sem, init_a.at("sel"))
                    if g or l or k:
                        act.wait_ge(rms_a.sem, rms_a.at("ss", l, k) - 2 + g)
                    orr.inc(AC(sqj, src(g), ACT.Square, accum_out=ss[:, g:g + 1]), "ss")

            def norm_(l, n):
                for g in range(G):
                    for h in range(2):
                        act.wait_ge(nrm_p.sem, nrm_p.at("t%d%d" % (g, h), l, n))
                        onr.inc(AC(hT[:, 0, 4 * h:4 * h + 4, g * P:(g + 1) * P],
                                   ps[:, 4 * g + h, :].rearrange("p (k t) -> p k t", k=4), ACT.Copy), "e%d%d" % (g, h))

            for l in range(DEPTH):
                act.wait_ge(init_v.sem, init_v.at("condT"))
                if l:
                    act.wait_ge(res_v.sem, res_v.at("x", l - 1, 1))
                def x_there(g):
                    if l:
                        act.wait_ge(res_v.sem, res_v.at("x", 0, 1) - 1 + g)
                if l:
                    ss_(l, 0, lambda g: xt[:, g, :], x_there)
                cT = condT.rearrange("p k (o c) -> p k o c", o=1).to_broadcast([P, KC, P // 2, 2])
                ocd.inc(AC(condR[0].rearrange("p k (o c) -> p k o c", c=2), cT, ACT.Copy), "hi")
                for j in range(U_ADA):
                    high(act, u_ada[l] + j)
                    if j == 4 and l == 0:
                        ss_(l, 0, lambda g: xt[:, g, :], x_there)
                act.wait_ge(ada_v.sem, ada_v.at("mod", l))
                omh.inc(AC(mod_hi[0][:, :], mod[:, 0, :], ACT.Copy), "h")
                up = u_proj[l]
                for n in range(WRING):
                    high(act, up + n)
                norm_(l, 0)

                def silu(p):
                    for s in range(2):
                        act.wait_ge(cnv_v.sem, cnv_v.at("t%d%d" % (TAPS - 1, s), l, p))
                        ocv.inc(AC(qkv[:, 2 * PAIRS[p] + s, :, PAD:PAD + P], acc[s], ACT.Silu), "s%d" % s)

                act.wait_ge(s_lay, 16 * LAY_DMAS * (l + 1))
                act.wait_ge(lay_g.sem, lay_g.at("pads", l))
                for n in range(U_PROJ + 2):
                    if WRING <= n < U_PROJ:
                        high(act, up + n)
                    if n == 2:
                        act.wait_ge(gat_v.sem, gat_v.at("ba", l))
                        oga.inc(AC(eb, ba[:, :, 0:16], ACT.Exp, scale=-1.0), "eb")
                        oga.inc(AC(ealog, alog, ACT.Exp), "ea")
                        act.wait_ge(gat_v.sem, gat_v.at("na", l))
                        oga.inc(AC(ga[2], ga[1], ACT.Exp), "el")
                        act.wait_ge(gat_v.sem, gat_v.at("e1", l))
                        oga.inc(AC(ga[3], ga[2], ACT.Ln), "ln")
                    if n == 6:
                        act.wait_ge(gat_v.sem, gat_v.at("kd", l))
                        oga.inc(AC(gex[:, 0:32], gcs[:, 0:32], ACT.Exp), "ex")
                        oga.inc(AC(gex[:, 32:64], gcs[:, 32:64], ACT.Exp), "ex")
                    m = n - 2
                    if 0 <= m < 12:
                        wait_used(act, up + m)
                        oev.inc(AC(qkv[:, 2 * PAIRS[m]:2 * PAIRS[m] + 2, :, PAD:PAD + P],
                                   ps[:, 2 + m % 6, :].rearrange("p (c g t) -> p c g t", c=2, g=G), ACT.Copy), "b%d" % m)
                    elif m >= 12 and m % 2:
                        j = (m - 12) // 2
                        wait_used(act, up + m)
                        oev.inc(AC(tok[:, :, 512 * j:512 * j + 512], ps[:, 2 + 2 * (j % 3):4 + 2 * (j % 3), :],
                                   ACT.Silu if j in (3, 4) else ACT.Copy), "t%d" % j)
                    if n >= 5 and n % 2 and (n - 5) // 2 < 12:
                        silu((n - 5) // 2)
                act.wait_ge(kt_p.sem, kt_p.at("k", l))
                okt.inc(AC(kTb[:, 0], ps[:, 6, 0:384].rearrange("p (a b) -> p a b", a=3), ACT.Copy), "k")
                okt.inc(AC(kTb[:, 1], ps[:, 7, 0:384].rearrange("p (a b) -> p a b", a=3), ACT.Copy), "o")
                with act.Fori(0, 4) as i:
                    for s in range(2):
                        act.wait_ge(dn_p.sem, dn_p.at("tr%d" % s, l, i))
                        act.wait_ge(dn_p.sem, dn_p.at("SF%d" % s, l, i - 1))
                        if s == 0:
                            act.wait_ge(l2_v.sem, l2_v.at("nm1", l, 3))
                        odn.inc(AC(ktv[s], ps[:, 3 * s, 0:384].rearrange("p (a b) -> p a b", a=3), ACT.Copy), "tok%d" % s)
                    for s in range(2):
                        act.wait_ge(dn_v.sem, dn_v.at("t%d" % s, l, i))
                        odn.inc(AC(ET[s], ET[s], ACT.Exp), "ET%d" % s)
                    for s in range(2):
                        act.wait_ge(dn_p.sem, dn_p.at("m%d" % s, l, i))
                        act.wait_ge(dn_v.sem, dn_v.at("E1_%d" % s, l, i))
                        odn.inc(AC(SS[s][:, 0].rearrange("p g k -> p (g k)"), ps[:, 3 * s + 2, 0:256], ACT.Copy), "X%d" % s)
                    for s in range(2):
                        act.wait_ge(dn_p.sem, dn_p.at("V%d" % s, l, i))
                        for d in range(2):
                            for g in range(G):
                                odn.inc(AC(VN[s][:, d, g], ps[:, 3 * s + 1, (2 * d + g) * P:(2 * d + g + 1) * P], ACT.Copy,
                                           scale=hc[s][:, 4, d, g:g + 1]), "VN%d" % s)
                    for s in range(2):
                        act.wait_ge(dn_p.sem, dn_p.at("SF%d" % s, l, i))
                        act.wait_ge(s_state[s], i * 16 + 64 * l)
                        odn.inc(AC(sfo[s], ps[:, 3 * s + 1, 0:256].rearrange("p (a b) -> p a b", a=2), ACT.Copy), "Sf%d" % s)
                    for s in range(2):
                        act.wait_ge(dn_v.sem, dn_v.at("ob%d" % s, l, i))
                        for g in range(G):
                            odn.inc(AC(junk[s][:, g], osb[s][:, g], ACT.Square, accum_out=oss[s][:, g:g + 1]), "sq%d" % s)
                with act.Fori(0, 4) as i:
                    for s in range(2):
                        act.wait_ge(at_p.sem, at_p.at("qt%d" % s, l, i))
                        act.wait_ge(at_p.sem, at_p.at("sc%d" % s, l, i - 1))
                        oat.inc(AC(qT[s], ps[:, 4 * s, 0:256].rearrange("p (a b) -> p a b", a=2), ACT.Copy, scale=SCALE), "qe%d" % s)
                    for s in range(2):
                        act.wait_ge(at_v.sem, at_v.at("nm%d" % s, l, i))
                        act.wait_ge(at_p.sem, at_p.at("pt%d" % s, l, i - 1))
                        for g in range(G):
                            oat.inc(AC(pr[s][:, g:1 + 2 * g], ps[:, 4 * s + 1, g * P:(1 + 2 * g) * P]
                                       .rearrange("p (a b) -> p a b", b=P), ACT.Exp, bias=am[s][2][:, g:g + 1],
                                       accum_out=am[s][3][:, g:g + 1]), "P%d" % s)
                    for s in range(2):
                        act.wait_ge(at_v.sem, at_v.at("sd%d" % s, l, i))
                        oat.inc(AC(am[s][5][:, 0:2], am[s][4][:, 0:2], ACT.Exp), "se%d" % s)
                    for s in range(2):
                        act.wait_ge(at_p.sem, at_p.at("pt%d" % s, l, i))
                        act.wait_ge(at_p.sem, at_p.at("pv%d" % s, l, i - 1))
                        oat.inc(AC(prT[s], ps[:, 4 * s + 2, 0:384].rearrange("p (a b) -> p a b", a=3), ACT.Copy), "pe%d" % s)
                gt = tok[:, :, T_GA:COLS]
                act.wait_ge(evac.sem, evac.at("t8", l))
                onl.inc(AC(gt, gt, ACT.Sigmoid), "sig")
                act.wait_ge(dn_v.sem, dn_v.at("y1", l, 3))
                for s in range(2):
                    act.wait_ge(s_state[s], 64 * (l + 1))
                for j in range(8):
                    b, g, h = j // 4, j // 2 % 2, j % 2
                    act.wait_ge(out_p.sem, out_p.at("tr%d" % j, l))
                    oout.inc(AC((hT, bT)[b][:, 0, 4 * h:4 * h + 4, g * P:(g + 1) * P],
                                ps[:, j, :].rearrange("p (k t) -> p k t", k=4), ACT.Copy), "ev%d" % j)
                for j in range(11):
                    high(act, u_out[l] + j)
                    if j == 2:
                        act.wait_ge(adm_v.sem, adm_v.at("mod", l))
                        omh.inc(AC(mod_hi[1][:, :], mod[:, 1, :], ACT.Copy), "h")
                for j in range(4):
                    h, g = j // 2, j % 2
                    act.wait_ge(out_p.sem, out_p.at("mt%d" % j, l))
                    oout.inc(AC(hT[:, 0, 4 * h:4 * h + 4, g * P:(g + 1) * P],
                                ps[:, j, :].rearrange("p (k t) -> p k t", k=4), ACT.Copy), "me%d" % j)
                high(act, u_out[l] + 11)
                ss_(l, 1, y_ps, lambda g: act.wait_ge(out_v.sem, out_v.at("y", l) - 1) if g else wait_used(act, u_out[l] + U_OUT - 1))
                ss_(l, 2, lambda g: xt[:, g, :], lambda g: act.wait_ge(res_v.sem, res_v.at("x", l, 0) - 1 + g))
                nxt = (u_ff, u_moe)[l]
                for n in range(2):
                    high(act, nxt + n)
                norm_(l, 1)
                act.wait_ge(s_out, 32 * (l + 1))
                if l == 0:
                    def silus(f, first=False):
                        if first:
                            wait_used(act, u_ff + 1)
                        else:
                            act.wait_ge(unit_used, f * 3 + (sp_(u_ff) + 1 + WRING))
                        act.wait_ge(ff_v.sem, ff_v.at("mu", 0, f - 1))
                        for g in range(G):
                            off.inc(AC(f_hs[0][:, 256 * g:256 * g + 256], ps[:, g, 0:256], ACT.Silu), "si")

                    def hiddenT(f, s):
                        act.wait_ge(ff_p.sem, ff_p.at("ht", 0, f))
                        ofh.inc(AC(fT[:, s, 0].rearrange("p a b -> p (a b)"), ps[:, 2 + s, :], ACT.Copy), "he")

                    high(act, u_ff + 2)
                    silus(0, True)
                    high(act, u_ff + 3)
                    hiddenT(0, 0)
                    high(act, u_ff + 4)
                    silus(1)
                    with act.Fori(0, (FF_STEPS - 3) // 4) as i:
                        for j in range(4):
                            for x in range(3):
                                if x == 2:
                                    hiddenT(i * 4 + (1 + j), (1 + j) % 2)
                                high(act, u_ff + 5 + 3 * j + x, i)
                            silus(i * 4 + (2 + j))
                    for x in range(3):
                        if x == 2:
                            hiddenT(FF_STEPS - 2, 1)
                        high(act, u_ff + 29 + x)
                    silus(FF_STEPS - 1)
                    high(act, u_ff + 32)
                    hiddenT(FF_STEPS - 1, 0)
                else:
                    act.wait_ge(rt_v.sem, rt_v.at("d"))
                    ort.inc(AC(rcol[3], rcol[2], ACT.Exp), "ex")

                    def fetch(i, e, slot, f, block_=0):
                        h = f - 4
                        if h >= 0:
                            act.wait_ge(pre_p.sem, pre_p.at("ga%d" % h, 0, i))
                            opr.inc(AC(hTe[slot][0][:, 4 * h:4 * h + 4], ps[:, 6 + h, :].rearrange("p (k t) -> p k t", k=4), ACT.Copy),
                                    "ge%d" % h)

                    def body(i, slot, u, r, hook):
                        for f in range(FB + 1):
                            n = u + gu(f)
                            if f < FB:
                                for x in range(4):
                                    if not (isinstance(i, int) and i == 0 and f == 0 and x < 2):
                                        high(act, n + x, r)
                                n += 4
                            if f:
                                act.wait_ge(moe_p.sem, moe_p.at("ht%d" % (f - 1), 0, i))
                                omo.inc(AC(fT[:, (f - 1) % 2, 0].rearrange("p a b -> p (a b)"), ps[:, 2 + (f - 1) % 2, :], ACT.Copy),
                                        "he%d" % (f - 1))
                                high(act, n, r)
                                high(act, n + 1, r)
                            if f < FB:
                                wait_used(act, u + gu(f) + 3, r)
                                act.wait_ge(moe_v.sem, moe_v.at("mu%d" % (f - 1), 0, i) if f else moe_v.at("mu%d" % (FB - 1), 0, i - 1))
                                omo.inc(AC(f_hs[0], ps[:, 0, :], ACT.Silu), "si%d" % f)
                                hook(f)
                    experts(act, fetch, body, lambda i, slot, f: None)
                if l == 0:
                    ss_(l, 3, y_ps, lambda g: act.wait_ge(ffe_v.sem, ffe_v.at("y", l) - 1) if g else wait_used(act, u_ff + U_FF - 1))
                else:
                    ss_(l, 3, lambda g: y_sb[:, g, :], lambda g: act.wait_ge(ffe_v.sem, ffe_v.at("y", l) - 1 + g))

        @block.tensor
        def _(pe):
            for s in P_STEPS:
                pe.sem_inc(s.sem, s.per)
            (oi, onr, oga, ol2, odn, okt, oat, oout, ore, off, ort, omo, opr, opo) = (Order(s) for s in P_STEPS)
            mm = pe.matmul

            def tr(out, src, n=P):
                return pe.transpose(out, src, con[0:n, K_ID:K_ID + n])

            pe.wait_ge(init_a.sem, init_a.at("cond"))
            for k in range(KC):
                ins = tr(ps[:, 0, 2 * k:2 * k + 2], condS[:, k * P:(k + 1) * P], 2)
            oi.inc(ins, "condT")
            pe.wait_ge(init_v.sem, init_v.at("condT"))

            def used(ins):
                ins.then_inc(unit_used, 1)

            def prod(u, i, outs, wide=512):
                wait_hi(pe, u, i)
                for x in range(2):
                    for o, hi, lo, c, first, _ in outs:
                        mm(o, (hi, lo)[x], part(u, 0)[:, c:c + wide], start=(first and x == 0), stop=False)
                wait_lo(pe, u, i)
                for o, hi, lo, c, _, last in outs:
                    ins = mm(o, hi, part(u, 1)[:, c:c + wide], start=False, stop=last)
                used(ins)

            def bcast(bank, m, g):
                q, c = MODS[m]
                for n in range(2):
                    for x, r in enumerate((mod_hi[c][32 * q:32 * q + 2, 512 * n:512 * n + 512], mod_lo[32 * q:32 * q + 2, c, 512 * n:512 * n + 512])):
                        ins = mm(ps[:, bank + n, :], selR[32 * q:32 * q + 2, g * P:(g + 1) * P], r, start=(x == 0), stop=(x == 1))
                return ins

            def norm_(l, n):
                for g in range(G):
                    bcast(4 * g, (1, 4)[n], g)
                    onr.inc(bcast(4 * g + 2, (0, 3)[n], g), "bc%d" % g)
                for g in range(G):
                    pe.wait_ge(nrm_v.sem, nrm_v.at("h%d" % g, l, n))
                    for h in range(2):
                        for k in range(4):
                            ins = tr(ps[:, 4 * g + h, k * P:(k + 1) * P], h_tok[:, g, (4 * h + k) * P:(4 * h + k + 1) * P])
                        onr.inc(ins, "t%d%d" % (g, h))
                pe.wait_ge(nrm_v.sem, nrm_v.at("l11", l, n))

            for l in range(DEPTH):
                if l:
                    pe.wait_ge(res_v.sem, res_v.at("x", l - 1, 1))
                pe.wait_ge(cnd_v.sem, cnd_v.at("lo", l))
                for j in range(U_ADA // 2):
                    for h in range(2):
                        prod(u_ada[l] + 2 * j + h, 0,
                             [(ps[:, j, :], condR[0][:, 4 * h + k], condR[1][:, 4 * h + k], k * 512, h + k == 0, h == 1 and k == 3)
                              for k in range(4)])
                pe.wait_ge(mdl_v.sem, mdl_v.at("l", l, 0))
                if l:
                    pe.wait_ge(res_v.sem, res_v.at("x", l - 1, 1))
                norm_(l, 0)
                pe.wait_ge(s_lay, 16 * LAY_DMAS * (l + 1))
                for g in range(G):
                    for k in range(KC):
                        for x in range(2):
                            ins = mm(ps[:, 0, 32 * g:32 * g + 32], hT[:, x, k, g * P:(g + 1) * P].bitcast(F32), wba[:, k, :],
                                     start=(k + x == 0), stop=(k == KC - 1 and x == 1))
                oga.inc(ins, "ba")
                oga.inc(tr(ps[:, 0, P:P + TAPS * QKV_CH], cwr[0:TAPS * QKV_CH, :], TAPS * QKV_CH), "cw")
                up = u_proj[l]
                for n in range(12):
                    if n >= 6:
                        pe.wait_ge(evac.sem, evac.at("b%d" % (n - 6), l))
                    elif n == 0:
                        pe.wait_ge(nrm_v.sem, nrm_v.at("l11", l, 0))
                    wait_hi(pe, up + n)
                    wait_lo(pe, up + n)
                    for c in range(2):
                        for k in range(KC):
                            for y, x in ((0, 0), (0, 1), (1, 0)):
                                ins = mm(ps[:, 2 + n % 6, 256 * c:256 * c + 256], part(up + n, y)[:, k * 256 + c * P:k * 256 + (c + 1) * P],
                                         hT[:, x, k, :], start=(k + x + y == 0), stop=(k == KC - 1 and y == 1))
                    used(ins)
                    if n == 3:
                        pe.wait_ge(gat_v.sem, gat_v.at("g0", l))
                        for d in range(2):
                            gd = ga[4][:, :, 8 * d:8 * d + 8]
                            mm(ps[:, 1, 16 * d:16 * d + 16], tri(d), gd, start=True, stop=True)
                            ins = mm(ps[:, 1, 32 + 16 * d:48 + 16 * d], ones, gd, start=True, stop=True)
                        oga.inc(ins, "gc")
                    l2_pe = {4 * i + 9: (0, i) for i in range(4)}
                    l2_pe.update({4 * i + 12: (1, i) for i in range(4)})

                    def l2_(n):
                        if n not in l2_pe:
                            return
                        what, i = l2_pe[n]
                        if what == 0:
                            pe.wait_ge(l2_g.sem, l2_g.at("sq1", l, i))
                            pe.wait_ge(l2_v.sem, l2_v.at("nm1", l, i - 1))
                            if i == 0:
                                pe.wait_ge(gat_v.sem, gat_v.at("ba", l))
                            for s in range(2):
                                for c in range(2):
                                    for g in range(G):
                                        ins = mm(ps[:, 0, 4 * s + 2 * c + g:4 * s + 2 * c + g + 1], l2s[s][:, c, g], ones[:, 0:1],
                                                 start=True, stop=True)
                            ol2.inc(ins, "ss")
                        else:
                            pe.wait_ge(l2_g.sem, l2_g.at("pw", l, i))
                            if i == 0:
                                pe.wait_ge(gat_v.sem, gat_v.at("gcs", l))
                            for s in range(2):
                                for x in range(4):
                                    ins = mm(ps[:, 1 - s, x * P:(x + 1) * P], l2c[:, 4 * s + x:4 * s + x + 1].to_broadcast([P, P]),
                                             ident, start=True, stop=True)
                                ol2.inc(ins, "bc%d" % s)
                    l2_(n)
                for n in range(12, U_PROJ):
                    j, h = (n - 12) // 2, n % 2
                    if h == 0:
                        for m in ([6 + 2 * j, 7 + 2 * j] if j < 3 else []):
                            pe.wait_ge(evac.sem, evac.at("b%d" % m, l))
                        if j >= 3:
                            pe.wait_ge(evac.sem, evac.at("t%d" % (j - 3), l))
                    prod(up + n, 0, [(ps[:, 2 + 2 * (j % 3) + g, :], hT[:, 0, 4 * h + k, g * P:(g + 1) * P],
                                      hT[:, 1, 4 * h + k, g * P:(g + 1) * P], k * 512, h + k == 0, h == 1 and k == 3)
                                     for k in range(4) for g in range(G)])
                    l2_(n)
                pe.wait_ge(evac.sem, evac.at("t8", l))
                pe.wait_ge(l2_v.sem, l2_v.at("nm1", l, 3))
                pe.wait_ge(rp_v.sem, rp_v.at("x2", l, 2))
                for v in range(HKV):
                    tr(ps[:, 6 + v, 0:P], tok[:, 0, T_K + v * P:T_K + (v + 1) * P])
                    tr(ps[:, 6 + v, P:2 * P], cache_k[:, v, :])
                    ins = tr(ps[:, 6 + v, 2 * P:3 * P], tok[:, 1, T_K + v * P:T_K + (v + 1) * P])
                okt.inc(ins, "k")
                pe.wait_ge(kt_a.sem, kt_a.at("o", l))
                with pe.Fori(0, 4) as i:
                    def each(f):
                        for s in range(2):
                            f(s, 3 * s)

                    def inst():
                        return [(d, g, (2 * d + g) * P) for d in range(2) for g in range(G)]

                    def turn(s, b):
                        pe.wait_ge(dq_g.sem, dq_g.at("kqv%d" % s, l, i))
                        pe.wait_ge(dn_v.sem, dn_v.at("ob%d" % s, l, i - 1))
                        tr(ps[:, b, 0:P], kqv[s][:, 1, 0])
                        tr(ps[:, b, P:2 * P], kqv[s][:, 2, 0])
                        odn.inc(tr(ps[:, b, 2 * P:3 * P], kqv[s][:, 2, 1]), "tr%d" % s)
                    each(turn)

                    def gram(s, b):
                        pe.wait_ge(dn_a.sem, dn_a.at("Sf%d" % s, l, i - 1))
                        for g in range(G):
                            ins = mm(ps[:, b + 1, 256 * g:256 * g + 256], kqv[s][:, 1, g], kqv[s][:, 0:2, g, :], start=True, stop=True)
                        odn.inc(ins, "G%d" % s)
                    each(gram)

                    def decay(s, b):
                        pe.wait_ge(dq_g.sem, dq_g.at("hc%d" % s, l, i))
                        pe.wait_ge(dn_v.sem, dn_v.at("oc%d" % s, l, i - 1))
                        for d, g, c in inst():
                            ins = mm(ps[:, b + 2, c:c + P], hc[s][:, 0, d, g:g + 1].to_broadcast([P, P]), tri(d), start=True, stop=True)
                        odn.inc(ins, "gr%d" % s)
                    each(decay)

                    def rest_(q):
                        u = u_adb[l] + q
                        wait_in(pe, u, i, 4)
                        pe.wait_ge(adb_v.sem, adb_v.at("r%d" % (q - 2), l, i) if q > 1 else adb_v.at("r%d" % (q + 2), l, i - 1))
                        for k in range(KC):
                            ins = mm(ps[0:2, 6 + q % 2, 0:256], condT[:, k], unit(u)[:, 256 * k:256 * k + 256],
                                     start=(k == 0), stop=(k == KC - 1))
                        ins.then_inc(unit_lo, 1)
                    rest_(0)
                    rest_(1)

                    def first(s, b):
                        pe.wait_ge(dn_v.sem, dn_v.at("I%d" % s, l, i))
                        for g in range(G):
                            ins = tr(ps[:, b + 2, g * P:(g + 1) * P], SS[s][:, 1, g])
                        odn.inc(ins, "m%d" % s)
                    each(first)
                    for v in lv:
                        def left(s, b):
                            if v == 1:
                                pe.wait_ge(dn_a.sem, dn_a.at("tok%d" % s, l, i))
                            pe.wait_ge(dn_v.sem, dn_v.at("E%d_%d" % (v, s), l, i))
                            for g in range(G):
                                ins = mm(ps[:, b, g * P:(g + 1) * P], MM[s][:, 1, g], XX[s][:, 0, 0, g], start=True, stop=True)
                            odn.inc(ins, "a%d_%d" % (v, s))
                        each(left)

                        def right(s, b):
                            pe.wait_ge(dn_v.sem, dn_v.at("T%d_%d" % (v, s), l, i))
                            if v == 1:
                                pe.wait_ge(dn_a.sem, dn_a.at("X%d" % s, l, i))
                            else:
                                pe.wait_ge(dn_g.sem, dn_g.at("Et%d_%d" % (v, s), l, i))
                            for g in range(G):
                                if v < LEVELS - 1:
                                    mm(ps[:, b + 2, g * P:(g + 1) * P], XX[s][:, 0, 1, g], MM[s][:, 0, g], start=True, stop=True)
                                ins = mm(ps[:, b + 2, (2 + g) * P:(3 + g) * P], MM[s][:, 0, g], XX[s][:, 0, 1, g], start=True, stop=True)
                            odn.inc(ins, "b%d_%d" % (v, s))
                        each(right)

                    def state(s, b):
                        pe.wait_ge(s_st, 32 * (l + 1))
                        for x in range(2):
                            ins = mm(ps[:, b, 256 * x:256 * x + 256], kqv[s][:, 1 - x, 1],
                                     s0[:, bass.ds(i * 2 + s, 1)].rearrange("p h d v -> p (h d v)"), start=True, stop=True)
                        odn.inc(ins, "kS%d" % s)
                    each(state)

                    def values(s, b):
                        pe.wait_ge(dn_v.sem, dn_v.at("E%d_%d" % (LEVELS, s), l, i))
                        pe.wait_ge(dn_v.sem, dn_v.at("R%d" % s, l, i))
                        for d, g, c in inst():
                            ins = mm(ps[:, b + 1, c:c + P], XX[s][:, 1, d, g], RP[s][:, d] if g else ktv[s][:, 1],
                                     start=True, stop=True)
                        odn.inc(ins, "V%d" % s)
                    each(values)
                    rest_(2)

                    def out(s, b):
                        pe.wait_ge(dn_a.sem, dn_a.at("VN%d" % s, l, i))
                        pe.wait_ge(dn_g.sem, dn_g.at("EM%d" % s, l, i))
                        for g in range(G):
                            for d in range(2):
                                ins = mm(ps[:, b + 2, g * P:(g + 1) * P], attn[s][:, d, g], VN[s][:, d, g],
                                         start=(d == 0), stop=(d == 1))
                        odn.inc(ins, "O%d" % s)
                    each(out)

                    def final(s, b):
                        pe.wait_ge(dn_v.sem, dn_v.at("VD%d" % s, l, i))
                        odn.inc(mm(ps[:, b + 1, 0:256], ktv[s][:, 0], VD[s].rearrange("p d v -> p (d v)"),
                                   start=True, stop=True), "SF%d" % s)
                    each(final)
                    rest_(3)
                pe.wait_ge(dn_v.sem, dn_v.at("ob1", l, 3))
                pe.wait_ge(dn_a.sem, dn_a.at("Sf1", l, 3))
                pe.wait_ge(adb_v.sem, adb_v.at("r3", l, 3))
                with pe.Fori(0, 4) as i:
                    for s in range(2):
                        pe.wait_ge(at_g.sem, at_g.at("q%d" % s, l, i))
                        pe.wait_ge(at_a.sem, at_a.at("qe%d" % s, l, i - 1))
                        tr(ps[:, 4 * s, 0:P], qst[s][:, 0])
                        oat.inc(tr(ps[:, 4 * s, P:2 * P], qst[s][:, 1]), "qt%d" % s)
                    for s in range(2):
                        pe.wait_ge(at_a.sem, at_a.at("qe%d" % s, l, i))
                        pe.wait_ge(at_a.sem, at_a.at("P%d" % s, l, i - 1))
                        mm(ps[:, 4 * s + 1, 0:P], qT[s][:, 0], kTb[:, s, 0], start=True, stop=True)
                        oat.inc(mm(ps[:, 4 * s + 1, P:3 * P], qT[s][:, 1], kTb[:, s, 1:3].rearrange("p a b -> p (a b)"),
                                   start=True, stop=True), "sc%d" % s)
                    for s in range(2):
                        pe.wait_ge(at_a.sem, at_a.at("P%d" % s, l, i))
                        pe.wait_ge(at_a.sem, at_a.at("pe%d" % s, l, i - 1))
                        for k in range(3):
                            ins = tr(ps[:, 4 * s + 2, k * P:(k + 1) * P], pr[s][:, k])
                        oat.inc(ins, "pt%d" % s)
                    for s in range(2):
                        pe.wait_ge(at_a.sem, at_a.at("pe%d" % s, l, i))
                        pe.wait_ge(at_v.sem, at_v.at("o%d" % s, l, i - 1))
                        mm(ps[:, 4 * s + 3, 0:P], prT[s][:, 0], tok[:, 0, T_V + s * P:T_V + (s + 1) * P], start=True, stop=True)
                        mm(ps[:, 4 * s + 3, P:2 * P], prT[s][:, 1], cache_v[:, s, :], start=True, stop=False)
                        oat.inc(mm(ps[:, 4 * s + 3, P:2 * P], prT[s][:, 2], tok[:, 1, T_V + s * P:T_V + (s + 1) * P],
                                   start=False, stop=True), "pv%d" % s)
                pe.wait_ge(at_v.sem, at_v.at("o1", l, 3))
                for j in range(8):
                    b, g, h = j // 4, j // 2 % 2, j % 2
                    for k in range(4):
                        c = (0, T_Z)[b] + (4 * h + k) * P
                        ins = tr(ps[:, j, k * P:(k + 1) * P], tok[:, g, c:c + P])
                    oout.inc(ins, "tr%d" % j)
                pe.wait_ge(out_v.sem, out_v.at("lv7", l))
                u = [u_out[l]]

                def project(src, bank):
                    for n in range(2):
                        for h in range(2):
                            prod(u[0], 0, [(ps[:, bank(n, g), :], src[:, 0, 4 * h + k, g * P:(g + 1) * P],
                                            src[:, 1, 4 * h + k, g * P:(g + 1) * P], k * 512, h + k == 0, h == 1 and k == 3)
                                           for k in range(4) for g in range(G)])
                            u[0] += 1
                project(hT, lambda n, g: 2 * n + g)
                project(bT, lambda n, g: 4 + 2 * n + g)
                for j in range(4):
                    h, g = j // 2, j % 2
                    pe.wait_ge(out_v.sem, out_v.at("m%d" % h, l))
                    for k in range(4):
                        c = T_GA + (4 * h + k) * P
                        ins = tr(ps[:, j, k * P:(k + 1) * P], tok[:, g, c:c + P])
                    oout.inc(ins, "mt%d" % j)
                pe.wait_ge(out_v.sem, out_v.at("ml3", l))
                project(hT, lambda n, g: 4 + 2 * g + n)

                def gate_rows(n):
                    for g in range(G):
                        ins = bcast(2 * g, (2, 5)[n], g)
                    ore.inc(ins, "gb")
                pe.wait_ge(mdl_v.sem, mdl_v.at("l", l, 1))
                gate_rows(0)
                pe.wait_ge(res_v.sem, res_v.at("t", l, 0))
                norm_(l, 1)
                if l == 0:
                    def gate_up(u, i, f, s=None):
                        pe.wait_ge(ff_v.sem, ff_v.at("mu", 0, f - 1))
                        for x in range(2):
                            if x and s is not None:
                                hidden(f - 1, s)
                            prod(u + x, i, [(ps[:, g, 256 * x:256 * x + 256], hT[:, 0, k, g * P:(g + 1) * P],
                                             hT[:, 1, k, g * P:(g + 1) * P], k * 256, k == 0, k == KC - 1)
                                            for k in range(KC) for g in range(G)], 256)

                    def hidden(f, s):
                        pe.wait_ge(ff_v.sem, ff_v.at("mu", 0, f))
                        for k in range(4):
                            ins = tr(ps[:, 2 + s, k * P:(k + 1) * P], f_hid[s][:, k * P:(k + 1) * P])
                        off.inc(ins, "ht")

                    def down(u, i, f, s, at_=None):
                        pe.wait_ge(ff_l.sem, ff_l.at("hl", 0, f))
                        prod(u, i, [(ps[:, 4 + 2 * g + n, :], fT[:, s, 0, 2 * g + k], fT[:, s, 1, 2 * g + k],
                                     k * 1024 + n * 512, at_ == 0 and k == 0, at_ == 1 and k == 1)
                                    for k in range(2) for g in range(G) for n in range(2)])
                    gate_up(u_ff, 0, 0)
                    gate_up(u_ff + 2, 0, 1, 0)
                    down(u_ff + 4, 0, 0, 0, 0)
                    with pe.Fori(0, (FF_STEPS - 3) // 4) as i:
                        for j in range(4):
                            gate_up(u_ff + 5 + 3 * j, i, i * 4 + (2 + j), (1 + j) % 2)
                            down(u_ff + 7 + 3 * j, i, i * 4 + (1 + j), (1 + j) % 2)
                    w = u_ff + 3 * FF_STEPS - 4
                    gate_up(w, 0, FF_STEPS - 1, 1)
                    down(w + 2, 0, FF_STEPS - 2, 1)
                    hidden(FF_STEPS - 1, 0)
                    down(w + 3, 0, FF_STEPS - 1, 0, 1)
                else:
                    for g in range(G):
                        for k in range(KC):
                            for x in range(2):
                                ins = mm(ps[:, 0, NEXP * g:NEXP * (g + 1)], hT[:, x, k, g * P:(g + 1) * P].bitcast(F32), wr[:, k, :],
                                         start=(k + x == 0), stop=(k == KC - 1 and x == 1))
                    ort.inc(ins, "lg")
                    pe.wait_ge(rt_v.sem, rt_v.at("mk"))
                    before = con[:, K_STR:K_STR + P]
                    mk = rt[6]
                    mm(ps[:, 1, 0:8], before, mk[:, 0], start=True, stop=True)
                    mm(ps[:, 1, 8:16], before, mk[:, 1], start=True, stop=False)
                    mm(ps[:, 1, 8:16], ones, mk[:, 0], start=False, stop=True)
                    mm(ps[:, 1, 16:24], ones, mk[:, 0], start=True, stop=False)
                    ort.inc(mm(ps[:, 1, 16:24], ones, mk[:, 1], start=False, stop=True), "pos")
                    pe.wait_ge(rt_v.sem, rt_v.at("pos"))

                    def fetch(i, e, slot, f, block_=0):
                        if f == 3:
                            pe.wait_ge(pre_v.sem, pre_v.at("selc", 0, i))
                            for g in range(G):
                                ins = tr(ps[:, 7, g * P:(g + 1) * P], selc[:, g])
                            opr.inc(ins, "sct")
                        h = f - 4
                        if h >= 0:
                            pe.wait_ge(pre_v.sem, pre_v.at("selT", 0, i))
                            for k in range(4):
                                for g in range(G):
                                    ins = mm(ps[:, 6 + h, k * P:(k + 1) * P], h_tok[:, g, (4 * h + k) * P:(4 * h + k + 1) * P],
                                             sel[:, g], start=(g == 0), stop=(g == 1))
                            opr.inc(ins, "ga%d" % h)

                    def back(i, slot, f):
                        g = f - 1
                        if f == 3:
                            pe.wait_ge(post_v.sem, post_v.at("add1", 0, i))
                        elif g >= 0:
                            pe.wait_ge(post_v.sem, post_v.at(("ye", "add0")[g], 0, i))
                            for n in range(2):
                                ins = mm(ps[:, 6 + n, :], selT[slot][:, g], ye[:, n * 512:(n + 1) * 512], start=True, stop=True)
                            opo.inc(ins, "sc%d" % g)

                    def body(i, slot, u, r, hook):
                        pe.wait_ge(pre_v.sem, pre_v.at("gl1", 0, i))
                        for f in range(FB + 1):
                            n = u + gu(f)
                            if f < FB:
                                pe.wait_ge(moe_v.sem, moe_v.at("mu%d" % (f - 1), 0, i) if f else moe_v.at("mu%d" % (FB - 1), 0, i - 1))
                            for x in range(2):
                                if x and f:
                                    b = (f - 1) % 2
                                    pe.wait_ge(moe_v.sem, moe_v.at("mu%d" % (f - 1), 0, i))
                                    for k in range(4):
                                        ins = tr(ps[:, 2 + b, k * P:(k + 1) * P], f_hid[b][:, k * P:(k + 1) * P])
                                    omo.inc(ins, "ht%d" % (f - 1))
                                if x and f < FB:
                                    hook(f)
                                for h in range(2 if f < FB else 0):
                                    prod(n, r, [(ps[:, x, :], hTe[slot][0][:, 4 * h + k], hTe[slot][1][:, 4 * h + k], k * 512,
                                                 h + k == 0, h == 1 and k == 3) for k in range(4)])
                                    n += 1
                            if f:
                                pe.wait_ge(moe_v.sem, moe_v.at("hl%d" % (f - 1), 0, i))
                                for h in range(2):
                                    if f == 1 and h == 0:
                                        pe.wait_ge(post_v.sem, post_v.at("ye", 0, i - 1))
                                    prod(n, r, [(ps[:, 4 + n_, :], fT[:, b, 0, 2 * h + k], fT[:, b, 1, 2 * h + k],
                                                 k * 1024 + n_ * 512, f == 1 and h + k == 0, f == FB and h + k == 2)
                                                for k in range(2) for n_ in range(2)])
                                    n += 1
                    experts(pe, fetch, body, back)
                if l:
                    pe.wait_ge(ffe_v.sem, ffe_v.at("y", l))
                gate_rows(1)

        @block.vector
        def _(dve):
            for s in V_STEPS:
                dve.sem_inc(s.sem, s.per)
            (oi, ocd, oad, orm, onr, oga, ocv, onl, ol2, odn, orp, oat, oout, ore, off, ofl, ofe, ort, omo, opr, opo, oab, oam, oml, ocl) = (Order(s) for s in V_STEPS)
            TT, TS, STT, CP = dve.tensor_tensor, dve.tensor_scalar, dve.scalar_tensor_tensor, dve.tensor_copy

            def own(st, name, l=0, i=0):
                dve.wait_ge(st.sem, st.at(name, l, i))

            ocl.inc(dve.memset(mod[:, :, :], 0.0), "mod")
            oi.inc(dve.memset(mhalf, -0.5), "half")
            dve.wait_ge(init_p.sem, init_p.at("condT"))
            oi.inc(CP(condT, ps[:, 0, 0:16].rearrange("p (k c) -> p k c", c=2)), "condT")

            def ms_(l, k):
                dve.wait_ge(rms_a.sem, rms_a.at("ss", l, k))
                if k or l:
                    dve.wait_ge(rms_g.sem, rms_g.at("rstd", l, k - 1))
                orm.inc(TS(ms, ss, 1.0 / D, EPS, ALU.mult, ALU.add), "ms")

            def take_y(o, l, k):
                for g in (1, 0):
                    if g == 0:
                        dve.wait_ge(rms_a.sem, rms_a.at("ss", l, k) - 1)
                    o.inc(CP(y_sb[:, g, :], y_ps(g)), "y")

            def rest(dst, h, g, bank):
                hi, lo = (dst[:, x, 4 * h:4 * h + 4, g * P:(g + 1) * P] for x in range(2))
                return TT(lo, ps[:, bank, :].rearrange("p (k t) -> p k t", k=4), hi.bitcast(F32), ALU.subtract)

            def norm_(l, n):
                if n:
                    ms_(l, 2 * n)
                dve.wait_ge(rms_g.sem, rms_g.at("rstd", l, 2 * n))
                for g in range(G):
                    dve.wait_ge(nrm_p.sem, nrm_p.at("bc%d" % g, l, n))
                    onr.inc(STT(h_tok[:, g, :], xt[:, g, :], rstd[:, g:g + 1],
                                ps[:, 4 * g:4 * g + 2, :].rearrange("p b c -> p (b c)"), ALU.mult, ALU.mult), "a%d" % g)
                    own(nrm_v, "a%d" % g, l, n)
                    onr.inc(TT(h_tok[:, g, :], h_tok[:, g, :], ps[:, 4 * g + 2:4 * g + 4, :].rearrange("p b c -> p (b c)"), ALU.add),
                            "h%d" % g)
                for g in range(G):
                    for h in range(2):
                        dve.wait_ge(nrm_a.sem, nrm_a.at("e%d%d" % (g, h), l, n))
                        onr.inc(rest(hT, h, g, 4 * g + h), "l%d%d" % (g, h))

            def resid(l, n):
                ms_(l, 2 * n + 1)
                dve.wait_ge(rms_g.sem, rms_g.at("rstd", l, 2 * n + 1))
                dve.wait_ge(res_p.sem, res_p.at("gb", l, n))
                for g in range(G):
                    ore.inc(STT(y_sb[:, g, :], y_sb[:, g, :], rstd[:, g:g + 1],
                                ps[:, 2 * g:2 * g + 2, :].rearrange("p b c -> p (b c)"), ALU.mult, ALU.mult), "t")
                own(res_v, "t", l, n)
                for g in range(G):
                    ore.inc(TT(xt[:, g, :], xt[:, g, :], y_sb[:, g, :], ALU.add), "x")

            for l in range(DEPTH):
                if l:
                    ocl.inc(dve.memset(mod[:, :, :], 0.0), "mod")
                dve.wait_ge(cnd_a.sem, cnd_a.at("hi", l))
                cT = condT.rearrange("p k (o c) -> p k o c", o=1).to_broadcast([P, KC, P // 2, 2])
                c0, c1 = (x.rearrange("p k (o c) -> p k o c", c=2) for x in condR)
                own(init_v, "condT")
                ocd.inc(TT(c1, cT, c0.bitcast(F32), ALU.subtract), "lo")
                for b in range(U_ADA):
                    low(dve, u_ada[l] + b)
                ms_(l, 0)
                dve.wait_ge(s_mod, 16 * MOD_DMAS * (l + 1))
                for b in range(4):
                    q, c = MODS[b // 2]
                    wait_used(dve, u_ada[l] + 2 * b + 1)
                    m = mod_row(q, c, b % 2)
                    oad.inc(TT(m, ps[0:2, b, :], m, ALU.add), "row")
                own(ada_v, "row", l)
                oad.inc(STT(mod[32:34, 0, :], mod[32:34, 0, :], 1.0, ngr[32:34, 0, :], ALU.add, ALU.mult), "mod")

                def mod_low(c):
                    dve.wait_ge(mdh_a.sem, mdh_a.at("h", l, c))
                    oml.inc(TT(mod_lo[:, c, :], mod[:, c, :], mod_hi[c][:, :].bitcast(F32), ALU.subtract), "l")
                mod_low(0)
                norm_(l, 0)
                up = u_proj[l]

                def split(x):
                    return x.rearrange("p g (d h) -> p g d h", d=2)

                def to_gt(q):
                    return GT[:, :, q, :, :].rearrange("p h d g -> p g d h")

                def dirs(x):
                    return x.rearrange("p (d g h) -> p d g h", d=2, g=G)

                def to_dirs(q):
                    return GT[:, :, q, :, :].rearrange("p h d g -> p d g h")

                dve.wait_ge(s_lay, 16 * LAY_DMAS * (l + 1))

                def decay_in():
                    dve.wait_ge(gat_p.sem, gat_p.at("cw", l))
                    oga.inc(CP(cw[:, 0:TAPS * QKV_CH], ps[:, 0, P:P + TAPS * QKV_CH]), "cw")
                    oga.inc(CP(ba, ps[:, 0, 0:64].rearrange("p (g c) -> p g c", g=G)), "ba")
                    own(gat_v, "ba", l)
                    oga.inc(TT(ga[0], ba[:, :, 16:32], dtb.rearrange("p (o c) -> p o c", o=1).to_broadcast([P, G, 16]), ALU.add), "a")
                    own(gat_v, "a", l)
                    oga.inc(STT(ga[1], ga[0], -1.0, ga[0], ALU.mult, ALU.min), "na")
                    dve.wait_ge(gat_a.sem, gat_a.at("el", l))
                    oga.inc(TS(ga[2], ga[2], 1.0, None, ALU.add), "e1")
                    dve.wait_ge(gat_a.sem, gat_a.at("ln", l))
                    oga.inc(STT(ga[3], ga[0], 0.0, ga[3], ALU.max, ALU.add), "sp")
                    own(gat_v, "sp", l)
                    oga.inc(STT(ga[4], ga[3], -1.0, ealog.rearrange("p (o c) -> p o c", o=1).to_broadcast([P, G, 16]),
                                ALU.mult, ALU.mult), "g0")
                    own(gat_v, "g0", l)
                    oga.inc(CP(to_gt(0), split(ga[4])), "gcol")

                def decay_sums():
                    dve.wait_ge(gat_p.sem, gat_p.at("gc", l))
                    oga.inc(CP(gcs, ps[:, 1, 0:64]), "gcs")
                    own(gat_v, "gcs", l)
                    oga.inc(TT(gcs[:, 32:64], gcs[:, 32:64], gcs[:, 0:32], ALU.subtract), "kd")
                    oga.inc(CP(to_dirs(1), dirs(gcs[:, 0:32])), "gc")

                def decay_out():
                    dve.wait_ge(gat_a.sem, gat_a.at("ex", l))
                    oga.inc(CP(to_dirs(2), dirs(gex[:, 0:32])), "egc")
                    oga.inc(TS(to_dirs(3), dirs(gex[:, 0:32]), -1.0, None, ALU.mult), "negc")
                    oga.inc(CP(to_dirs(5), dirs(gex[:, 32:64])), "ekd")
                    oga.inc(TS(eb, eb, 1.0, None, ALU.add), "b1")
                    own(gat_v, "b1", l)
                    oga.inc(dve.reciprocal(eb, eb), "rb")
                    own(gat_v, "rb", l)
                    oga.inc(CP(to_gt(4), split(eb)), "beta")

                def conv(p):
                    dve.wait_ge(evac.sem, evac.at("b%d" % p, l))
                    own(gat_v, "cw", l)
                    for j in range(TAPS):
                        for s in range(2):
                            c = 2 * PAIRS[p] + s
                            x, w = qkv[:, c, :, j:j + P], cw[:, j * QKV_CH + c:j * QKV_CH + c + 1]
                            if j == 0:
                                dve.wait_ge(cnv_a.sem, cnv_a.at("s%d" % s, l, p - 1))
                                ocv.inc(TS(acc[s], x, w, None, ALU.mult), "t%d%d" % (j, s))
                            else:
                                own(cnv_v, "t%d%d" % (j - 1, s), l, p)
                                ocv.inc(STT(acc[s], x, w, acc[s], ALU.mult, ALU.add), "t%d%d" % (j, s))

                def norm_in(i):
                    dve.wait_ge(l2_p.sem, l2_p.at("ss", l, i))
                    dve.wait_ge(l2_p.sem, l2_p.at("bc1", l, i - 1))
                    ol2.inc(TS(l2c, ps[:, 0, 0:8], EPS, None, ALU.add), "ep")

                def norm_out(i):
                    for s in range(2):
                        x = qkv[:, 2 * i + 8 * s:2 * i + 8 * s + 2, :, PAD:PAD + P].rearrange("p a g t -> p (a g) t")
                        dve.wait_ge(l2_p.sem, l2_p.at("bc%d" % s, l, i))
                        ol2.inc(STT(x, x, SCALE if s == 0 else 1.0, ps[:, 1 - s, :].rearrange("p (a t) -> p a t", a=4),
                                    ALU.mult, ALU.mult), "nm%d" % s)

                def rope(c):
                    h0, h1 = ROPE[c]
                    own(l2_v, "nm1", l, 3)
                    if c == 0:
                        dve.wait_ge(evac.sem, evac.at("t2", l))
                    else:
                        own(rp_v, "x2", l, c - 1)
                    xs = tok[:, 1, h0 * P:h1 * P].rearrange("p (h f x r) -> p h f x r", h=h1 - h0, f=2, x=2)
                    x1, x2 = xs[:, :, :, 0], xs[:, :, :, 1]
                    cos, sin = (con[:, K_ROPE + 64 * j:K_ROPE + 64 * j + 64].rearrange("p (o f r) -> p o f r", o=1, f=2)
                                .to_broadcast([P, h1 - h0, 2, 32]) for j in range(2))
                    t = [x[:, 0:h1 - h0] for x in rope_t]
                    for j, (a, b) in enumerate(((x1, cos), (x2, sin), (x2, cos), (x1, sin))):
                        orp.inc(TT(t[j], a, b, ALU.mult), "m%d" % j)
                    own(rp_v, "m3", l, c)
                    orp.inc(TT(x1, t[0], t[1], ALU.subtract), "x1")
                    orp.inc(TT(x2, t[2], t[3], ALU.add), "x2")

                for n in range(U_PROJ):
                    low(dve, up + n)
                    if n >= U_PROJ - 4 and n < U_PROJ - 1:
                        rope(n - (U_PROJ - 4))
                    if n == 2:
                        decay_in()
                    if n == 5:
                        decay_sums()
                    if n == 7:
                        decay_out()
                    if n >= 3 and n % 2 and (n - 3) // 2 < 12:
                        conv((n - 3) // 2)
                    if n >= 10 and (n - 10) % 4 == 0 and (n - 10) // 4 < 4:
                        norm_in((n - 10) // 4)
                    if n >= 13 and (n - 13) % 4 == 0 and (n - 13) // 4 < 4:
                        norm_out((n - 13) // 4)
                dve.wait_ge(evac.sem, evac.at("t4", l))
                z = tok[:, :, T_Z:T_Z + D].rearrange("p g (h v) -> p g h v", h=DH)
                onl.inc(TT(z, z, dng[:, :].rearrange("p (a b v) -> p a b v", a=1, b=1).to_broadcast([P, G, DH, P]), ALU.mult), "z")
                with dve.Fori(0, 4) as i:
                    def each(f):
                        for s in range(2):
                            f(s, 3 * s)

                    def w4(s, name):
                        own(dn_v, name % s, l, i)

                    def clamp(s, b):
                        dve.wait_ge(dn_p.sem, dn_p.at("gr%d" % s, l, i))
                        dve.wait_ge(dq_g.sem, dq_g.at("hc%d" % s, l, i))
                        for d in range(2):
                            for g in range(G):
                                c = (2 * d + g) * P
                                odn.inc(TS(ET[s][:, d, g], ps[:, b + 2, c:c + P], hc[s][:, 1, d, g:g + 1], 0.0,
                                           ALU.subtract, ALU.min), "t%d" % s)
                    each(clamp)

                    def pair(s, b, x):
                        return ps[:, b + 1, :].rearrange("p (o g x k) -> p o g x k", o=1, g=G, x=2)[:, :, :, x].to_broadcast([P, 2, G, P])

                    def w_(s, b):
                        dve.wait_ge(dn_a.sem, dn_a.at("ET%d" % s, l, i))
                        dve.wait_ge(dn_p.sem, dn_p.at("G%d" % s, l, i))
                        odn.inc(TT(AT[s], ET[s], pair(s, b, 1), ALU.mult), "W%d" % s)
                    each(w_)

                    def a_(s, b):
                        w4(s, "W%d")
                        for d in range(2):
                            for g in range(G):
                                odn.inc(STT(AT[s][:, d, g], AT[s][:, d, g], hc[s][:, 4, d, g:g + 1],
                                            con[:, K_STR + d * P:K_STR + (d + 1) * P], ALU.mult, ALU.mult), "A%d" % s)
                    each(a_)

                    def b_(s, b):
                        w4(s, "A%d")
                        odn.inc(TT(MM[s][:, 1], AT[s][:, 0], AT[s][:, 1], ALU.add), "B%d" % s)
                    each(b_)

                    def mask(j, n):
                        return lev[:, j * P:(j + n) * P].rearrange("p (d o k) -> p d o k", d=n, o=1).to_broadcast([P, n, G, P])

                    def s_(s, b):
                        w4(s, "B%d")
                        dve.wait_ge(s_lev, 16 * (l + 1))
                        odn.inc(TT(SS[s][:, 1:2], MM[s][:, 1:2], mask(0, 1), ALU.mult), "S%d" % s)
                    each(s_)

                    def i_(s, b):
                        w4(s, "S%d")
                        odn.inc(TT(SS[s][:, 1], SS[s][:, 1], ident.rearrange("p (o k) -> p o k", o=1).to_broadcast([P, G, P]),
                                   ALU.add), "I%d" % s)
                    each(i_)

                    def e1(s, b):
                        w4(s, "I%d")
                        odn.inc(TT(XX[s][:, 0, 1:2], SS[s][:, 1:2], mask(LEVELS, 1), ALU.mult), "E1_%d" % s)
                        dve.wait_ge(dn_p.sem, dn_p.at("m%d" % s, l, i))
                        odn.inc(TT(XX[s][:, 0, 0:1], ps[:, b + 2, 0:256].rearrange("p (d g k) -> p d g k", d=1, g=G),
                                   mask(LEVELS, 1), ALU.mult), "E1_%d" % s)
                    each(e1)

                    def attn_(s, b):
                        dve.wait_ge(dn_p.sem, dn_p.at("O%d" % s, l, i - 1))
                        odn.inc(TT(attn[s], ET[s], pair(s, b, 0), ALU.mult), "at%d" % s)
                    each(attn_)

                    def grow(v):
                        def f(s, b):
                            dve.wait_ge(dn_p.sem, dn_p.at("b%d_%d" % (v, s), l, i))
                            if v == 1:
                                dve.wait_ge(dn_a.sem, dn_a.at("X%d" % s, l, i))

                            def add(x, name):
                                odn.inc(TT(SS[s][:, x], SS[s][:, x], ps[:, b + 2, 256 * x:256 * x + 256]
                                           .rearrange("p (g k) -> p g k", g=G), ALU.add), "%s%d_%d" % (name, v, s))
                            add(0 if v < LEVELS - 1 else 1, "D")
                            own(dn_v, "D%d_%d" % (v, s), l, i)
                            if v < LEVELS - 1:
                                odn.inc(TT(XX[s][:, 0, 0:1], SS[s][:, 0:1], mask(LEVELS + v, 1), ALU.mult), "E%d_%d" % (v + 1, s))
                                add(1, "F")
                            else:
                                odn.inc(TT(XX[s][:, 1], SS[s][:, 1:2].to_broadcast([P, 2, G, P]), two(con[:, K_TRI:K_TRI + 2 * P]),
                                           ALU.mult), "E%d_%d" % (v + 1, s))
                        return f

                    def row_(q):
                        wait_lo(dve, u_adb[l] + q, i, 4)
                        m = mod[32 * q:32 * q + 2, 1, bass.ds(i * 256, 256)]
                        oab.inc(TT(m, ps[0:2, 6 + q % 2, 0:256], m, ALU.add), "r%d" % q)

                    for v in lv:
                        def t_(s, b):
                            dve.wait_ge(dn_p.sem, dn_p.at("a%d_%d" % (v, s), l, i))
                            odn.inc(TT(MM[s][:, 0:1], ps[:, b, 0:256].rearrange("p (d g k) -> p d g k", d=1, g=G), mask(v, 1),
                                       ALU.mult), "T%d_%d" % (v, s))
                        each(t_)
                        each(grow(v))
                        if v < 3:
                            row_(v - 1)

                    def r_(s, b):
                        dve.wait_ge(dn_p.sem, dn_p.at("kS%d" % s, l, i))
                        for d in range(2):
                            odn.inc(STT(RP[s][:, d], ps[:, b, d * P:(d + 1) * P], hc[s][:, 3, d, 1:2], ktv[s][:, 2],
                                        ALU.mult, ALU.add), "R%d" % s)
                    each(r_)

                    def vd(s, b):
                        dve.wait_ge(dn_a.sem, dn_a.at("VN%d" % s, l, i))
                        for d in range(2):
                            odn.inc(TS(VD[s][:, d], VN[s][:, d, 0], hc[s][:, 5, d, 0:1], None, ALU.mult), "VD%d" % s)
                    each(vd)
                    row_(2)

                    def oc(s, b):
                        dve.wait_ge(dn_p.sem, dn_p.at("O%d" % s, l, i))
                        dve.wait_ge(dn_a.sem, dn_a.at("sq%d" % s, l, i - 1))
                        odn.inc(CP(osb[s].rearrange("p g v -> p (g v)"), ps[:, b + 2, 0:256]), "oc%d" % s)
                    each(oc)
                    for d in range(2):
                        def oa(s, b):
                            w4(s, ("oc%d", "oa%d")[d])
                            odn.inc(STT(osb[s][:, 1], ps[:, b, 256 + d * P:256 + (d + 1) * P], hc[s][:, 2, d, 1:2], osb[s][:, 1],
                                        ALU.mult, ALU.add), ("oa%d", "ob%d")[d] % s)
                        each(oa)

                    def msq(s, b):
                        dve.wait_ge(dn_a.sem, dn_a.at("sq%d" % s, l, i))
                        odn.inc(TS(oss[s], oss[s], 1.0 / P, EPS, ALU.mult, ALU.add), "ms%d" % s)
                    each(msq)

                    def y_(s, b):
                        dve.wait_ge(dn_g.sem, dn_g.at("rs%d" % s, l, i))
                        own(nl_v, "z", l)
                        for g in range(G):
                            zz = tok[:, g, bass.ds(i * 256 + (T_Z + P * s), P)]
                            odn.inc(STT(zz, osb[s][:, g], ors[s][:, g:g + 1], zz, ALU.mult, ALU.mult), "y%d" % s)
                    each(y_)
                    row_(3)
                own(adb_v, "r3", l, 3)
                dve.wait_ge(s_gain, 16 * 3 * (l + 1))
                for m in (2, 4, 5):
                    q = MODS[m][0]
                    mo = mod[32 * q:32 * q + 2, 1, :]
                    oam.inc(STT(mo, mo, 1.0 if m == 4 else 0.0, ngh[32 * q:32 * q + 2, :], ALU.add, ALU.mult), "mod")
                with dve.Fori(0, 4) as i:
                    for s in range(2):
                        dve.wait_ge(at_p.sem, at_p.at("sc%d" % s, l, i))
                        dve.wait_ge(at_a.sem, at_a.at("P%d" % s, l, i - 1))
                        for g in range(G):
                            oat.inc(dve.tensor_reduce(am[s][0][:, g:g + 1], ps[:, 4 * s + 1, g * P:(1 + 2 * g) * P], AX_X, ALU.max),
                                    "mx%d" % s)
                    for s in range(2):
                        own(at_v, "mx%d" % s, l, i)
                        oat.inc(TS(am[s][1], am[s][0], sinkb[:, bass.ds(i + 4 * s, 1)], None, ALU.max), "mm%d" % s)
                    for s in range(2):
                        own(at_v, "mm%d" % s, l, i)
                        oat.inc(TS(am[s][2], am[s][1], -1.0, None, ALU.mult), "nm%d" % s)
                    for s in range(2):
                        own(at_v, "nm%d" % s, l, i)
                        dve.wait_ge(at_a.sem, at_a.at("se%d" % s, l, i - 1))
                        oat.inc(TS(am[s][4], am[s][2], sinkb[:, bass.ds(i + 4 * s, 1)], None, ALU.add), "sd%d" % s)
                    for s in range(2):
                        dve.wait_ge(at_a.sem, at_a.at("se%d" % s, l, i))
                        oat.inc(TT(am[s][5], am[s][5], am[s][3], ALU.add), "dn%d" % s)
                    for s in range(2):
                        own(at_v, "dn%d" % s, l, i)
                        oat.inc(dve.reciprocal(am[s][6], am[s][5]), "rc%d" % s)
                    for s in range(2):
                        own(at_v, "rc%d" % s, l, i)
                        dve.wait_ge(at_p.sem, at_p.at("pv%d" % s, l, i))
                        for g in range(G):
                            oat.inc(TS(tok[:, g, bass.ds(i * P + 4 * P * s, P)], ps[:, 4 * s + 3, g * P:(g + 1) * P],
                                       am[s][6][:, g:g + 1], None, ALU.mult), "o%d" % s)
                for j in range(8):
                    b, g, h = j // 4, j // 2 % 2, j % 2
                    dve.wait_ge(out_a.sem, out_a.at("ev%d" % j, l))
                    oout.inc(rest((hT, bT)[b], h, g, j), "lv%d" % j)
                dve.wait_ge(nl_a.sem, nl_a.at("sig", l))
                for j in range(3):
                    low(dve, u_out[l] + j)
                mod_low(1)
                for b, c0 in enumerate((T_GA, T_GB)):
                    for n in range(2):
                        for j in range(2 if b + n < 2 else 0):
                            low(dve, u_out[l] + 4 * b + 2 * n + 3 + j)
                        wait_used(dve, u_out[l] + 4 * b + 2 * n + 1)
                        for g in range(G):
                            x = tok[:, g, c0 + 512 * n:c0 + 512 * n + 512]
                            oout.inc(TT(x, x, ps[:, 4 * b + 2 * n + g, :], ALU.mult), "gb%d" % n if b else "ga")
                        if b:
                            own(out_v, "gb%d" % n, l)
                            for g in range(G):
                                x = tok[:, g, T_GA + 512 * n:T_GA + 512 * n + 512]
                                oout.inc(TT(x, x, tok[:, g, c0 + 512 * n:c0 + 512 * n + 512], ALU.add), "m%d" % n)
                low(dve, u_out[l] + 9)
                for j in range(4):
                    dve.wait_ge(out_a.sem, out_a.at("me%d" % j, l))
                    oout.inc(rest(hT, j // 2, j % 2, j), "ml%d" % j)
                low(dve, u_out[l] + 10)
                low(dve, u_out[l] + 11)
                wait_used(dve, u_out[l] + U_OUT - 1)
                take_y(oout, l, 1)
                resid(l, 0)
                own(res_v, "x", l, 0)
                norm_(l, 1)
                if l == 0:
                    def hidden(s, f, first=False):
                        dve.wait_ge(ff_a.sem, ff_a.at("si", 0, f))
                        for g in range(G):
                            off.inc(TT(f_hid[s][:, 256 * g:256 * g + 256], f_hs[0][:, 256 * g:256 * g + 256], ps[:, g, 256:512], ALU.mult), "mu")
                    dve.wait_ge(s_out, 32 * (l + 1))

                    def hl(f, s):
                        dve.wait_ge(ff_h.sem, ff_h.at("he", 0, f))
                        ofl.inc(TT(fT[:, s, 1].rearrange("p a b -> p (a b)"), ps[:, 2 + s, :],
                                   fT[:, s, 0].rearrange("p a b -> p (a b)").bitcast(F32), ALU.subtract), "hl")

                    low(dve, u_ff)
                    low(dve, u_ff + 1)
                    low(dve, u_ff + 2)
                    hidden(0, 0)
                    low(dve, u_ff + 3)
                    hl(0, 0)
                    low(dve, u_ff + 4)
                    hidden(1, 1)
                    with dve.Fori(0, (FF_STEPS - 3) // 4) as i:
                        for j in range(4):
                            for x in range(3):
                                if x == 2:
                                    hl(i * 4 + (1 + j), (1 + j) % 2)
                                low(dve, u_ff + 5 + 3 * j + x, i)
                            hidden(j % 2, i * 4 + (2 + j))
                    for x in range(3):
                        if x == 2:
                            hl(FF_STEPS - 2, 1)
                        low(dve, u_ff + 29 + x)
                    hidden(0, FF_STEPS - 1)
                    low(dve, u_ff + 32)
                    hl(FF_STEPS - 1, 0)
                    wait_used(dve, u_ff + U_FF - 1)
                    take_y(ofe, l, 3)
                else:
                    lg, e1, c1, f1, l2, e2, mk, f2, c2, a1, a2, cmb = rt
                    m1, m2, dd, ex, x1_, rc, w2, _ = rcol
                    pos = cut(tokf, 8220, (24,))
                    dve.wait_ge(rt_p.sem, rt_p.at("lg"))

                    def r(ins, name):
                        ort.inc(ins, name)
                        if rt_v.at(name) == rt_v.per + ort.n or ort.n == 0:
                            own(rt_v, name)

                    def wide(x):
                        return x.to_broadcast([P, G, NEXP])
                    r(CP(lg, ps[:, 0, 0:16].rearrange("p (g e) -> p g e", g=G)), "lg")
                    r(dve.tensor_reduce(m1, lg, AX_X, ALU.max), "m1")
                    r(TT(e1, lg, wide(m1), ALU.is_equal), "e1")
                    for g in range(G):
                        r(dve.tensor_tensor_scan(c1[:, g], con[:, K_ONE:K_ONE + NEXP], e1[:, g], 0.0, ALU.mult, ALU.add), "c1")
                    r(STT(f1, c1, 1.0, e1, ALU.is_equal, ALU.mult), "f1")
                    r(STT(l2, f1, NEG, lg, ALU.mult, ALU.add), "l2")
                    r(dve.tensor_reduce(m2, l2, AX_X, ALU.max), "m2")
                    r(TT(e2, l2, wide(m2), ALU.is_equal), "e2")
                    for g in range(G):
                        r(dve.tensor_tensor_scan(c2[:, g], con[:, K_ONE:K_ONE + NEXP], e2[:, g], 0.0, ALU.mult, ALU.add), "c2")
                    r(STT(f2, c2, 1.0, e2, ALU.is_equal, ALU.mult), "f2")
                    r(TT(mk, f1, f2, ALU.add), "mk")
                    r(TT(dd, m2, m1, ALU.subtract), "d")
                    dve.wait_ge(rt_a.sem, rt_a.at("ex"))
                    r(TS(x1_, ex, 1.0, None, ALU.add), "x1")
                    r(dve.reciprocal(rc, x1_), "rc")
                    r(TT(w2, ex, rc, ALU.mult), "w2")
                    r(TT(a1, f1, wide(rc), ALU.mult), "a1")
                    r(TT(a2, f2, wide(w2), ALU.mult), "a2")
                    r(TT(cmb, a1, a2, ALU.add), "cmb")
                    dve.wait_ge(rt_p.sem, rt_p.at("pos"))
                    r(CP(pos, ps[:, 1, 0:24]), "pos")
                    r(dve.memset(f_acc, 0.0), "acc")

                    ov, cum, ovi, eq = (cut(tokf, 8244 + 8 * j, (NEXP,)) for j in range(4))
                    idf = cut(tokf, 8276, (EXTRA + 1,))
                    seen = cut(tokf, 8280, (1,))
                    r(TS(ov, pos[:, 16:24], P + 0.5, None, ALU.is_gt), "ov")
                    r(dve.tensor_tensor_scan(cum, con[:, K_ONE:K_ONE + NEXP], ov, 0.0, ALU.mult, ALU.add), "cum")
                    r(TT(ovi, ov, con[:, K_IOTA:K_IOTA + NEXP], ALU.mult), "ovi")
                    for j in range(EXTRA):
                        r(STT(eq, cum, float(j + 1), ovi, ALU.is_equal, ALU.mult), "eq%d" % j)
                        r(dve.tensor_reduce(idf[:, j:j + 1], eq, AX_X, ALU.add), "id%d" % j)
                    r(CP(idf[:, EXTRA:EXTRA + 1], cum[:, NEXP - 1:NEXP]), "n")
                    r(CP(over_tab[:, :], idf), "tab")

                    def fetch(i, e, slot, f, block_=0):
                        if f == 2:
                            dve.wait_ge(pre_p.sem, pre_p.at("ga1", 0, i + (-1)))
                            for g in range(G):
                                opr.inc(TS(sel[:, g], con[:, K_IOTA + P * block_:K_IOTA + P * (block_ + 1)],
                                           pos[:, bass.ds(e + NEXP * g, 1)], mk.rearrange("p g e -> p (g e)")[:, bass.ds(e + NEXP * g, 1)],
                                           ALU.is_equal, ALU.mult), "sel")
                            own(pre_v, "sel", 0, i)
                            for g in range(G):
                                opr.inc(TS(selc[:, g], sel[:, g], cmb.rearrange("p g e -> p (g e)")[:, bass.ds(e + NEXP * g, 1)], None,
                                           ALU.mult), "selc")
                        elif f == 3:
                            dve.wait_ge(pre_p.sem, pre_p.at("sct", 0, i))
                            opr.inc(CP(selT[slot].rearrange("p g t -> p (g t)"), ps[:, 7, 0:256]), "selT")
                        else:
                            h = f - 4
                            dve.wait_ge(pre_a.sem, pre_a.at("ge%d" % h, 0, i))
                            opr.inc(TT(hTe[slot][1][:, 4 * h:4 * h + 4], ps[:, 6 + h, :].rearrange("p (k t) -> p k t", k=4),
                                       hTe[slot][0][:, 4 * h:4 * h + 4].bitcast(F32), ALU.subtract), "gl%d" % h)

                    def back(i, slot, f):
                        if f == 0:
                            dve.wait_ge(unit_used, i * U_EXP + (sp_(u_moe) + U_EXP + WRING))
                            dve.wait_ge(post_p.sem, post_p.at("sc1", 0, i + (-1)))
                            opo.inc(CP(ye, ps[:, 4:6, :].rearrange("p b c -> p (b c)")), "ye")
                        elif f < 3:
                            g = f - 1
                            dve.wait_ge(post_p.sem, post_p.at("sc%d" % g, 0, i))
                            own(post_v, "add%d" % g, 0, i + (-1))
                            opo.inc(TT(f_acc[:, g], f_acc[:, g], ps[:, 6:8, :].rearrange("p b c -> p (b c)"), ALU.add), "add%d" % g)
                            if g:
                                own(post_v, "add1", 0, i)
                                opo.inc(dve.memset(seen, 1.0), "done")

                    def body(i, slot, u, r, hook):
                        for f in range(FB + 1):
                            n = u + gu(f)
                            if f < FB:
                                for x in range(4):
                                    low(dve, n + x, r)
                                    if f == 0 and x == 1:
                                        hook(0)
                                n += 4
                            if f:
                                dve.wait_ge(moe_a.sem, moe_a.at("he%d" % (f - 1), 0, i))
                                omo.inc(TT(fT[:, (f - 1) % 2, 1].rearrange("p a b -> p (a b)"), ps[:, 2 + (f - 1) % 2, :],
                                           fT[:, (f - 1) % 2, 0].rearrange("p a b -> p (a b)").bitcast(F32), ALU.subtract), "hl%d" % (f - 1))
                                low(dve, n, r)
                                low(dve, n + 1, r)
                            if f < FB:
                                dve.wait_ge(moe_a.sem, moe_a.at("si%d" % f, 0, i))
                                omo.inc(TT(f_hid[f % 2], f_hs[0], ps[:, 1, :], ALU.mult), "mu%d" % f)
                                if f:
                                    hook(f)
                    experts(dve, fetch, body, back)
                    for g in range(G):
                        ofe.inc(CP(y_sb[:, g, :], f_acc[:, g]), "y")
                resid(l, 1)


_W = ["w_ada", "b_ada", "norm_g", "w_in", "attn_sink", "conv_w", "dn_a_log", "dn_dt_bias", "dn_norm_g", "w_pa", "w_pb",
      "w_o", "w_ff_gate", "w_ff_up", "w_ff_down", "w_router", "w_e_gate", "w_e_up", "w_e_down", "x_prompt", "x_sample",
      "c", "c_ctx"]
_LAYER = {"cache_k%d": "cache_k_l%d", "cache_v%d": "cache_v_l%d", "state%d": "state_delta_l%d"}


def kernel(**inputs):
    import concourse.bacc as _bacc
    from concourse.bass_utils import run_bass_kernel_spmd as _run

    nc = _bacc.Bacc("TRN2", target_bir_lowering=False, num_devices=1)
    arrays, args = {}, {}

    def put(name, a):
        a = np.ascontiguousarray(a)
        arrays["in_" + name] = a
        args[name] = nc.dram_tensor("in_" + name, a.shape, mybir.dt.from_np(a.dtype), kind="ExternalInput").ap()

    for name in _W:
        put(name, inputs[name])
    for ours, theirs in _LAYER.items():
        for l in range(DEPTH):
            put(ours % l, inputs[theirs % l])
    con, lev = constants()
    put("consts", con)
    put("levels", lev)
    outs = []

    def out(name, shape):
        args[name] = nc.dram_tensor("o_" + name, shape, F32, kind="ExternalOutput").ap()
        outs.append("o_" + name)

    out("y_out0", (1, P, D))
    out("y_out1", (1, P, D))
    for l in range(DEPTH):
        out("k_out%d" % l, (1, P, HKV, P))
        out("v_out%d" % l, (1, P, HKV, P))
        out("s_out%d" % l, (1, 2, DH, P, P))
    program(nc, args)
    r = _run(nc, [arrays], core_ids=[0])
    return tuple(r.results[0][n] for n in outs)
```
